# Optimizing a Trainium2 kernel written in Bass

```python
import jax
import jax.numpy as jnp
from jax import lax
import numpy as np

D_MODEL = 1024
BATCH = 1
SEQ = 256
DEPTH = 2

GRID_W = 64
CTX_LEN = 256
N_EVEN = (DEPTH + 1) // 2
N_ODD = DEPTH // 2
N_MOD = 6
EPS = 1e-6

RET_HEADS = 4
RET_DK = 64
RET_DV = 128
RET_QK = RET_HEADS * RET_DK
RET_V = RET_HEADS * RET_DV
RET_CHUNK = 128

RWKV_HEADS = 8
RWKV_N = 64
RWKV_W = RWKV_HEADS * RWKV_N
DECAY_RANK = 64
ICLR_RANK = 64
GATE_RANK = 160
GN_EPS = 64e-5
SHIFT_W = 3 * RWKV_W + 2 * DECAY_RANK + 2 * ICLR_RANK + GATE_RANK
EVEN_IN = 2 * RET_QK + 2 * RET_V + SHIFT_W
EVEN_OUT = RET_V + RWKV_W

MLA_HEADS = 8
Q_RANK = 384
KV_RANK = 256
QK_NOPE = 128
QK_ROPE = 64
V_HEAD = 128
ODD_IN = Q_RANK + KV_RANK + QK_ROPE
MLA_SCALE = (QK_NOPE + QK_ROPE) ** -0.5
ROPE_BASE = 10000.0
ATTN_BLOCK = 128

N_GROUPS = 4
EXPERTS_PER_GROUP = 8
N_EXPERTS = N_GROUPS * EXPERTS_PER_GROUP
EXPERT_HIDDEN = 256
TOP_K = 2

kernel_name = 'hybrid_retention_rwkv7_mla_hmoe_dit'

def split_cols(t, sizes):
    return jnp.split(t, np.cumsum(sizes)[:-1].tolist(), axis=-1)

def rmsnorm(x, g):
    xf = x.astype(jnp.float32)
    y = xf * lax.rsqrt(jnp.mean(xf * xf, axis=-1, keepdims=True) + EPS)
    return (y * g).astype(x.dtype)

def modulate(x, shift, scale):
    return x * (1.0 + scale[:, None]) + shift[:, None]

def centred_shift(y, mu):
    prev = jnp.pad(y[:, :-1], ((0, 0), (1, 0), (0, 0)))
    nxt = jnp.pad(y[:, 1:], ((0, 0), (0, 1), (0, 0)))
    return y + mu[0] * (prev - y) + mu[1] * (nxt - y)

def retention_chunkwise(q, k, v, log_gamma, state0):
    b, h, l, dk = q.shape
    dv = v.shape[-1]
    n, cs = l // RET_CHUNK, RET_CHUNK
    qc = q.reshape(b, h, n, cs, dk)
    kc = k.reshape(b, h, n, cs, dk)
    vc = v.reshape(b, h, n, cs, dv)
    pos = jnp.arange(cs, dtype=jnp.float32)
    lg = log_gamma[:, None]
    rel = pos[:, None] - pos[None, :]
    dmask = jnp.where(rel >= 0, jnp.exp(log_gamma[:, None, None] * jnp.maximum(rel, 0.0)), 0.0)
    scores = jnp.einsum('bhnid,bhnjd->bhnij', qc, kc) * dmask[None, :, None]
    o_inner = jnp.einsum('bhnij,bhnjv->bhniv', scores, vc)
    k_dec = jnp.exp(lg * (cs - 1.0 - pos))
    delta = jnp.einsum('bhnjd,bhnjv->nbhdv', kc * k_dec[None, :, None, :, None], vc)
    chunk_decay = jnp.exp(log_gamma * cs)[None, :, None, None]

    def step(s, d):
        return s * chunk_decay + d, s

    s_final, s_prev = lax.scan(step, state0, delta)
    q_dec = jnp.exp(lg * (pos + 1.0))
    o_cross = jnp.einsum('bhnid,nbhdv->bhniv', qc * q_dec[None, :, None, :, None], s_prev)
    return (o_inner + o_cross).reshape(b, h, l, dv), s_final

def bidir_retention(qkv_c, qkv_l, log_gamma):
    qc, kc, vc = qkv_c
    ql, kl, vl = qkv_l
    s0 = jnp.zeros(qc.shape[:2] + (RET_DK, RET_DV), jnp.float32)
    flip = lambda t: jnp.flip(t, axis=2)
    o_cf, s_cf = retention_chunkwise(qc, kc, vc, log_gamma, s0)
    o_lf, _ = retention_chunkwise(ql, kl, vl, log_gamma, s_cf)
    o_cb, s_cb = retention_chunkwise(flip(qc), flip(kc), flip(vc), log_gamma, s0)
    o_lb, _ = retention_chunkwise(flip(ql), flip(kl), flip(vl), log_gamma, s_cb)
    diag = lambda q, k, v: jnp.sum(q * k, axis=-1, keepdims=True) * v
    return (o_cf + flip(o_cb) - diag(qc, kc, vc), o_lf + flip(o_lb) - diag(ql, kl, vl))

def rwkv7_scan(s0, r, w, kk, a, kt, v, reverse):
    def step(s, inp):
        r_t, w_t, kk_t, a_t, k_t, v_t = inp
        sa = jnp.einsum('bhvk,bhk->bhv', s, kk_t)
        s = (s * w_t[:, :, None, :] - sa[..., None] * (kk_t * a_t)[:, :, None, :]
             + v_t[..., None] * k_t[:, :, None, :])
        return s, jnp.einsum('bhvk,bhk->bhv', s, r_t)

    xs = tuple(jnp.swapaxes(t, 0, 1) for t in (r, w, kk, a, kt, v))
    s_final, ys = lax.scan(step, s0, xs, reverse=reverse)
    return jnp.swapaxes(ys, 0, 1), s_final

def bidir_rwkv7(seq_c, seq_l):
    rc, kkc, vc, dc = seq_c
    rl, kkl, vl, dl = seq_l
    s0 = jnp.zeros(rc.shape[:1] + (RWKV_HEADS, RWKV_N, RWKV_N), jnp.float32)
    ys_c, ys_l = [], []
    for direction in range(2):
        rev = direction == 1
        wc, ac, ktc = dc[direction]
        y_c, s_c = rwkv7_scan(s0, rc, wc, kkc, ac, ktc, vc, rev)
        wl, al, ktl = dl[direction]
        y_l, _ = rwkv7_scan(s_c, rl, wl, kkl, al, ktl, vl, rev)
        ys_c.append(y_c)
        ys_l.append(y_l)
    return ys_c[0] + ys_c[1], ys_l[0] + ys_l[1]

def even_mixer(xc, xl, w_in, shift_mu, w0, w2, a0, a2, g2, k_k, k_a, r_k, lnx_w, lnx_b, w_out):
    log_gamma = jnp.log1p(-jnp.exp2(-5.0 - jnp.arange(RET_HEADS, dtype=jnp.float32)))

    def features(x):
        b, l, _ = x.shape
        p = (x @ w_in).astype(jnp.float32)
        q, k, v, g, rw = split_cols(p, [RET_QK, RET_QK, RET_V, RET_V, SHIFT_W])
        to_heads = lambda t: t.reshape(b, l, RET_HEADS, -1).transpose(0, 2, 1, 3)
        ret = (to_heads(q) * RET_DK ** -0.5, to_heads(k), to_heads(v), g)
        rw = centred_shift(rw, shift_mu)
        r, kr, vr, wd_f, wd_b, ad_f, ad_b, gd = split_cols(
            rw, [RWKV_W] * 3 + [DECAY_RANK] * 2 + [ICLR_RANK] * 2 + [GATE_RANK])
        hd = lambda t: t.reshape(b, l, RWKV_HEADS, RWKV_N)
        r, kr, vr = hd(r), hd(kr), hd(vr)
        kk = kr * k_k.reshape(RWKV_HEADS, RWKV_N)
        kk = kk / jnp.maximum(jnp.linalg.norm(kk, axis=-1, keepdims=True), 1e-12)
        dirs = []
        for d, (wd, ad) in enumerate(((wd_f, ad_f), (wd_b, ad_b))):
            wlog = -jax.nn.softplus(-(w0[d] + jnp.tanh(wd) @ w2[d])) - 0.5
            decay = hd(jnp.exp(-jnp.exp(wlog)))
            a = hd(jax.nn.sigmoid(a0[d] + ad @ a2[d]))
            kt = kr * (1.0 + (a - 1.0) * k_a.reshape(RWKV_HEADS, RWKV_N))
            dirs.append((decay, a, kt))
        gate = jax.nn.sigmoid(gd) @ g2
        return ret, (r, kk, vr, dirs, gate)

    def ret_out(o, g):
        o = o * lax.rsqrt(jnp.mean(o * o, axis=-1, keepdims=True) + EPS)
        bb, hh, ll, dv = o.shape
        return o.transpose(0, 2, 1, 3).reshape(bb, ll, hh * dv) * jax.nn.silu(g)

    def rwkv_out(y, feats):
        r, kk, v, dirs, gate = feats
        bb, ll = r.shape[:2]
        mu = jnp.mean(y, axis=-1, keepdims=True)
        var = jnp.mean(jnp.square(y - mu), axis=-1, keepdims=True)
        yn = ((y - mu) * lax.rsqrt(var + GN_EPS) * lnx_w.reshape(RWKV_HEADS, RWKV_N)
              + lnx_b.reshape(RWKV_HEADS, RWKV_N))
        bonus = jnp.sum(r * (dirs[0][2] + dirs[1][2]) * r_k, axis=-1, keepdims=True) * v
        return (yn + bonus).reshape(bb, ll, RWKV_W) * gate

    (qc, kc, vc, gc), rwc = features(xc)
    (ql, kl, vl, gl), rwl = features(xl)
    oc, ol = bidir_retention((qc, kc, vc), (ql, kl, vl), log_gamma)
    yc, yl = bidir_rwkv7(rwc[:4], rwl[:4])
    out_c = jnp.concatenate([ret_out(oc, gc), rwkv_out(yc, rwc)], axis=-1).astype(xc.dtype) @ w_out
    out_l = jnp.concatenate([ret_out(ol, gl), rwkv_out(yl, rwl)], axis=-1).astype(xl.dtype) @ w_out
    return out_c, out_l

def axial_rope_angles(length):
    rows = length // GRID_W
    row = jnp.repeat(jnp.arange(rows, dtype=jnp.float32), GRID_W)
    col = jnp.tile(jnp.arange(GRID_W, dtype=jnp.float32), rows)
    n_freq = QK_ROPE // 4
    inv_freq = ROPE_BASE ** (-jnp.arange(n_freq, dtype=jnp.float32) / n_freq)
    return row[:, None] * inv_freq, col[:, None] * inv_freq

def rotate_half_axis(t, ang):
    cos = jnp.cos(ang)[None, :, None, :]
    sin = jnp.sin(ang)[None, :, None, :]
    t1, t2 = jnp.split(t, 2, axis=-1)
    return jnp.concatenate([t1 * cos - t2 * sin, t2 * cos + t1 * sin], axis=-1)

def apply_axial_rope(t, ang_row, ang_col):
    half = t.shape[-1] // 2
    out = jnp.concatenate([rotate_half_axis(t[..., :half], ang_row),
                           rotate_half_axis(t[..., half:], ang_col)], axis=-1)
    return out.astype(t.dtype)

def softmax_attention(q, k, v):
    s = jnp.einsum('bqhd,bkhd->bhqk', q, k).astype(jnp.float32) * MLA_SCALE
    p = jax.nn.softmax(s, axis=-1).astype(v.dtype)
    return jnp.einsum('bhqk,bkhd->bqhd', p, v)

def blocked_attention(q, k, v):
    b, l, h, d = q.shape
    qb = jnp.swapaxes(q.reshape(b, l // ATTN_BLOCK, ATTN_BLOCK, h, d), 0, 1)
    ob = lax.map(lambda blk: softmax_attention(blk, k, v), qb)
    return jnp.swapaxes(ob, 0, 1).reshape(b, l, h, v.shape[-1])

def mla_mixer(xc, xl, w_in, q_norm_g, w_uq, kv_norm_g, w_ukv, w_o, need_ctx):
    b, l, _ = xl.shape
    ang_r, ang_c = axial_rope_angles(l)

    def project_q(x, rotate):
        bb, ll, _ = x.shape
        c_q = rmsnorm(x @ w_in[:, :Q_RANK], q_norm_g)
        q = (c_q @ w_uq).reshape(bb, ll, MLA_HEADS, QK_NOPE + QK_ROPE)
        q_nope, q_pe = q[..., :QK_NOPE], q[..., QK_NOPE:]
        if rotate:
            q_pe = apply_axial_rope(q_pe, ang_r, ang_c)
        return jnp.concatenate([q_nope, q_pe], axis=-1)

    def project_kv(x, rotate):
        bb, ll, _ = x.shape
        kv_a = x @ w_in[:, Q_RANK:]
        c_kv = rmsnorm(kv_a[..., :KV_RANK], kv_norm_g)
        k_pe = kv_a[..., KV_RANK:][:, :, None, :]
        if rotate:
            k_pe = apply_axial_rope(k_pe, ang_r, ang_c)
        kv = (c_kv @ w_ukv).reshape(bb, ll, MLA_HEADS, QK_NOPE + V_HEAD)
        k = jnp.concatenate([kv[..., :QK_NOPE],
                             jnp.broadcast_to(k_pe, (bb, ll, MLA_HEADS, QK_ROPE))], axis=-1)
        return k, kv[..., QK_NOPE:]

    kc, vc = project_kv(xc, False)
    kl, vl = project_kv(xl, True)
    ql = project_q(xl, True)
    k_all = jnp.concatenate([kc, kl], axis=1)
    v_all = jnp.concatenate([vc, vl], axis=1)
    out_l = blocked_attention(ql, k_all, v_all).reshape(b, l, MLA_HEADS * V_HEAD) @ w_o
    out_c = None
    if need_ctx:
        qc = project_q(xc, False)
        out_c = softmax_attention(qc, kc, vc).reshape(b, xc.shape[1], MLA_HEADS * V_HEAD) @ w_o
    return out_c, out_l

def hier_moe(x, w_grp, b_grp, w_exp, b_exp, w_gate, w_up, w_down):
    xf = x.astype(jnp.float32)
    p_grp = jax.nn.softmax(xf @ w_grp.astype(jnp.float32) + b_grp.astype(jnp.float32), axis=-1)
    pg, g_idx = lax.top_k(p_grp, 1)
    e_logits = (xf @ w_exp.astype(jnp.float32) + b_exp.astype(jnp.float32)).reshape(
        -1, N_GROUPS, EXPERTS_PER_GROUP)
    e_sel = jnp.einsum('tg,tge->te', jax.nn.one_hot(g_idx[:, 0], N_GROUPS, dtype=jnp.float32), e_logits)
    pe, e_idx = lax.top_k(jax.nn.softmax(e_sel, axis=-1), TOP_K)
    wts = pg * pe / jnp.sum(pe, axis=-1, keepdims=True)
    flat = g_idx * EXPERTS_PER_GROUP + e_idx
    gates = jnp.einsum('tk,tke->te', wts, jax.nn.one_hot(flat, N_EXPERTS, dtype=jnp.float32)).astype(x.dtype)
    y = jnp.zeros_like(x)
    for e in range(N_EXPERTS):
        hidden = jax.nn.silu(x @ w_gate[e]) * (x @ w_up[e])
        y = y + gates[:, e:e + 1] * (hidden @ w_down[e])
    return y

def setup_inputs(seed: int = 0) -> dict:
    key = jax.random.key(seed)
    keys = iter(jax.random.split(key, 40))

    def normal(shape, scale):
        return jax.random.normal(next(keys), shape, jnp.float32) * scale

    def uniform(shape, lo, hi):
        return jax.random.uniform(next(keys), shape, jnp.float32, lo, hi)

    def gain(shape):
        return 1.0 + normal(shape, 0.05)

    d = D_MODEL
    return {
        'x': normal((BATCH, SEQ, d), 1.0),
        'c': normal((BATCH, d), 1.0),
        'ctx': normal((BATCH, CTX_LEN, d), 1.0),
        'c_ctx': normal((d,), 1.0),
        'ada_w': normal((DEPTH, d, N_MOD * d), 0.5 * d ** -0.5),
        'ada_b': normal((DEPTH, N_MOD * d), 0.02),
        'norm1_g': gain((DEPTH, d)),
        'norm2_g': gain((DEPTH, d)),
        'final_g': gain((d,)),
        'ev_w_in': normal((N_EVEN, d, EVEN_IN), d ** -0.5),
        'ev_shift_mu': uniform((N_EVEN, 2, SHIFT_W), 0.0, 0.5),
        'rwkv_w0': uniform((N_EVEN, 2, RWKV_W), -6.0, 0.0),
        'rwkv_w2': normal((N_EVEN, 2, DECAY_RANK, RWKV_W), 0.5 * DECAY_RANK ** -0.5),
        'rwkv_a0': normal((N_EVEN, 2, RWKV_W), 0.5),
        'rwkv_a2': normal((N_EVEN, 2, ICLR_RANK, RWKV_W), 0.5 * ICLR_RANK ** -0.5),
        'rwkv_g2': normal((N_EVEN, GATE_RANK, RWKV_W), GATE_RANK ** -0.5),
        'rwkv_k_k': 0.85 + normal((N_EVEN, RWKV_W), 0.1),
        'rwkv_k_a': uniform((N_EVEN, RWKV_W), 0.5, 1.0),
        'rwkv_r_k': normal((N_EVEN, RWKV_HEADS, RWKV_N), 0.1),
        'rwkv_lnx_w': gain((N_EVEN, RWKV_W)),
        'rwkv_lnx_b': normal((N_EVEN, RWKV_W), 0.02),
        'ev_w_out': normal((N_EVEN, EVEN_OUT, d), EVEN_OUT ** -0.5),
        'mla_w_in': normal((N_ODD, d, ODD_IN), d ** -0.5),
        'mla_q_norm_g': gain((N_ODD, Q_RANK)),
        'mla_w_uq': normal((N_ODD, Q_RANK, MLA_HEADS * (QK_NOPE + QK_ROPE)), Q_RANK ** -0.5),
        'mla_kv_norm_g': gain((N_ODD, KV_RANK)),
        'mla_w_ukv': normal((N_ODD, KV_RANK, MLA_HEADS * (QK_NOPE + V_HEAD)), KV_RANK ** -0.5),
        'mla_w_o': normal((N_ODD, MLA_HEADS * V_HEAD, d), (MLA_HEADS * V_HEAD) ** -0.5),
        'moe_w_grp': normal((DEPTH, d, N_GROUPS), d ** -0.5),
        'moe_b_grp': normal((DEPTH, N_GROUPS), 0.01),
        'moe_w_exp': normal((DEPTH, d, N_EXPERTS), d ** -0.5),
        'moe_b_exp': normal((DEPTH, N_EXPERTS), 0.01),
        'moe_w_gate': normal((DEPTH, N_EXPERTS, d, EXPERT_HIDDEN), d ** -0.5),
        'moe_w_up': normal((DEPTH, N_EXPERTS, d, EXPERT_HIDDEN), d ** -0.5),
        'moe_w_down': normal((DEPTH, N_EXPERTS, EXPERT_HIDDEN, d), EXPERT_HIDDEN ** -0.5),
    }

def reference(x, c, ctx, c_ctx, ada_w, ada_b, norm1_g, norm2_g, final_g,
              ev_w_in, ev_shift_mu, rwkv_w0, rwkv_w2, rwkv_a0, rwkv_a2, rwkv_g2,
              rwkv_k_k, rwkv_k_a, rwkv_r_k, rwkv_lnx_w, rwkv_lnx_b, ev_w_out,
              mla_w_in, mla_q_norm_g, mla_w_uq, mla_kv_norm_g, mla_w_ukv, mla_w_o,
              moe_w_grp, moe_b_grp, moe_w_exp, moe_b_exp, moe_w_gate, moe_w_up, moe_w_down):
    b, l, d = x.shape
    lc = ctx.shape[1]
    h, hc = x, ctx
    s_lat = jax.nn.silu(c)
    s_ctx = jax.nn.silu(c_ctx)[None]
    for layer in range(DEPTH):
        last = layer == DEPTH - 1
        i = layer // 2
        m = jnp.split(s_lat @ ada_w[layer] + ada_b[layer], N_MOD, axis=-1)
        mc = jnp.split(s_ctx @ ada_w[layer] + ada_b[layer], N_MOD, axis=-1)
        xl = modulate(rmsnorm(h, norm1_g[layer]), m[0], m[1])
        xc = modulate(rmsnorm(hc, norm1_g[layer]), mc[0], mc[1])
        if layer % 2 == 0:
            yc, yl = even_mixer(xc, xl, ev_w_in[i], ev_shift_mu[i], rwkv_w0[i], rwkv_w2[i],
                                rwkv_a0[i], rwkv_a2[i], rwkv_g2[i], rwkv_k_k[i], rwkv_k_a[i],
                                rwkv_r_k[i], rwkv_lnx_w[i], rwkv_lnx_b[i], ev_w_out[i])
        else:
            yc, yl = mla_mixer(xc, xl, mla_w_in[i], mla_q_norm_g[i], mla_w_uq[i],
                               mla_kv_norm_g[i], mla_w_ukv[i], mla_w_o[i], not last)
        h = h + m[2][:, None] * yl
        xl = modulate(rmsnorm(h, norm2_g[layer]), m[3], m[4])

        def channel_mix(t):
            return hier_moe(t, moe_w_grp[layer], moe_b_grp[layer], moe_w_exp[layer], moe_b_exp[layer],
                            moe_w_gate[layer], moe_w_up[layer], moe_w_down[layer])

        if last:
            h = h + m[5][:, None] * channel_mix(xl.reshape(b * l, d)).reshape(b, l, d)
        else:
            hc = hc + mc[2][:, None] * yc
            xc = modulate(rmsnorm(hc, norm2_g[layer]), mc[3], mc[4])
            y = channel_mix(jnp.concatenate([xc.reshape(b * lc, d), xl.reshape(b * l, d)], axis=0))
            hc = hc + mc[5][:, None] * y[: b * lc].reshape(b, lc, d)
            h = h + m[5][:, None] * y[b * lc:].reshape(b, l, d)
    return rmsnorm(h, final_g)


_drawn_inputs = setup_inputs


def setup_inputs(seed=0):
    import zlib

    import numpy as np

    out = dict(_drawn_inputs(seed))
    spreads = {}
    factors = {'rwkv_w2': 7.383,
     'rwkv_a0': 2.811,
     'rwkv_a2': 3.897,
     'rwkv_lnx_w': 8.0,
     'rwkv_lnx_b': 8.0,
     'mla_q_norm_g': 8.0,
     'mla_kv_norm_g': 8.0,
     'moe_b_grp': 8.0,
     'moe_b_exp': 8.0}
    for name, (base, spread) in spreads.items():
        noise = np.random.default_rng([zlib.crc32(name.encode()), seed]).standard_normal(out[name].shape)
        drawn = base * np.exp(spread * noise) if base else spread * noise
        out[name] = jnp.asarray(drawn.astype(out[name].dtype))
    for name, factor in factors.items():
        out[name] = (out[name] * factor).astype(out[name].dtype)
    return out
```

```python
from contextlib import ExitStack
import math

import concourse.bass as bass
from concourse import mybir

F32 = mybir.dt.float32
U8 = mybir.dt.uint8
ALU = mybir.AluOpType
ACT = mybir.ActivationFunctionType
AX = mybir.AxisListType.X

P = 128
D = 1024
DC = D // P
TC = 256
T = 2 * TC
NT = T // P
EPS = 1e-6
RH = 4
NPAIR = 4
GN_EPS = 64e-5
MH = 8
NE, NG, EPG = 32, 4, 8
NR = NG + NE
MLA_SCALE = (128 + 64) ** -0.5
LOG_DECAY = -math.exp(-0.5)

VEC, NV = {}, 0
for _name, _w in (("c", 8), ("c_ctx", 8), ("norm1_g0", 8), ("norm1_g1", 8), ("norm2_g0", 8), ("norm2_g1", 8),
                  ("final_g", 8), ("ada_b0", 48), ("ada_b1", 48), ("mu0", 16), ("mu1", 16), ("w0_0", 4),
                  ("w0_1", 4), ("a0_0", 4), ("a0_1", 4), ("k_k", 4), ("k_a", 4), ("r_k", 4), ("lnx_w", 4),
                  ("lnx_b", 4), ("q_norm", 3), ("kv_norm", 2)):
    VEC[_name] = (NV, _w)
    NV += _w
MASKS = ("ident", "ones", "half_ones", "swap", "lt", "le", "gt", "ge", "eye2")
SLOT = 6144
LEVELS = (1, 2, 4, 8, 16, 32, 64)
ORDER = ((0, 1, 2, 3), (1, 0, 3, 2))


def stream_items():
    first = [("ada", n, 4096) for n in range(12)] + [("win", n, 4096) for n in range(6)]
    first += [("win6", 0, 8 * 416), ("lora", 0, 2048)]
    first += [("ada", n, 4096) for n in range(12, 24)] + [("wout", n, 4096) for n in range(2)]
    items = [(a, i, w, n % 2) for n, (a, i, w) in enumerate(first)]
    items += [("expert", e, SLOT, e % 4) for e in range(NE)]
    mla = [("mla_in", 0, SLOT), ("mla_uq", 0, 4608), ("mla_ukv", 0, 4096), ("mla_o", 0, 4096), ("mla_o", 1, 4096)]
    items += [(a, i, w, n % 4) for n, (a, i, w) in enumerate(mla)]
    items += [("expert", NE + e, SLOT, e % 4) for e in range(NE)]
    return items


def named(prefix, key):
    return f"ev:{prefix}{key[3:]}" if key.startswith("ev:") else prefix + key


class Layout:

    def __init__(self, sems, spare, marks):
        self.spare = spare
        self.sems, self.marks, self.new = sems, marks, {}
        self.count = {e: 0 for e in sems}
        self.loop = {e: None for e in sems}
        self.rotation, self.user = 0, {}
        self.waited, self.pending = {}, {}

    def did(self, engine, *keys):
        self.count[engine] += 1
        for key in keys:
            assert key not in self.new, key
            self.new[key] = (engine, self.loop[engine], self.count[engine])
        return self.sems[engine], 1

    def seen(self, eng, key, it=None, back=0):
        if not self.marks:
            return self.sems["pe"], 1
        engine, loop, n = self.marks[key]
        waiter, kind = str(eng.engine), None
        if loop is not None:
            base, per, times = self.marks["loop", engine, loop]
            if it is None:
                n += base + (times - 1) * per
            else:
                n, kind = n + base - back * per, loop
                assert n > 0, ("a wait below one", key, n, per)
        high = self.waited.get((waiter, engine, kind), 0)
        if kind is None:
            return self.sems[engine], n
        if high < n and self.pending.get(waiter) == engine:
            eng.sem_inc(self.spare, 1)
        self.pending[waiter] = engine
        self.waited[waiter, engine, kind] = n = max(n, high)
        return self.sems[engine], it * per + n

    def enter(self, engine, loop):
        self.loop[engine], base, self.count[engine] = loop, self.count[engine], 0
        self.waited = {}
        return base

    def leave(self, engine, base, times):
        loop, per = self.loop[engine], self.count[engine]
        self.new["loop", engine, loop] = (base, per, times)
        self.loop[engine], self.count[engine] = None, base + times * per
        self.waited = {}

    def bank(self, job):
        b, loop = self.rotation, self.loop["pe"]
        self.rotation = (b + 1) % 8
        before, back = self.user.get(b), 0
        if before is None and loop is not None:
            before, back = self.marks.get(("last", loop, b)), 1
        self.user[b] = job
        self.new["bank", job] = b
        if loop is not None:
            self.new["last", loop, b] = job
        return b, before, back

    def empty(self):
        self.rotation, self.user = 0, {}


def build(nc, dram, out, dbg, marks):
    items = stream_items()
    ctx = ExitStack()
    with ctx:
        def sb(name, shape, dt=F32):
            return ctx.enter_context(nc.sbuf_tensor(name, shape, dt))

        def sem(name):
            return ctx.enter_context(nc.semaphore(name))

        ring = sb("ring", [P, 4 * SLOT])
        xT_t = sb("xT", [P, DC * T])
        hm_t = sb("h_or_mix", [P, DC * T])
        feat_t = sb("features", [P, 8 * NPAIR * T])
        vec = sb("vec", [P, NV])
        mask_t = sb("masks", [P, len(MASKS) * P])
        level_t = sb("level_masks", [P, 2 * len(LEVELS) * P], U8)
        silu_c = sb("silu_c", [P, DC, 2])
        mods = sb("mods", [P, 2, 48, 2])
        gains = sb("gains", [P, 4, DC, 2])
        small = sb("small", [P, 64])
        gate_in = sb("gate_in", [P, 2, T])

        psum = [ctx.enter_context(nc.psum_tensor(f"bank{b}", [P, 512], F32)) for b in range(8)]

        sems = {e: sem(f"{e}_done") for e in ("pe", "act", "dve", "pool")}
        loaded = [sem(f"slot{s}_loaded") for s in range(4)]
        consts_in, h_in, h_again = sem("consts_in"), sem("h_in"), sem("h_again")
        router_in, gates_out, rope_in = sem("router_in"), sem("gates_out"), sem("rope_in")
        gate_rows = [sem(f"gate_row{s}") for s in range(4)]
        stored, phase = sem("stored"), sem("phase")
        waited = sem("waited")
        L = Layout(sems, waited, marks)
        did, seen = L.did, L.seen
        block = ctx.enter_context(nc.Block())

        def V(name, j=None):
            a, w = VEC[name]
            return vec[:, a:a + w] if j is None else vec[:, a + j:a + j + 1]

        M = {n: mask_t[:, i * P:(i + 1) * P] for i, n in enumerate(MASKS)}
        level = level_t[:].rearrange("p (d n c) -> p d n c", d=2, c=P)
        xT = xT_t[:].rearrange("p (c t) -> p c t", t=T)
        hm = hm_t[:].rearrange("p (c t) -> p c t", t=T)
        mix = hm

        def part(t, off, *shape):
            n = math.prod(shape)
            v = t[:, off:off + n]
            if len(shape) == 2:
                v = v.rearrange("p (a b) -> p a b", b=shape[1])
            if len(shape) == 3:
                v = v.rearrange("p (a b c) -> p a b c", b=shape[1], c=shape[2])
            return v

        def slot(s, *shape):
            return part(ring, s * SLOT, *shape)

        r_t, kr_t, kk_t, v_t, a_t0, a_t1, lw_t0, lw_t1 = (part(feat_t, i * 2048, NPAIR, T) for i in range(8))
        a_t, lw_t = (a_t0, a_t1), (lw_t0, lw_t1)
        hT = part(feat_t, 0, DC, T)
        yT = part(feat_t, 4096, DC, T)
        WORK = 2 * SLOT

        turn, previous, last_in = {}, {}, {}
        uses = [0] * 4
        for a, i, w, s in items:
            uses[s] += 1
            turn[a, i] = (s, uses[s])
            previous[a, i] = last_in.get(s)
            last_in[s] = (a, i)

        def arrived(key):
            s, n = turn[key]
            return loaded[s], 16 * n

        def take(pe, job, it=None):
            b, before, back = L.bank(job)
            if before is not None:
                pe.wait_ge(*seen(pe, "ev:" + before, it, back))
            return psum[b]

        def bank(job):
            return psum[marks.get(("bank", job), 0)]

        barriers = {"pe": 0, "act": 0, "dve": 0, "pool": 0}

        def barrier(eng, name):
            barriers[name] += 1
            eng.drain().then_inc(phase, 1)
            eng.wait_ge(phase, 4 * barriers[name])
            if name == "pe":
                L.empty()

        SEGS = ((0, TC), (TC, T))

        def norm_bufs(at):
            return part(at[0], at[1], 2, T), part(at[0], at[1] + 2 * T, T)

        def norm_pe(pe, tag, n, chunks, at):
            sq, _ = norm_bufs(at)
            b = take(pe, tag)
            for k in range(chunks):
                pe.wait_ge(*seen(pe, f"{tag}.sq{k}"))
                pe.matmul(b[:, 0:n], M["ones"], sq[:, k % 2, 0:n], start=k == 0, stop=k == chunks - 1)\
                    .then_inc(*did("pe", f"{tag}.sum{k}"))

        def norm_act(act, tag, src, n, chunks, at, ready=()):
            sq, rt = norm_bufs(at)
            for k in range(chunks):
                for key in ready[k:k + 1]:
                    act.wait_ge(*seen(act, key))
                if k >= 2:
                    act.wait_ge(*seen(act, f"{tag}.sum{k - 2}"))
                act.activation(sq[:, k % 2, 0:n], src(k), ACT.Square).then_inc(*did("act", f"{tag}.sq{k}"))
            act.wait_ge(*seen(act, f"{tag}.sum{chunks - 1}"))
            act.activation(rt[:, 0:n], bank(tag)[:, 0:n], ACT.Sqrt, bias=small[:, 0:1], scale=1.0 / (chunks * P))\
                .then_inc(*did("act", "ev:" + tag))

        def norm_dve(dve, tag, src, dst, n, chunks, at):
            _, rt = norm_bufs(at)
            dve.wait_ge(*seen(dve, "ev:" + tag))
            dve.reciprocal(rt[:, 0:n], rt[:, 0:n]).then_inc(*did("dve", tag + ".inv"))
            dve.wait_ge(*seen(dve, tag + ".inv"))
            for k in range(chunks):
                dve.tensor_tensor(dst(k), src(k), rt[:, 0:n], ALU.mult).then_inc(*did("dve", f"{tag}.xr{k}"))

        def modulate_act(act, tag, layer, which, segs):
            for k in range(DC):
                act.wait_ge(*seen(act, f"{tag}.xr{k}"))
                for i, (a, b) in enumerate(segs):
                    seg = a // TC
                    act.activation(xT[:, k, a:b], xT[:, k, a:b], ACT.Identity,
                                   scale=gains[:, 2 * layer + which, k, seg:seg + 1],
                                   bias=mods[:, layer, 24 * which + k, seg:seg + 1])\
                        .then_inc(*did("act", *([f"{tag}.x{k}"] if i == len(segs) - 1 else [])))

        NORM = (ring, WORK)

        def ada_pe(pe, layer):
            for g in range(12):
                key = ("ada", 12 * layer + g)
                w = slot(turn[key][0], DC, 512)
                b = take(pe, f"ada{layer}.{g}")
                pe.wait_ge(*arrived(key))
                for m in range(4):
                    for k in range(DC):
                        mm = pe.matmul(b[:, 2 * m:2 * m + 2], w[:, k, m * P:(m + 1) * P], silu_c[:, k, :],
                                       start=k == 0, stop=k == DC - 1)
                mm.then_inc(*did("pe", f"ada{layer}.{g}", f"used:ada{key[1]}"))

        def ada_dve(dve, layer):
            for g in range(12):
                dve.wait_ge(*seen(dve, f"ada{layer}.{g}"))
                bias = V(f"ada_b{layer}")[:, 4 * g:4 * g + 4].unsqueeze(2).broadcast_to([P, 4, 2])
                dve.tensor_tensor(mods[:, layer, 4 * g:4 * g + 4, :],
                                  bank(f"ada{layer}.{g}")[:, 0:8].rearrange("p (a b) -> p a b", b=2), bias, ALU.add)\
                    .then_inc(*did("dve", f"ev:ada{layer}.{g}"))
            for which in range(2):
                dve.wait_ge(*seen(dve, f"ev:ada{layer}.{11}"))
                g = V(f"norm{which + 1}_g{layer}").unsqueeze(2).broadcast_to([P, DC, 2])
                dve.scalar_tensor_tensor(gains[:, 2 * layer + which], mods[:, layer, 24 * which + 8:24 * which + 16, :],
                                         1.0, g, ALU.add, ALU.mult).then_inc(*did("dve", f"gain{layer}.{which}"))

        q_t = part(ring, WORK, 2, T)
        k_t = part(ring, WORK + 1024, 2, T)
        vtok = part(ring, WORK + 2048, NT, 512)
        g_t = part(ring, WORK + 4096, RH, T)
        decay = part(ring, WORK + 6144, RH, 768)
        scores = part(ring, WORK + 9216, NT, T)
        rtmp = part(ring, WORK + 11264, 2, T)

        def proj_pe(pe, job, w, k_n, m0, rhs, n, m=P, ready=None):
            b = take(pe, job)
            for k in range(k_n):
                if ready is not None:
                    pe.wait_ge(*seen(pe, ready(k)))
                mm = pe.matmul(b[0:m, 0:n], w[:, k, m0:m0 + m], rhs(k), start=k == 0, stop=k == k_n - 1)
            return mm

        def win_pe(pe, groups):
            for g in groups:
                key = ("win", g) if g < 6 else ("win6", 0)
                pe.wait_ge(*arrived(key))
                w = slot(turn[key][0], DC, 512 if g < 6 else 416)
                for j in range(4):
                    last = [f"used:{key[0]}{key[1]}"] if j == 3 else []
                    m = P if g < 6 or j < 3 else 32
                    if g == 1:
                        b = take(pe, f"win1.{j}")
                        for k in range(DC):
                            mm = pe.matmul(b[:, :], xT[:, k, j * P:(j + 1) * P], w[:, k, :],
                                           start=k == 0, stop=k == DC - 1)
                    else:
                        mm = proj_pe(pe, f"win{g}.{j}", w, DC, j * P, lambda k: xT[:, k, :], T, m,
                                     (lambda k: f"n1.x{k}") if g == 0 and j == 0 else None)
                    mm.then_inc(*did("pe", f"win{g}.{j}", *last))

        def ret_feat_act(act):
            act.wait_ge(*seen(act, "n1.sum7"))
            for j in range(4):
                act.wait_ge(*seen(act, f"win0.{j}"))
                dst, c = ((q_t, 64 ** -0.5) if j < 2 else (k_t, 1.0))
                act.activation(dst[:, j % 2, :], bank(f"win0.{j}")[:, :], ACT.Copy, scale=c)\
                    .then_inc(*did("act", f"ev:win0.{j}"))
            for j in range(4):
                act.wait_ge(*seen(act, f"win1.{j}"))
                act.activation(vtok[:, j, :], bank(f"win1.{j}")[:, :], ACT.Copy).then_inc(*did("act", f"ev:win1.{j}"))
            for j in range(4):
                act.wait_ge(*seen(act, f"win2.{j}"))
                act.activation(g_t[:, j, :], bank(f"win2.{j}")[:, :], ACT.Silu).then_inc(*did("act", f"ev:win2.{j}"))

        def ret_pe(pe):
            for h in range(RH):
                half = slice(64 * (h % 2), 64 * (h % 2) + 64)
                for J in range(NT):
                    i0 = 0 if J < 2 else TC
                    b = take(pe, f"sc{h}.{J}")
                    if h == 0 and J == 0:
                        pe.wait_ge(*seen(pe, "ev:win0.3"))
                    pe.matmul(b[:, i0:T], k_t[half, h // 2, J * P:(J + 1) * P], q_t[half, h // 2, i0:T],
                              start=True, stop=True).then_inc(*did("pe", f"sc{h}.{J}"))
                b = take(pe, f"ro{h}")
                for J in range(NT):
                    i0 = 0 if J < 2 else TC
                    pe.wait_ge(*seen(pe, f"ev:sc{h}.{J}"))
                    if h == 0 and J == 0:
                        pe.wait_ge(*seen(pe, "ev:win1.3"))
                    mm = pe.matmul(b[:, i0:T], vtok[:, J, h * P:(h + 1) * P], scores[:, J, i0:T],
                                   start=J == 0, stop=J == NT - 1)
                mm.then_inc(*did("pe", f"ro{h}"))
                b = take(pe, f"rs{h}")
                pe.wait_ge(*seen(pe, f"rsq{h}"))
                pe.matmul(b[:, :], M["ones"], rtmp[:, 0, :], start=True, stop=True).then_inc(*did("pe", f"rs{h}"))

        def ret_act(act):
            for h in range(RH):
                act.wait_ge(*seen(act, f"ro{h}"))
                if h:
                    act.wait_ge(*seen(act, f"rs{h - 1}"))
                act.activation(rtmp[:, 0, :], bank(f"ro{h}")[:, :], ACT.Square).then_inc(*did("act", f"rsq{h}"))
                act.activation(mix[:, h, :], bank(f"ro{h}")[:, :], ACT.Copy).then_inc(*did("act", f"ev:ro{h}"))
                act.wait_ge(*seen(act, f"rs{h}"))
                if h:
                    act.wait_ge(*seen(act, f"rmul{h - 1}"))
                act.activation(rtmp[:, 1, :], bank(f"rs{h}")[:, :], ACT.Sqrt, bias=small[:, 0:1], scale=1.0 / P)\
                    .then_inc(*did("act", f"ev:rs{h}"))

        def ret_dve(dve):
            dve.wait_ge(*seen(dve, "levels"))
            for h in range(RH):
                for J in range(NT):
                    dve.wait_ge(*seen(dve, f"sc{h}.{J}"))
                    if h:
                        dve.wait_ge(*seen(dve, f"ro{h - 1}"))
                    u = 128 - P * (J % 2)
                    b = bank(f"sc{h}.{J}")
                    if J < 2:
                        dve.tensor_tensor(scores[:, J, 0:TC], b[:, 0:TC], decay[:, h, u:u + TC], ALU.mult)\
                            .then_inc(*did("dve"))
                        table = decay[:, h, 384 + u:384 + u + TC]
                    else:
                        table = decay[:, h, u:u + TC]
                    dve.tensor_tensor(scores[:, J, TC:T], b[:, TC:T], table, ALU.mult)\
                        .then_inc(*did("dve", f"ev:sc{h}.{J}"))
                dve.wait_ge(*seen(dve, f"ev:rs{h}"))
                dve.reciprocal(rtmp[:, 1, :], rtmp[:, 1, :]).then_inc(*did("dve", f"rinv{h}"))
                dve.wait_ge(*seen(dve, f"rinv{h}"))
                dve.tensor_tensor(g_t[:, h, :], g_t[:, h, :], rtmp[:, 1, :], ALU.mult).then_inc(*did("dve", f"rmul{h}"))
                dve.wait_ge(*seen(dve, f"rmul{h}"))
                dve.tensor_tensor(mix[:, h, :], mix[:, h, :], g_t[:, h, :], ALU.mult).then_inc(*did("dve", f"ret{h}"))

        wd_t = part(xT_t, 0, T)
        SHIFTED = [(3, r_t), (4, kr_t), (5, v_t)]
        lora_tmp = part(ring, WORK, 4, T)

        def shift_dve(dve):
            one = small[:, 8:24]
            for g in range(3, 7):
                for j in range(4):
                    m = P if g < 6 or j < 3 else 32
                    c = 4 * (g - 3) + j
                    dst = (r_t, kr_t, v_t)[g - 3][:, j, :] if g < 6 else \
                        (lora_tmp[:, 0, :], lora_tmp[:, 1, :], gate_in[:, 0, :], gate_in[:, 1, :])[j]
                    d3 = dst[0:m].rearrange("p (s t) -> p s t", s=2)
                    b3 = bank(f"win{g}.{j}")[0:m, :].rearrange("p (s t) -> p s t", s=2)
                    dve.wait_ge(*seen(dve, f"win{g}.{j}"))
                    dve.tensor_scalar(d3, b3, one[0:m, c:c + 1], None, ALU.mult).then_inc(*did("dve", f"sh{c}a"))
                    dve.wait_ge(*seen(dve, f"sh{c}a"))
                    dve.scalar_tensor_tensor(d3[:, :, 1:], b3[:, :, 0:TC - 1], V("mu0", c)[0:m], d3[:, :, 1:],
                                             ALU.mult, ALU.add).then_inc(*did("dve", f"sh{c}b"))
                    dve.wait_ge(*seen(dve, f"sh{c}b"))
                    dve.scalar_tensor_tensor(d3[:, :, 0:TC - 1], b3[:, :, 1:], V("mu1", c)[0:m], d3[:, :, 0:TC - 1],
                                             ALU.mult, ALU.add).then_inc(*did("dve", f"ev:win{g}.{j}"))

        def lora_pe(pe):
            w = slot(turn["lora", 0][0], 4, 512)
            pe.wait_ge(*arrived(("lora", 0)))
            for d in range(2):
                rows = slice(64 * d, 64 * d + 64)
                for c in range(NPAIR):
                    for what, i in (("lw", 0), ("la", 1)):
                        b = take(pe, f"{what}{d}.{c}")
                        if d == 0 and c == 0:
                            pe.wait_ge(*seen(pe, "tanh" if i == 0 else "ev:win6.1"))
                        pe.matmul(b[:, :], w[rows, i, c * P:(c + 1) * P], lora_tmp[rows, i, :], start=True, stop=True)\
                            .then_inc(*did("pe", f"{what}{d}.{c}"))
            for c in range(NPAIR):
                b = take(pe, f"kn{c}")
                pe.wait_ge(*seen(pe, f"ksq{c}"))
                pe.matmul(b[:, :], M["half_ones"], lora_tmp[:, 2, :], start=True, stop=True)\
                    .then_inc(*did("pe", f"kn{c}"))

        def lora_act(act):
            act.wait_ge(*seen(act, "ev:win6.0"))
            act.activation(lora_tmp[:, 0, :], lora_tmp[:, 0, :], ACT.Tanh).then_inc(*did("act", "tanh"))
            act.wait_ge(*seen(act, "ev:win6.3"))
            act.activation(gate_in[:, 0, :], gate_in[:, 0, :], ACT.Sigmoid).then_inc(*did("act"))
            act.activation(gate_in[0:32, 1, :], gate_in[0:32, 1, :], ACT.Sigmoid).then_inc(*did("act", "gate_in"))
            for d in range(2):
                for c in range(NPAIR):
                    act.wait_ge(*seen(act, f"lw{d}.{c}"))
                    act.activation(lw_t[d][:, c, :], bank(f"lw{d}.{c}")[:, :], ACT.Sigmoid, bias=V(f"w0_{d}", c))\
                        .then_inc(*did("act", f"ev:lw{d}.{c}"))
                    act.wait_ge(*seen(act, f"la{d}.{c}"))
                    act.activation(a_t[d][:, c, :], bank(f"la{d}.{c}")[:, :], ACT.Sigmoid, bias=V(f"a0_{d}", c))\
                        .then_inc(*did("act", f"ev:la{d}.{c}"))
            for c in range(NPAIR):
                act.wait_ge(*seen(act, f"kk0.{c}"))
                if c:
                    act.wait_ge(*seen(act, f"kn{c - 1}"))
                act.activation(lora_tmp[:, 2, :], kk_t[:, c, :], ACT.Square).then_inc(*did("act", f"ksq{c}"))
                act.wait_ge(*seen(act, f"kn{c}"))
                if c:
                    act.wait_ge(*seen(act, f"kk{c - 1}"))
                act.activation(lora_tmp[:, 3, :], bank(f"kn{c}")[:, :], ACT.Sqrt).then_inc(*did("act", f"ev:kn{c}"))

        def lora_dve(dve):
            dve.wait_ge(*seen(dve, "ev:win6.3"))
            for c in range(NPAIR):
                dve.tensor_scalar(kk_t[:, c, :], kr_t[:, c, :], V("k_k", c), None, ALU.mult)\
                    .then_inc(*did("dve", f"kk0.{c}"))
            for c in range(NPAIR):
                dve.wait_ge(*seen(dve, f"ev:kn{c}"))
                dve.tensor_scalar(lora_tmp[:, 3, :], lora_tmp[:, 3, :], 1e-12, None, ALU.max)\
                    .then_inc(*did("dve", f"kmax{c}"))
                dve.wait_ge(*seen(dve, f"kmax{c}"))
                dve.reciprocal(lora_tmp[:, 3, :], lora_tmp[:, 3, :]).then_inc(*did("dve", f"kinv{c}"))
                dve.wait_ge(*seen(dve, f"kinv{c}"))
                dve.tensor_tensor(kk_t[:, c, :], kk_t[:, c, :], lora_tmp[:, 3, :], ALU.mult)\
                    .then_inc(*did("dve", f"kk{c}"))
            for d in range(2):
                dve.wait_ge(*seen(dve, f"ev:lw{d}.3"))
                dve.tensor_scalar(lw_t[d], lw_t[d], LOG_DECAY, None, ALU.mult).then_inc(*did("dve", f"logw{d}"))

        def gate_pe(pe):
            w = slot(turn["lora", 0][0], 4, 512)
            for c in range(NPAIR):
                b = take(pe, f"gt{c}")
                if c == 0:
                    pe.wait_ge(*seen(pe, "gate_in"))
                pe.matmul(b[:, :], w[:, 2, c * P:(c + 1) * P], gate_in[:, 0, :], start=True, stop=False)
                pe.matmul(b[:, :], w[0:32, 3, c * P:(c + 1) * P], gate_in[0:32, 1, :], start=False, stop=True)\
                    .then_inc(*did("pe", f"gt{c}", *(["used:lora0"] if c == NPAIR - 1 else [])))

        def gate_act(act):
            for c in range(NPAIR):
                act.wait_ge(*seen(act, f"gt{c}"))
                act.activation(mix[:, 4 + c, :], bank(f"gt{c}")[:, :], ACT.Copy).then_inc(*did("act", f"ev:gt{c}"))

        w0 = WORK
        KR = part(ring, w0, NT, 2, P)
        BE = part(ring, w0 + 1024, 2, T)
        AT = part(ring, w0 + 2048, 8, P)
        RE = part(ring, w0 + 3072, 8, P)
        RB = part(ring, w0 + 4096, 8, P)
        BT = part(ring, w0 + 5120, 8, P)
        TI = BT
        TI_T = part(ring, w0 + 6144, 8, P)
        YL = part(ring, w0 + 7168, 8, P)
        WZ = YL
        RHS = part(ring, w0 + 8192, 8, P)
        b_tok = part(ring, w0 + 9216, NT, P)
        e_tok = part(ring, w0 + 9728, NT, P)
        v_pair = part(ring, w0 + 10240, T)
        v_tok = part(ring, w0 + 10752, NT, P)
        GM = part(ring, w0 + 11264, NT, 64)
        FM = part(ring, w0 + 11520, NT, 64)
        SH = part(ring, w0 + 11776, NT, 64)
        mid = part(ring, w0 + 12032, 4)
        rest = part(ring, w0 + 12036, 4)
        dmid = part(ring, w0 + 12040, 4)
        drest = part(ring, w0 + 12044, 4)
        step_decay = part(ring, w0 + 12048, 4)
        Fc, e1, e2, e3, kt, akk, ysum, bsum = (part(xT_t, i * T, T) for i in range(8))
        QM = e1
        UNITS = [(t, h) for h in range(2) for t in range(NT)]

        def settled(eng):
            eng.sem_inc(waited, 1)

        def half(h):
            return slice(64 * h, 64 * h + 64)

        def four(m):
            return m.unsqueeze(1).broadcast_to([P, 4, P])

        def pair_pe(pe, d, it):
            k = lambda s: named(f"{d}.", s)
            sn = lambda s: seen(pe, k(s), it)
            dd = lambda s: did("pe", k(s))
            first = ORDER[d][0]
            if d == 0:
                b = take(pe, k("vt"), it)
                pe.wait_ge(*sn("v_pair"))
                for t in range(NT):
                    mm = pe.transpose(b[:, t * P:(t + 1) * P], v_pair[:, t * P:(t + 1) * P], M["ident"])
                mm.then_inc(*dd("vt"))
            for name, ready, src in (("kt", "kappa", lambda t: KR[:, t, 0, :]),
                                     ("bt", "beta", lambda t: BE[:, 0, t * P:(t + 1) * P]),
                                     ("et", "eta", lambda t: BE[:, 1, t * P:(t + 1) * P])):
                b = take(pe, k(name), it)
                pe.wait_ge(*sn(ready))
                for t in range(NT):
                    mm = pe.transpose(b[:, t * P:(t + 1) * P], src(t), M["ident"])
                mm.then_inc(*dd(name))
            beta = lambda t, h: BE[half(h), 0, t * P:(t + 1) * P]
            eta = lambda t, h: BE[half(h), 1, t * P:(t + 1) * P]
            kappa = lambda t, h: KR[half(h), t, 0, :]
            rho = lambda t, h: KR[half(h), t, 1, :]

            def gram(name, lhs, rhs):
                for g in range(2):
                    b = take(pe, k(f"{name}{g}"), it)
                    for u, (t, h) in enumerate(UNITS[4 * g:4 * g + 4]):
                        mm = pe.matmul(b[:, u * P:(u + 1) * P], lhs(t, h), rhs(t, h), start=True, stop=True)
                    mm.then_inc(*dd(f"{name}{g}"))

            gram("BT", eta, kappa)
            gram("AT", beta, kappa)
            b = take(pe, k("BV"), it)
            pe.wait_ge(*sn("ev:BT1"))
            pe.wait_ge(*seen(pe, "ev:0.vt", it))
            for u, (t, h) in enumerate(UNITS):
                mm = pe.matmul(b[:, u * 64:(u + 1) * 64], BT[:, u, :], v_tok[:, t, half(h)], start=True, stop=True)
            mm.then_inc(*dd("BV"))
            gram("A", kappa, beta)
            pe.wait_ge(*sn("rho"))
            gram("RE", eta, rho)
            gram("RB", beta, rho)
            for li in range(1, len(LEVELS)):
                for g in range(2):
                    b = take(pe, k(f"Y{li}.{g}"), it)
                    pe.wait_ge(*sn(f"T{li - 1}.{g}"))
                    for u in range(4 * g, 4 * g + 4):
                        mm = pe.matmul(b[:, (u % 4) * P:(u % 4 + 1) * P], AT[:, u, :], TI[:, u, :], start=True, stop=True)
                    mm.then_inc(*dd(f"Y{li}.{g}"))
                for g in range(2):
                    pe.wait_ge(*sn(f"ev:Y{li}.{g}"))
                    pe.wait_ge(*sn(f"TT{li - 1}.{g}"))
                    if li < len(LEVELS) - 1:
                        b = take(pe, k(f"U{li}.{g}"), it)
                        for u in range(4 * g, 4 * g + 4):
                            mm = pe.matmul(b[:, (u % 4) * P:(u % 4 + 1) * P], TI_T[:, u, :], YL[:, u, :],
                                           start=True, stop=True)
                        mm.then_inc(*dd(f"U{li}.{g}"))
                    b = take(pe, k(f"V{li}.{g}"), it)
                    for u in range(4 * g, 4 * g + 4):
                        mm = pe.matmul(b[:, (u % 4) * P:(u % 4 + 1) * P], YL[:, u, :], TI_T[:, u, :], start=True, stop=True)
                    mm.then_inc(*dd(f"V{li}.{g}"))
            for g in range(2):
                b = take(pe, k(f"WZ{g}"), it)
                pe.wait_ge(*sn(f"TT{len(LEVELS) - 1}.{g}"))
                pe.wait_ge(*sn("ev:kt"))
                pe.wait_ge(*sn("ev:BV"))
                for u in range(4 * g, 4 * g + 4):
                    mm = pe.matmul(b[:, (u % 4) * P:(u % 4 + 1) * P], TI_T[:, u, :], RHS[:, u, :], start=True, stop=True)
                mm.then_inc(*dd(f"WZ{g}"))
            b = take(pe, k("GF"), it)
            pe.wait_ge(*sn("ev:WZ1"))
            for i in range(3):
                t = ORDER[d][i]
                for h in range(2):
                    u = 4 * h + t
                    if i:
                        pe.matmul(b[half(h), i * 64:(i + 1) * 64], WZ[:, u, 0:64], b_tok[:, t, half(h)],
                                  start=True, stop=True)
                    f = b[half(h), 256 + i * 64:256 + (i + 1) * 64]
                    pe.matmul(f, e_tok[:, t, half(h)], v_tok[:, t, half(h)], start=True, stop=False)
                    mm = pe.matmul(f, b_tok[:, t, half(h)], WZ[:, u, 64:128], start=False, stop=True)
            mm.then_inc(*dd("GF"))
            b = take(pe, k("Q"), it)
            pe.wait_ge(*sn("ev:RB1"))
            for t, h in UNITS:
                if t != first:
                    mm = pe.matmul(b[half(h), t * P:(t + 1) * P], WZ[:, 4 * h + t, 0:64], RB[:, 4 * h + t, :],
                                   start=True, stop=True)
            mm.then_inc(*dd("Q"))
            for i in (1, 2):
                b = take(pe, k(f"S{i}"), it)
                pe.wait_ge(*sn("ev:GF" if i == 1 else "ev:S1"))
                settled(pe)
                for h in range(2):
                    mm = pe.matmul(b[half(h), 0:64], GM[half(h), i, :], (FM[half(h), 0, :] if i == 1 else SH[half(h), i, :]),
                                   start=True, stop=True)
                mm.then_inc(*dd(f"S{i}"))
            b = take(pe, k("y"), it)
            pe.wait_ge(*sn("ev:Q"))
            pe.wait_ge(*sn("ev:S2"))
            for i in range(NT):
                t = ORDER[d][i]
                state = (None, FM[:, 0, :], SH[:, 2, :], SH[:, 3, :])[i]
                for h in range(2):
                    u, o = 4 * h + t, b[half(h), t * P:(t + 1) * P]
                    pe.matmul(o, v_tok[:, t, half(h)], RE[:, u, :], start=True, stop=False)
                    mm = pe.matmul(o, WZ[:, u, 64:128], RB[:, u, :], start=False, stop=i == 0)
                    if i:
                        mm = pe.matmul(o, state[half(h)], QM[half(h), t * P:(t + 1) * P], start=False, stop=True)
            mm.then_inc(*dd("y"))

        def pair_act(act, d, it):
            k = lambda s: named(f"{d}.", s)
            sn = lambda s: seen(act, k(s), it)
            dd = lambda s: did("act", k(s))
            if d == 0:
                act.wait_ge(*seen(act, "ev:1.y", it, 1))
                act.activation(v_pair, v_t[:, it, :], ACT.Copy).then_inc(*dd("v_pair"))
                act.wait_ge(*sn("vt"))
                act.activation(v_tok, bank(k("vt"))[:, :].rearrange("p (a b) -> p a b", b=P), ACT.Copy)\
                    .then_inc(*dd("ev:vt"))
            act.wait_ge(*sn("F"))
            for dst, src, sign, ready in (((e1, e1, 1.0, "E"), (e2, Fc, 1.0, "F"), (e3, Fc, -1.0, "F")) if d == 0 else
                                          ((e2, e1, -1.0, "E"), (e3, e1, 1.0, "E"), (e1, Fc, -1.0, "F"))):
                act.wait_ge(*sn(ready))
                name = "e1" if dst is e1 else "e2" if dst is e2 else "e3"
                if d == 1 and dst is e1:
                    act.wait_ge(*sn("e3"))
                act.activation(dst, src, ACT.Exp, scale=sign).then_inc(*dd(name))
            act.activation(part(ring, w0 + 12040, 8), part(ring, w0 + 12032, 8), ACT.Exp).then_inc(*dd("dmid"))
            act.wait_ge(*sn("kt"))
            act.activation(RHS[:, :, 0:64].rearrange("p (h t) c -> p h t c", h=2),
                           bank(k("kt"))[:, :].rearrange("p (t h c) -> p h t c", h=2, c=64), ACT.Copy)\
                .then_inc(*dd("ev:kt"))
            for name, dst in (("bt", b_tok), ("et", e_tok)):
                act.wait_ge(*sn(name))
                act.activation(dst, bank(k(name))[:, :].rearrange("p (a b) -> p a b", b=P), ACT.Copy)\
                    .then_inc(*dd("ev:" + name))
            act.wait_ge(*sn("BV"))
            act.activation(RHS[:, :, 64:128], bank(k("BV"))[:, :].rearrange("p (u c) -> p u c", c=64), ACT.Copy)\
                .then_inc(*dd("ev:BV"))
            for li in range(1, len(LEVELS)):
                for g in range(2):
                    act.wait_ge(*sn(f"Y{li}.{g}"))
                    act.activation(YL[:, 4 * g:4 * g + 4, :],
                                   bank(k(f"Y{li}.{g}"))[:, :].rearrange("p (a b) -> p a b", b=P), ACT.Copy)\
                        .then_inc(*dd(f"ev:Y{li}.{g}"))
            for g in range(2):
                act.wait_ge(*sn(f"WZ{g}"))
                act.activation(WZ[:, 4 * g:4 * g + 4, :], bank(k(f"WZ{g}"))[:, :].rearrange("p (a b) -> p a b", b=P),
                               ACT.Copy).then_inc(*dd(f"ev:WZ{g}"))

        def pair_pool(pool, d, it):
            k = lambda s: named(f"{d}.", s)
            pool.wait_ge(*seen(pool, *(("ev:1.y", it, 1) if d == 0 else ("ev:0.y", it))))
            settled(pool)
            for g in range(2):
                pool.tensor_copy(TI_T[:, 4 * g:4 * g + 4, :], four(M["ident"])).then_inc(*did("pool", k(f"TT_id{g}")))
            pool.wait_ge(*seen(pool, k("BV"), it))
            settled(pool)
            for g in range(2):
                pool.tensor_copy(TI[:, 4 * g:4 * g + 4, :], four(M["ident"])).then_inc(*did("pool", k(f"T_id{g}")))

        def pair_dve(dve, d, it):
            k = lambda s: named(f"{d}.", s)
            sn = lambda s: seen(dve, k(s), it)
            dd = lambda *s: did("dve", *[k(x) for x in s])
            r, kr, kk, a, lw = (t[:, it, :] for t in (r_t, kr_t, kk_t, a_t[d], lw_t[d]))
            f4 = Fc.rearrange("p (t c) -> p t c", c=P)
            dve.wait_ge(*seen(dve, *(("ev:1.y", it, 1) if d == 0 else ("ev:0.y", it))))
            for t in range(NT):
                dve.tensor_tensor_scan(Fc[:, t * P:(t + 1) * P], M["ones"], lw_t[d][:, it, t * P:(t + 1) * P], 0.0,
                                       ALU.mult, ALU.add).then_inc(*dd(f"scan{t}"))
            dve.tensor_tensor(akk, a, kk, ALU.mult).then_inc(*dd("akk"))
            ka = vec[:, bass.ds(VEC["k_a"][0] + it, 1)]
            dve.tensor_scalar(kt, a, 1.0, ka, ALU.subtract, ALU.mult).then_inc(*dd("kt1"))
            dve.wait_ge(*sn("scan3"))
            dve.tensor_copy(mid, f4[:, :, 63]).then_inc(*dd("mid"))
            dve.wait_ge(*sn("mid"))
            dve.tensor_tensor(rest, f4[:, :, P - 1], mid, ALU.subtract).then_inc(*dd("rest"))
            dve.wait_ge(*sn("rest"))
            dve.tensor_tensor(f4, f4, mid.unsqueeze(2).broadcast_to([P, NT, P]), ALU.subtract).then_inc(*dd("F"))
            dve.wait_ge(*sn("F"))
            dve.tensor_tensor(e1, Fc, lw, ALU.subtract).then_inc(*dd("E"))
            dve.wait_ge(*sn("kt1"))
            dve.scalar_tensor_tensor(kt, kt, 1.0, kr, ALU.add, ALU.mult).then_inc(*dd("kt2"))
            dve.wait_ge(*sn("kt2"))
            if d == 0:
                dve.tensor_tensor(bsum, kt, r, ALU.mult).then_inc(*dd("bsum"))
            r4, kk4 = (x.rearrange("p (t c) -> p t c", c=P) for x in (e2, e1))
            dve.wait_ge(*sn("e1"))
            dve.tensor_tensor(KR[:, :, 0, :], kk_t[:, it, :].rearrange("p (t c) -> p t c", c=P), kk4, ALU.mult)\
                .then_inc(*dd("kappa"))
            dve.wait_ge(*sn("e3"))
            dve.scalar_tensor_tensor(BE[:, 0, :], akk, -1.0, e3, ALU.mult, ALU.mult).then_inc(*dd("beta"))
            dve.tensor_tensor(BE[:, 1, :], kt, e3, ALU.mult).then_inc(*dd("eta"))
            dve.wait_ge(*sn("e2"))
            dve.tensor_tensor(KR[:, :, 1, :], r_t[:, it, :].rearrange("p (t c) -> p t c", c=P), r4, ALU.mult)\
                .then_inc(*dd("rho"))
            dve.wait_ge(*sn("dmid"))
            leave, come = (drest, dmid) if d == 0 else (dmid, drest)
            for i in range(3):
                x, y = ORDER[d][i], ORDER[d][i + 1]
                dve.tensor_tensor(step_decay[:, i:i + 1], leave[:, x:x + 1], come[:, y:y + 1], ALU.mult)\
                    .then_inc(*dd(f"dc{i}"))
            strict, incl = ("lt", "le") if d == 0 else ("gt", "ge")

            def v3(job):
                return bank(k(job))[:, :].rearrange("p (a b) -> p a b", b=P)

            def masked(name, dst, m, g):
                dve.wait_ge(*sn(f"{name}{g}"))
                dve.tensor_tensor(dst[:, 4 * g:4 * g + 4, :], v3(f"{name}{g}"), four(M[m]), ALU.mult)\
                    .then_inc(*dd(f"ev:{name}{g}"))

            for g in range(2):
                masked("BT", BT, strict, g)
            for g in range(2):
                masked("AT", AT, strict, g)
            for g in range(2):
                gs = slice(4 * g, 4 * g + 4)
                dve.wait_ge(*seen(dve, k(f"TT_id{g}"), it))
                dve.wait_ge(*sn(f"ev:AT{g}"))
                settled(dve)
                dve.copy_predicated(TI_T[:, gs, :], four(level[:, 1 - d, 0, :]), AT[:, gs, :]).then_inc(*dd(f"TT0.{g}"))
                dve.wait_ge(*seen(dve, k(f"T_id{g}"), it))
                dve.wait_ge(*sn(f"A{g}"))
                settled(dve)
                dve.copy_predicated(TI[:, gs, :], four(level[:, d, 0, :]), v3(f"A{g}")).then_inc(*dd(f"T0.{g}", f"ev:A{g}"))
            for g in range(2):
                masked("RE", RE, incl, g)
            for g in range(2):
                masked("RB", RB, incl, g)
            for li in range(1, len(LEVELS)):
                for g in range(2):
                    gs = slice(4 * g, 4 * g + 4)
                    if li < len(LEVELS) - 1:
                        dve.wait_ge(*sn(f"U{li}.{g}"))
                        settled(dve)
                        dve.copy_predicated(TI[:, gs, :], four(level[:, d, li, :]), v3(f"U{li}.{g}"))\
                            .then_inc(*dd(f"T{li}.{g}", f"ev:U{li}.{g}"))
                    dve.wait_ge(*sn(f"V{li}.{g}"))
                    settled(dve)
                    dve.copy_predicated(TI_T[:, gs, :], four(level[:, 1 - d, li, :]), v3(f"V{li}.{g}"))\
                        .then_inc(*dd(f"TT{li}.{g}", f"ev:V{li}.{g}"))
            dve.wait_ge(*sn("GF"))
            gf = bank(k("GF"))[:, :].rearrange("p (a b) -> p a b", b=64)
            dve.tensor_tensor(GM[:, 1:3, :], gf[:, 1:3, :], M["eye2"][:, 0:64].unsqueeze(1).broadcast_to([P, 2, 64]),
                              ALU.add).then_inc(*dd("GM"))
            dve.wait_ge(*sn("dc2"))
            dve.tensor_tensor(FM[:, 0:3, :], gf[:, 4:7, :], step_decay[:, 0:3].unsqueeze(2).broadcast_to([P, 3, 64]),
                              ALU.mult).then_inc(*dd("ev:GF"))
            dve.wait_ge(*sn("Q"))
            q0, q1 = (1, 4) if d == 0 else (0, 4)
            lots = [(1, 4)] if d == 0 else [(0, 1), (2, 4)]
            for n, (x, y) in enumerate(lots):
                dve.tensor_tensor(QM.rearrange("p (t c) -> p t c", c=P)[:, x:y, :], v3("Q")[:, x:y, :], KR[:, x:y, 1, :],
                                  ALU.add).then_inc(*dd(*(["ev:Q"] if n == len(lots) - 1 else [])))
            for i in (1, 2):
                dve.wait_ge(*sn(f"S{i}"))
                dve.wait_ge(*sn("ev:GF"))
                dve.scalar_tensor_tensor(SH[:, i + 1, :], bank(k(f"S{i}"))[:, 0:64], step_decay[:, i:i + 1],
                                         FM[:, i, :], ALU.mult, ALU.add).then_inc(*dd(f"ev:S{i}"))
            if d == 1:
                dve.tensor_tensor(kt, kt, r, ALU.mult).then_inc(*dd("bs1"))
                dve.wait_ge(*sn("bs1"))
                dve.tensor_tensor(r_t[:, it, :], bsum, kt, ALU.add).then_inc(*dd("bs2"))
            dve.wait_ge(*sn("y"))
            if d == 0:
                dve.tensor_copy(ysum, bank(k("y"))[:, :]).then_inc(*dd("ev:y"))
            else:
                dve.tensor_tensor(kk_t[:, it, :], bank(k("y"))[:, :], ysum, ALU.add).then_inc(*dd("ev:y"))

        def pair_loop(eng, name, body):
            base = L.enter(name, "pair")
            with eng.Fori(0, NPAIR) as it:
                for d in range(2):
                    body(eng, d, it)
            L.leave(name, base, NPAIR)

        post = part(ring, WORK, 4, T)

        def post_pe(pe):
            for c in range(NPAIR):
                for name, ready, src in (("pm", None, kk_t[:, c, :]), ("pv", f"psq{c}", post[:, 0, :]),
                                         ("pb", f"prk{c}", post[:, 1, :])):
                    b = take(pe, f"{name}{c}")
                    if ready:
                        pe.wait_ge(*seen(pe, ready))
                    pe.matmul(b[:, :], M["half_ones"], src, start=True, stop=True).then_inc(*did("pe", f"{name}{c}"))

        def post_act(act):
            for c in range(NPAIR):
                act.wait_ge(*seen(act, f"ev:pm{c}"))
                if c:
                    act.wait_ge(*seen(act, f"pv{c - 1}"))
                act.activation(post[:, 0, :], kk_t[:, c, :], ACT.Square).then_inc(*did("act", f"psq{c}"))
                act.wait_ge(*seen(act, f"pv{c}"))
                if c:
                    act.wait_ge(*seen(act, f"pn{c - 1}"))
                act.activation(post[:, 2, :], bank(f"pv{c}")[:, :], ACT.Sqrt, bias=small[:, 1:2], scale=1.0 / 64)\
                    .then_inc(*did("act", f"ev:pv{c}"))

        def post_dve(dve):
            for c in range(NPAIR):
                y = kk_t[:, c, :]
                if c:
                    dve.wait_ge(*seen(dve, f"pb{c - 1}"))
                dve.tensor_scalar(post[:, 1, :], r_t[:, c, :], V("r_k", c), None, ALU.mult).then_inc(*did("dve", f"prk{c}"))
                dve.wait_ge(*seen(dve, f"pm{c}"))
                dve.scalar_tensor_tensor(y, bank(f"pm{c}")[:, :], -1.0 / 64, y, ALU.mult, ALU.add)\
                    .then_inc(*did("dve", f"ev:pm{c}"))
                dve.wait_ge(*seen(dve, f"pb{c}"))
                dve.tensor_tensor(v_t[:, c, :], bank(f"pb{c}")[:, :], v_t[:, c, :], ALU.mult)\
                    .then_inc(*did("dve", f"ev:pb{c}"))
                dve.wait_ge(*seen(dve, f"ev:pv{c}"))
                dve.reciprocal(post[:, 2, :], post[:, 2, :]).then_inc(*did("dve", f"pinv{c}"))
                dve.wait_ge(*seen(dve, f"pinv{c}"))
                dve.tensor_tensor(y, y, post[:, 2, :], ALU.mult).then_inc(*did("dve", f"pn{c}"))
                dve.wait_ge(*seen(dve, f"pn{c}"))
                dve.tensor_scalar(y, y, V("lnx_w", c), V("lnx_b", c), ALU.mult, ALU.add).then_inc(*did("dve", f"pl{c}"))
                dve.wait_ge(*seen(dve, f"pl{c}"))
                dve.tensor_tensor(y, y, v_t[:, c, :], ALU.add).then_inc(*did("dve", f"py{c}"))
                dve.wait_ge(*seen(dve, f"py{c}"))
                dve.tensor_tensor(mix[:, 4 + c, :], mix[:, 4 + c, :], y, ALU.mult).then_inc(*did("dve", f"mix{c}"))

        def wout_pe(pe, array, tag, a, ready):
            for g in range(2):
                key = (array, g)
                pe.wait_ge(*arrived(key))
                w = slot(turn[key][0], DC, 512)
                for j in range(4):
                    if g == 0 and j == 0:
                        pe.wait_ge(*seen(pe, ready))
                    mm = proj_pe(pe, f"{tag}.{4 * g + j}", w, DC, j * P, lambda k: mix[:, k, a:T], T - a)
                    mm.then_inc(*did("pe", f"{tag}.{4 * g + j}", *([f"used:{array}{g}"] if j == 3 else [])))

        def residual_dve(dve, tag, layer, m, a, h):
            for c in range(DC):
                dve.wait_ge(*seen(dve, f"{tag}.{c}"))
                for x in range(a, T, TC):
                    dve.scalar_tensor_tensor(h[:, c, x:x + TC], bank(f"{tag}.{c}")[:, x - a:x - a + TC],
                                             mods[:, layer, 8 * m + c, x // TC:x // TC + 1], h[:, c, x:x + TC],
                                             ALU.mult, ALU.add)\
                        .then_inc(*did("dve", *([f"ev:{tag}.{c}", f"{tag}.h{c}"] if x == T - TC else [])))

        route_w = part(feat_t, 8192, DC, NR)
        logits = part(feat_t, 8480, NT, NR)
        route = part(feat_t, 8624, 30, NT * EPG)
        gates = part(feat_t, 9584, NT, NE)
        gates_T = part(feat_t, 9712, T)
        gate_row = part(feat_t, 10224, 4, T)
        hid = part(feat_t, 12272, 2, T)
        sil = part(feat_t, 13296, 2, T)
        route_b = part(feat_t, 14320, NR)
        rank = part(feat_t, 14356, EPG)

        def route_pe(pe, l, a):
            tag, nt = f"m{l}", (T - a) // P
            b = take(pe, tag + ".logits")
            pe.wait_ge(router_in, 48 * (l + 1))
            for t in range(nt):
                for k in range(DC):
                    if t == 0:
                        pe.wait_ge(*seen(pe, f"n2{l}.x{k}"))
                    pe.matmul(b[:, t * NR:(t + 1) * NR], xT[:, k, a + t * P:a + (t + 1) * P], route_w[:, k, :],
                              start=k == 0, stop=False)
                mm = pe.matmul(b[:, t * NR:(t + 1) * NR], M["ones"][0:1, :], route_b[0:1, :], start=False, stop=True)
            mm.then_inc(*did("pe", tag + ".logits"))
            b = take(pe, tag + ".gT")
            pe.wait_ge(*seen(pe, tag + ".gates"))
            for t in range(nt):
                mm = pe.transpose(b[0:NE, t * P:(t + 1) * P], gates[:, t, :], M["ident"])
            mm.then_inc(*did("pe", tag + ".gT"))

        def route_dve(dve, l, a):
            tag, nt = f"m{l}", (T - a) // P
            n = [0]

            def link(ins):
                n[0] += 1
                ins.then_inc(*did("dve", f"{tag}.route{n[0]}"))
                dve.wait_ge(*seen(dve, f"{tag}.route{n[0]}"))

            def row(i, w):
                return route[:, i, 0:nt * w].rearrange("p (t w) -> p t w", w=w)

            def wide(x, w):
                return x.broadcast_to([P, nt, w])

            lg, one = logits[:, 0:nt, :], lambda i: row(i, 1)

            def first_of(dst, x, top, w, i):
                link(dve.tensor_tensor(row(i, w), x, wide(top, w), ALU.is_equal))
                link(dve.tensor_tensor(row(i, w), row(i, w),
                                       rank[:, EPG - w:EPG].unsqueeze(1).broadcast_to([P, nt, w]), ALU.mult))
                link(dve.tensor_reduce(one(i + 1), row(i, w), AX, ALU.max))
                link(dve.tensor_tensor(dst, row(i, w), wide(one(i + 1), w), ALU.is_equal))

            dve.wait_ge(*seen(dve, tag + ".logits"))
            dve.tensor_copy(lg, bank(tag + ".logits")[:, 0:nt * NR].rearrange("p (t r) -> p t r", r=NR))\
                .then_inc(*did("dve", f"ev:{tag}.logits"))
            dve.wait_ge(*seen(dve, f"ev:{tag}.logits"))
            groups, experts = lg[:, :, 0:NG], lg[:, :, NG:NR]
            link(dve.tensor_reduce(one(0), groups, AX, ALU.max))
            link(dve.tensor_tensor(row(1, NG), groups, wide(one(0), NG), ALU.subtract))
            first_of(row(2, NG), groups, one(0), NG, 3)
            chosen = row(5, EPG)
            for g in range(NG):
                x = experts[:, :, g * EPG:(g + 1) * EPG]
                oh = wide(row(2, NG)[:, :, g:g + 1], EPG)
                link(dve.tensor_tensor(chosen if g == 0 else row(6, EPG), x, oh, ALU.mult))
                if g:
                    link(dve.tensor_tensor(chosen, chosen, row(6, EPG), ALU.add))
            link(dve.tensor_reduce(one(7), chosen, AX, ALU.max))
            first_of(row(8, EPG), chosen, one(7), EPG, 9)
            link(dve.scalar_tensor_tensor(row(11, EPG), row(8, EPG), -3e38, chosen, ALU.mult, ALU.add))
            link(dve.tensor_reduce(one(12), row(11, EPG), AX, ALU.max))
            first_of(row(13, EPG), row(11, EPG), one(12), EPG, 14)
            dve.tensor_tensor(one(16), one(12), one(7), ALU.subtract).then_inc(*did("dve", tag + ".gap"))
            dve.wait_ge(*seen(dve, tag + ".exps"))
            link(dve.tensor_reduce(one(17), row(1, NG), AX, ALU.add))
            link(dve.tensor_scalar(one(18), one(16), 1.0, None, ALU.add))
            link(dve.tensor_tensor(one(17), one(17), one(18), ALU.mult))
            link(dve.reciprocal(one(19), one(17)))
            link(dve.tensor_tensor(one(20), one(19), one(16), ALU.mult))
            link(dve.tensor_tensor(row(21, EPG), row(8, EPG), wide(one(19), EPG), ALU.mult))
            link(dve.tensor_tensor(row(22, EPG), row(13, EPG), wide(one(20), EPG), ALU.mult))
            link(dve.tensor_tensor(row(21, EPG), row(21, EPG), row(22, EPG), ALU.add))
            for g in range(NG):
                dve.tensor_tensor(gates[:, 0:nt, g * EPG:(g + 1) * EPG], row(21, EPG),
                                  wide(row(2, NG)[:, :, g:g + 1], EPG), ALU.mult)\
                    .then_inc(*did("dve", *([tag + ".gates"] if g == NG - 1 else [])))
            dve.wait_ge(*seen(dve, tag + ".gT"))
            dve.tensor_copy(gates_T[0:NE, 0:T - a], bank(tag + ".gT")[0:NE, 0:T - a]).then_inc(*did("dve", f"ev:{tag}.gT"))

        def route_act(act, l, a):
            tag, nt = f"m{l}", (T - a) // P
            act.wait_ge(*seen(act, tag + ".gap"))
            act.activation(route[:, 1, 0:nt * NG], route[:, 1, 0:nt * NG], ACT.Exp).then_inc(*did("act"))
            act.activation(route[:, 16, 0:nt], route[:, 16, 0:nt], ACT.Exp).then_inc(*did("act", tag + ".exps"))

        def expert_pe(pe, l, a, s, it, first_turn):
            n, k_ = T - a, lambda x: named(f"e{l}.{s}.", x)
            w = slot(s, 3, DC, 256)
            down = part(ring, s * SLOT + 4096, 2, D)
            pe.wait_ge(loaded[s], it * 16 + 16 * first_turn)
            for hc in range(2):
                for what, i in (("g", 0), ("u", 1)):
                    mm = None
                    b = take(pe, k_(f"{what}{hc}"), it)
                    for k in range(DC):
                        mm = pe.matmul(b[:, 0:n], w[:, i, k, hc * P:(hc + 1) * P], xT[:, k, a:T],
                                       start=k == 0, stop=k == DC - 1)
                    mm.then_inc(*did("pe", k_(f"{what}{hc}")))
            for c in range(DC):
                b = take(pe, k_(f"y{c}"), it)
                for hc in range(2):
                    if c == 0:
                        pe.wait_ge(*seen(pe, k_(f"hid{hc}"), it))
                    mm = pe.matmul(b[:, 0:n], down[:, hc, c * P:(c + 1) * P], hid[:, hc, 0:n], start=hc == 0, stop=hc == 1)
                mm.then_inc(*did("pe", k_(f"y{c}")))

        def expert_act(act, l, a, s, it):
            n, k_ = T - a, lambda x: named(f"e{l}.{s}.", x)
            before = (f"e{l}.{s - 1}.", 0) if s else (f"e{l}.3.", 1)
            for hc in range(2):
                act.wait_ge(*seen(act, k_(f"g{hc}"), it))
                act.wait_ge(*seen(act, f"{before[0]}hid{hc}", it, before[1]))
                act.activation(sil[:, hc, 0:n], bank(k_(f"g{hc}"))[:, 0:n], ACT.Silu).then_inc(*did("act", k_(f"ev:g{hc}")))

        def expert_dve(dve, l, a, s, it, first_turn):
            n, k_ = T - a, lambda x: named(f"e{l}.{s}.", x)
            before = (f"e{l}.{s - 1}.", 0) if s else (f"e{l}.3.", 1)
            for hc in range(2):
                dve.wait_ge(*seen(dve, k_(f"u{hc}"), it))
                dve.wait_ge(*seen(dve, k_(f"ev:g{hc}"), it))
                dve.tensor_tensor(sil[:, hc, 0:n], bank(k_(f"u{hc}"))[:, 0:n], sil[:, hc, 0:n], ALU.mult)\
                    .then_inc(*did("dve", k_(f"ev:u{hc}")))
                dve.wait_ge(*seen(dve, k_(f"ev:u{hc}"), it))
                if hc == 0:
                    dve.wait_ge(gate_rows[s], it * 16 + 16 * first_turn)
                dve.wait_ge(*seen(dve, before[0] + "y7", it, before[1]))
                dve.tensor_tensor(hid[:, hc, 0:n], sil[:, hc, 0:n], gate_row[:, s, 0:n], ALU.mult)\
                    .then_inc(*did("dve", k_(f"hid{hc}")))
            for c in range(DC):
                dve.wait_ge(*seen(dve, k_(f"y{c}"), it))
                dve.tensor_tensor(yT[:, c, 0:n], bank(k_(f"y{c}"))[:, 0:n], yT[:, c, 0:n], ALU.add)\
                    .then_inc(*did("dve", k_(f"ev:y{c}")))

        def expert_loop(eng, name, l, body):
            base = L.enter(name, f"experts{l}")
            with eng.Fori(0, NE // 4) as it:
                for s in range(4):
                    body(s, it)
            L.leave(name, base, NE // 4)

        def gate_turn(l, s):
            return l * (NE // 4) + 1

        def add_mixture_dve(dve, l, a):
            for c in range(DC):
                for x in range(a, T, TC):
                    dve.scalar_tensor_tensor(hT[:, c, x:x + TC], yT[:, c, x - a:x - a + TC],
                                             mods[:, l, 40 + c, x // TC:x // TC + 1], hT[:, c, x:x + TC],
                                             ALU.mult, ALU.add).then_inc(*did("dve", *([f"h{l}.{c}"] if x == T - TC else [])))

        F0 = 8192
        cq = part(feat_t, F0, 3, TC)
        ckv = part(feat_t, F0 + 768, 2, T)
        kpe = part(feat_t, F0 + 1792, T)
        qn = part(feat_t, F0 + 2304, MH, TC)
        qpe = part(feat_t, F0 + 4352, 4, TC)
        rope = part(feat_t, F0 + 5376, 2, TC)
        pmax = part(feat_t, F0 + 5888, 16)
        psum_ = part(feat_t, F0 + 5904, 16)
        kn = yT
        val = part(xT_t, 0, NT, D)
        prob = part(feat_t, F0 + 6144, 2, T)
        rope_tmp = part(feat_t, F0 + 7168, T)

        def mla_pe(pe):
            w = slot(turn["mla_in", 0][0], DC, 768)
            pe.wait_ge(*arrived(("mla_in", 0)))
            for j in range(6):
                a = TC if j < 3 else 0
                mm = proj_pe(pe, f"mi{j}", w, DC, j * P, lambda k: xT[:, k, a:T], T - a, P,
                             (lambda k: f"n11.x{k}") if j == 0 else None)
                mm.then_inc(*did("pe", f"mi{j}", *(["used:mla_in0"] if j == 5 else [])))
            b = take(pe, "kswap")
            pe.wait_ge(*seen(pe, "ev:mi5"))
            pe.matmul(b[:, 0:TC], M["swap"], kpe[:, TC:T], start=True, stop=True).then_inc(*did("pe", "kswap"))
            norm_pe(pe, "nq", TC, 3, (hm_t, 0))
            norm_pe(pe, "nkv", T, 2, (hm_t, 1536))
            w = slot(turn["mla_uq", 0][0], 3, 1536)
            pe.wait_ge(*arrived(("mla_uq", 0)))
            for j in range(12):
                mm = proj_pe(pe, f"uq{j}", w, 3, j * P, lambda k: cq[:, k, :], TC, P,
                             (lambda k: f"cq{k}") if j == 0 else None)
                mm.then_inc(*did("pe", f"uq{j}", *(["used:mla_uq0"] if j == 11 else [])))
            for j in range(4):
                b = take(pe, f"qswap{j}")
                pe.wait_ge(*seen(pe, f"ev:uq{8 + j}"))
                pe.matmul(b[:, 0:TC], M["swap"], qpe[:, j, :], start=True, stop=True).then_inc(*did("pe", f"qswap{j}"))
            w = slot(turn["mla_ukv", 0][0], 2, 2048)
            pe.wait_ge(*arrived(("mla_ukv", 0)))
            for j in range(8):
                proj_pe(pe, f"uk{j}", w, 2, j * P, lambda k: ckv[:, k, :], T, P,
                        (lambda k: f"ckv{k}") if j == 0 else None).then_inc(*did("pe", f"uk{j}"))
            for t in range(NT):
                for g in range(2):
                    b = take(pe, f"uv{t}.{g}")
                    for k in range(2):
                        mm = pe.matmul(b[:, :], ckv[:, k, t * P:(t + 1) * P], w[:, k, 1024 + 512 * g:1536 + 512 * g],
                                       start=k == 0, stop=k == 1)
                    mm.then_inc(*did("pe", f"uv{t}.{g}", *(["used:mla_ukv0"] if t == 3 and g == 1 else [])))
            for h in range(MH + 1):
                if h < MH:
                    for qt in range(2):
                        qs = slice(qt * P, (qt + 1) * P)
                        b = take(pe, f"s{h}.{qt}")
                        if h == 0:
                            pe.wait_ge(*seen(pe, "ev:uk7"))
                            pe.wait_ge(*seen(pe, "qpe3"))
                        pe.matmul(b[:, :], qn[:, h, qs], kn[:, h, :], start=True, stop=False)
                        pe.matmul(b[:, :], qpe[half(h % 2), h // 2, qs], kpe[half(h % 2), :], start=False, stop=True)\
                            .then_inc(*did("pe", f"s{h}.{qt}"))
                if h:
                    g = h - 1
                    for kp in range(2):
                        b = take(pe, f"pt{g}.{kp}")
                        for i in range(2):
                            for qt in range(2):
                                if kp == 0 and i == 0:
                                    pe.wait_ge(*seen(pe, f"p{g}.{qt}"))
                                mm = pe.transpose(b[:, (2 * i + qt) * P:(2 * i + qt + 1) * P],
                                                  prob_of(g)[:, qt, (2 * kp + i) * P:(2 * kp + i + 1) * P], M["ident"])
                        mm.then_inc(*did("pe", f"pt{g}.{kp}"))
                    b = take(pe, f"o{g}")
                    for kt_ in range(NT):
                        pe.wait_ge(*seen(pe, f"ev:pt{g}.{kt_ // 2}"))
                        if g == 0 and kt_ == 0:
                            pe.wait_ge(*seen(pe, "ev:uv3.1"))
                        mm = pe.matmul(b[:, 0:TC], val[:, kt_, g * P:(g + 1) * P], prob_T[:, kt_, :],
                                       start=kt_ == 0, stop=kt_ == NT - 1)
                    mm.then_inc(*did("pe", f"o{g}"))

        mix_lo = hm_t[:].rearrange("p (c t) -> p c t", t=T)[:, :, 0:TC]
        prob_T = mix_lo[:, 4:8, :]

        def prob_of(h):
            return prob

        def mla_act(act):
            for j in range(6):
                act.wait_ge(*seen(act, f"mi{j}"))
                dst = cq[:, j, :] if j < 3 else ckv[:, j - 3, :] if j < 5 else kpe[:, :]
                act.activation(dst, bank(f"mi{j}")[:, 0:(TC if j < 3 else T)], ACT.Copy).then_inc(*did("act", f"ev:mi{j}"))
            norm_act(act, "nq", lambda k: cq[:, k, :], TC, 3, (hm_t, 0), ["ev:mi0", "ev:mi1", "ev:mi2"])
            norm_act(act, "nkv", lambda k: ckv[:, k, :], T, 2, (hm_t, 1536), ["ev:mi3", "ev:mi4"])
            for j in range(12):
                act.wait_ge(*seen(act, f"uq{j}"))
                dst = qn[:, j, :] if j < 8 else qpe[:, j - 8, :]
                act.activation(dst, bank(f"uq{j}")[:, 0:TC], ACT.Copy).then_inc(*did("act", f"ev:uq{j}"))
            for t in range(NT):
                for g in range(2):
                    act.wait_ge(*seen(act, f"uv{t}.{g}"))
                    act.activation(val[:, t, 512 * g:512 * g + 512], bank(f"uv{t}.{g}")[:, :], ACT.Copy)\
                        .then_inc(*did("act", f"ev:uv{t}.{g}"))
            for h in range(MH):
                for qt in range(2):
                    i = 2 * h + qt
                    act.wait_ge(*seen(act, f"max{h}.{qt}"))
                    if h:
                        act.wait_ge(*seen(act, f"pt{h - 1}.1"))
                    act.activation(prob[:, qt, :], bank(f"s{h}.{qt}")[:, :], ACT.Exp, bias=pmax[:, i:i + 1],
                                   scale=MLA_SCALE, accum_out=psum_[:, i:i + 1]).then_inc(*did("act", f"ev:s{h}.{qt}"))

        def rope_dve(dve, x, job, key, tmp, at):
            dve.wait_ge(*seen(dve, job))
            dve.tensor_tensor(tmp, bank(job)[:, 0:TC], rope[:, 1, :], ALU.mult).then_inc(*did("dve", "ev:" + job))
            dve.tensor_tensor(x, x, rope[:, 0, :], ALU.mult).then_inc(*did("dve", key + ".c"))
            dve.wait_ge(*seen(dve, key + ".c"))
            dve.tensor_tensor(x, x, tmp, ALU.add).then_inc(*did("dve", key))

        def mla_dve(dve):
            dve.wait_ge(rope_in, 16)
            rope_dve(dve, kpe[:, TC:T], "kswap", "kpe", rope_tmp[:, 0:TC], 0)
            for tag, x, n, chunks, g, at in (("nq", cq, TC, 3, "q_norm", 0), ("nkv", ckv, T, 2, "kv_norm", 1536)):
                norm_dve(dve, tag, lambda k: x[:, k, :], lambda k: x[:, k, :], n, chunks, (hm_t, at))
                for k in range(chunks):
                    dve.wait_ge(*seen(dve, f"{tag}.xr{k}"))
                    dve.tensor_scalar(x[:, k, :], x[:, k, :], V(g, k), None, ALU.mult)\
                        .then_inc(*did("dve", f"{'cq' if tag == 'nq' else 'ckv'}{k}"))
            for j in range(4):
                if j:
                    dve.wait_ge(*seen(dve, f"qpe{j - 1}"))
                rope_dve(dve, qpe[:, j, :], f"qswap{j}", f"qpe{j}", rope_tmp[:, 0:TC], 0)
            for j in range(8):
                dve.wait_ge(*seen(dve, f"uk{j}"))
                dve.tensor_copy(kn[:, j, :], bank(f"uk{j}")[:, :]).then_inc(*did("dve", f"ev:uk{j}"))
            def head_end(h):
                for qt in range(2):
                    i = 2 * h + qt
                    dve.wait_ge(*seen(dve, f"ev:s{h}.{qt}"))
                    dve.reciprocal(psum_[:, i:i + 1], psum_[:, i:i + 1]).then_inc(*did("dve", f"ri{h}.{qt}"))
                    dve.wait_ge(*seen(dve, f"ri{h}.{qt}"))
                    dve.tensor_scalar(prob[:, qt, :], prob[:, qt, :], psum_[:, i:i + 1], None, ALU.mult)\
                        .then_inc(*did("dve", f"p{h}.{qt}"))
                for kp in range(2):
                    dve.wait_ge(*seen(dve, f"pt{h}.{kp}"))
                    if h:
                        dve.wait_ge(*seen(dve, f"o{h - 1}"))
                    dve.tensor_copy(prob_T[:, 2 * kp:2 * kp + 2, :],
                                    bank(f"pt{h}.{kp}")[:, :].rearrange("p (a b) -> p a b", b=TC))\
                        .then_inc(*did("dve", f"ev:pt{h}.{kp}"))
                dve.wait_ge(*seen(dve, f"o{h}"))
                dve.tensor_copy(mix[:, h, TC:T], bank(f"o{h}")[:, 0:TC]).then_inc(*did("dve", f"ev:o{h}"))

            for h in range(MH + 1):
                if h < MH:
                    for qt in range(2):
                        i = 2 * h + qt
                        dve.wait_ge(*seen(dve, f"s{h}.{qt}"))
                        dve.tensor_reduce(pmax[:, i:i + 1], bank(f"s{h}.{qt}")[:, :], AX, ALU.max, negate=True)\
                            .then_inc(*did("dve", f"mx{h}.{qt}"))
                        dve.wait_ge(*seen(dve, f"mx{h}.{qt}"))
                        dve.tensor_scalar(pmax[:, i:i + 1], pmax[:, i:i + 1], MLA_SCALE, None, ALU.mult)\
                            .then_inc(*did("dve", f"max{h}.{qt}"))
                if h:
                    head_end(h - 1)

        @block.tensor
        def _(pe):
            pe.wait_ge(consts_in, 16 * N_CONST)
            pe.wait_ge(*seen(pe, "silu_c"))
            ada_pe(pe, 0)
            norm_pe(pe, "n1", T, DC, NORM)
            win_pe(pe, range(3))
            ret_pe(pe)
            barrier(pe, "pe")
            win_pe(pe, range(3, 7))
            lora_pe(pe)
            gate_pe(pe)
            ada_pe(pe, 1)
            barrier(pe, "pe")
            pair_loop(pe, "pe", pair_pe)
            barrier(pe, "pe")
            post_pe(pe)
            wout_pe(pe, "wout", "wo", 0, "mix3")
            norm_pe(pe, "n20", T, DC, NORM)
            route_pe(pe, 0, 0)
            barrier(pe, "pe")
            expert_loop(pe, "pe", 0, lambda s, it: expert_pe(pe, 0, 0, s, it, turn["expert", 0][1] if s == 0 else turn["expert", s][1]))
            barrier(pe, "pe")
            norm_pe(pe, "n11", T, DC, (hm_t, 0))
            mla_pe(pe)
            wout_pe(pe, "mla_o", "mo", TC, f"ev:o{MH - 1}")
            norm_pe(pe, "n21", TC, DC, (hm_t, 0))
            route_pe(pe, 1, TC)
            barrier(pe, "pe")
            expert_loop(pe, "pe", 1, lambda s, it: expert_pe(pe, 1, TC, s, it, turn["expert", NE + s][1]))
            barrier(pe, "pe")
            norm_pe(pe, "nf", TC, DC, (hm_t, 0))

        @block.scalar
        def _(act):
            act.wait_ge(consts_in, 16 * N_CONST)
            for i, name in enumerate(("c_ctx", "c")):
                act.activation(silu_c[:, :, i], V(name), ACT.Silu).then_inc(*did("act", *(["silu_c"] if i else [])))
            act.wait_ge(h_in, 16)
            act.wait_ge(*seen(act, "eps"))
            norm_act(act, "n1", lambda k: hm[:, k, :], T, DC, NORM)
            act.wait_ge(*seen(act, "gain0.1"))
            modulate_act(act, "n1", 0, 0, SEGS)
            ret_feat_act(act)
            ret_act(act)
            barrier(act, "act")
            lora_act(act)
            gate_act(act)
            barrier(act, "act")
            pair_loop(act, "act", pair_act)
            barrier(act, "act")
            post_act(act)
            norm_act(act, "n20", lambda k: hT[:, k, :], T, DC, NORM, [f"wo.h{k}" for k in range(DC)])
            modulate_act(act, "n20", 0, 1, SEGS)
            route_act(act, 0, 0)
            barrier(act, "act")
            expert_loop(act, "act", 0, lambda s, it: expert_act(act, 0, 0, s, it))
            barrier(act, "act")
            norm_act(act, "n11", lambda k: hT[:, k, :], T, DC, (hm_t, 0), [f"h0.{k}" for k in range(DC)])
            modulate_act(act, "n11", 1, 0, SEGS)
            mla_act(act)
            norm_act(act, "n21", lambda k: hT[:, k, TC:T], TC, DC, (hm_t, 0), [f"mo.h{k}" for k in range(DC)])
            modulate_act(act, "n21", 1, 1, SEGS[1:])
            route_act(act, 1, TC)
            barrier(act, "act")
            expert_loop(act, "act", 1, lambda s, it: expert_act(act, 1, TC, s, it))
            barrier(act, "act")
            norm_act(act, "nf", lambda k: hT[:, k, TC:T], TC, DC, (hm_t, 0), [f"h1.{k}" for k in range(DC)])

        @block.vector
        def _(dve):
            dve.memset(small[:, 0:1], EPS).then_inc(*did("dve"))
            dve.memset(small[:, 1:2], GN_EPS).then_inc(*did("dve", "eps"))
            dve.wait_ge(consts_in, 16 * N_CONST)
            dve.tensor_tensor(small[:, 8:24], V("mu0"), V("mu1"), ALU.add).then_inc(*did("dve", "mu"))
            dve.wait_ge(*seen(dve, "mu"))
            dve.tensor_scalar(small[:, 8:24], small[:, 8:24], -1.0, 1.0, ALU.mult, ALU.add).then_inc(*did("dve", "one_mu"))
            dve.wait_ge(*seen(dve, "one_mu"))
            ada_dve(dve, 0)
            dve.wait_ge(h_in, 16)
            norm_dve(dve, "n1", lambda k: hm[:, k, :], lambda k: xT[:, k, :], T, DC, NORM)
            ret_dve(dve)
            barrier(dve, "dve")
            shift_dve(dve)
            lora_dve(dve)
            ada_dve(dve, 1)
            barrier(dve, "dve")
            pair_loop(dve, "dve", pair_dve)
            barrier(dve, "dve")
            post_dve(dve)
            dve.wait_ge(h_again, 16)
            residual_dve(dve, "wo", 0, 2, 0, hT)
            norm_dve(dve, "n20", lambda k: hT[:, k, :], lambda k: xT[:, k, :], T, DC, NORM)
            dve.wait_ge(router_in, 48)
            route_dve(dve, 0, 0)
            barrier(dve, "dve")
            expert_loop(dve, "dve", 0, lambda s, it: expert_dve(dve, 0, 0, s, it, 1))
            barrier(dve, "dve")
            add_mixture_dve(dve, 0, 0)
            norm_dve(dve, "n11", lambda k: hT[:, k, :], lambda k: xT[:, k, :], T, DC, (hm_t, 0))
            mla_dve(dve)
            residual_dve(dve, "mo", 1, 2, TC, hT)
            norm_dve(dve, "n21", lambda k: hT[:, k, TC:T], lambda k: xT[:, k, TC:T], TC, DC, (hm_t, 0))
            dve.wait_ge(router_in, 96)
            route_dve(dve, 1, TC)
            barrier(dve, "dve")
            expert_loop(dve, "dve", 1, lambda s, it: expert_dve(dve, 1, TC, s, it, 1 + NE // 4))
            barrier(dve, "dve")
            add_mixture_dve(dve, 1, TC)
            norm_dve(dve, "nf", lambda k: hT[:, k, TC:T], lambda k: xT[:, k, 0:TC], TC, DC, (hm_t, 0))
            for k in range(DC):
                dve.wait_ge(*seen(dve, f"nf.xr{k}"))
                dve.tensor_scalar(xT[:, k, 0:TC], xT[:, k, 0:TC], V("final_g", k), None, ALU.mult)\
                    .then_inc(*did("dve", f"out{k}"))

        @block.gpsimd
        def _(pool):
            pool.wait_ge(consts_in, 16 * N_CONST)
            pool.tensor_copy(level_t[:], part(ring, WORK + 9216, 2 * len(LEVELS) * P)).then_inc(*did("pool", "levels"))
            barrier(pool, "pool")
            barrier(pool, "pool")
            pair_loop(pool, "pool", pair_pool)
            barrier(pool, "pool")
            for l, a in ((0, 0), (1, TC)):
                pool.wait_ge(*seen(pool, f"o{MH - 1}" if l else "mix3"))
                for c in range(DC):
                    pool.memset(yT[:, c, :], 0.0).then_inc(*did("pool"))
                barrier(pool, "pool")
                barrier(pool, "pool")

        @block.sync
        def _(sp):
            sp.dma_start(vec[:], dram["vec"]).then_inc(consts_in, 16)
            sp.dma_start(mask_t[:], dram["masks"]).then_inc(consts_in, 16)
            sp.dma_start(part(ring, WORK + 9216, 2 * len(LEVELS) * P), dram["levels"]).then_inc(consts_in, 16)
            sp.dma_start(part(ring, WORK + 6144, RH * 768), dram["decay"]).then_inc(consts_in, 16)
            sp.dma_start(hm_t[:], dram["hT"]).then_inc(h_in, 16)

            def load(key):
                a, i = key
                before = previous[key]
                if before is not None:
                    sp.wait_ge(*seen(sp, f"used:{before[0]}{before[1]}"))
                s, n = turn[key]
                w = next(w for x, j, w, _ in items if (x, j) == key)
                sp.dma_start(ring[:, s * SLOT:s * SLOT + w], dram[a][i]).then_inc(loaded[s], 16)

            for l in range(2):
                layer = [(a, i) for a, i, _, _ in items]
                split = layer.index(("expert", NE * l))
                start = 0 if l == 0 else layer.index(("expert", NE - 1)) + 1
                for key in layer[start:split]:
                    if key == ("wout", 1):
                        sp.wait_ge(*seen(sp, "mix3"))
                        sp.dma_start(part(feat_t, 0, DC * T), dram["hT"]).then_inc(h_again, 16)
                        sp.dma_start(route_w, dram["route_w"][0]).then_inc(router_in, 16)
                        sp.dma_start(route_b[0:1, :], dram["route_b"][0:1]).then_inc(router_in, 16)
                        sp.dma_start(rank, dram["rank"]).then_inc(router_in, 16)
                    if key == ("mla_in", 0):
                        sp.wait_ge(phase, 4 * 5)
                        sp.dma_start(rope, dram["rope"]).then_inc(rope_in, 16)
                    load(key)
                if l:
                    sp.wait_ge(*seen(sp, "ev:o7"))
                    sp.wait_ge(*seen(sp, "mo.7"))
                    sp.dma_start(route_w, dram["route_w"][1]).then_inc(router_in, 16)
                    sp.dma_start(route_b[0:1, :], dram["route_b"][1:2]).then_inc(router_in, 16)
                    sp.dma_start(rank, dram["rank"]).then_inc(router_in, 16)
                n = T - (TC if l else 0)
                for s in range(4):
                    if l == 0 and s == 2:
                        sp.wait_ge(*seen(sp, "n20.x7"))
                    load(("expert", NE * l + s))
                sp.wait_ge(*seen(sp, f"ev:m{l}.gT"))
                sp.dma_start(dram["gates"][:, 0:n], gates_T[0:NE, 0:n]).then_inc(gates_out, 16)
                sp.wait_ge(gates_out, 16 * (l + 1))
                for s in range(4):
                    sp.dma_start(gate_row[:, s, 0:n], dram["gates"][s:s + 1, 0:n].partition_broadcast(P))\
                        .then_inc(gate_rows[s], 16)
                with sp.Fori(0, NE // 4 - 1) as it:
                    for s in range(4):
                        sp.wait_ge(*seen(sp, f"e{l}.{s}.y7", it))
                        sp.dma_start(slot(s, SLOT), dram["expert"][bass.ds(it * 4 + (NE * l + 4 + s), 1)]
                                     .rearrange("o p n -> (o p) n")).then_inc(loaded[s], 16)
                        sp.wait_ge(*seen(sp, f"e{l}.{s}.hid1", it))
                        sp.dma_start(gate_row[:, s, 0:n], dram["gates"][bass.ds(it * 4 + (4 + s), 1), 0:n]
                                     .partition_broadcast(P)).then_inc(gate_rows[s], 16)
            for k in range(DC):
                sp.wait_ge(*seen(sp, f"out{k}"))
                sp.dma_start(out[:, k, :], xT[:, k, 0:TC]).then_inc(stored, 16)
            sp.wait_ge(stored, 16 * DC)

        for l in range(2):
            for s in range(4):
                L.new[f"used:expert{NE * l + NE - 4 + s}"] = L.new[f"e{l}.{s}.y7"]
    return L.new


N_CONST = 4


def tables():
    import numpy as np

    i = np.arange(P)
    p, c = i[:, None], i[None, :]
    swap = ((p // 32 == c // 32) & ((p - c) % 32 == 16)).astype(np.float32)
    masks = dict(ident=p == c, ones=np.ones((P, P)), half_ones=p // 64 == c // 64, swap=swap, lt=p < c, le=p <= c,
                 gt=p > c, ge=p >= c, eye2=p % 64 == c % 64)
    masks = np.concatenate([np.asarray(masks[n], np.float32) for n in MASKS], 1)
    low = [((p // (2 * n) == c // (2 * n)) & (p // n % 2 == 1) & (c // n % 2 == 0)) for n in LEVELS]
    levels = np.concatenate([np.concatenate(low, 1), np.concatenate([m.T for m in low], 1)], 1).astype(np.float32)
    decay = np.zeros((P, RH, 768), np.float64)
    u, w = np.arange(-128, 256), np.arange(128, 512)
    for h in range(RH):
        lg = math.log1p(-2.0 ** (-5 - h))
        decay[:, h, :384] = np.exp(lg * np.abs(u[None] - p))
        decay[:, h, 384:] = np.exp(lg * (w[None] - p)) + np.exp(lg * (512 - w[None] + p))
    t = np.arange(TC)
    freq = (10000.0 ** (-np.arange(16, dtype=np.float32) / 16)).astype(np.float32)
    row, col = (t // 64).astype(np.float32)[None] * freq[:, None], (t % 64).astype(np.float32)[None] * freq[:, None]
    cos = np.concatenate([np.cos(row)] * 2 + [np.cos(col)] * 2, 0)
    sin = np.concatenate([-np.sin(row), np.sin(row), -np.sin(col), np.sin(col)], 0)
    rope = np.stack([np.tile(cos, (2, 1)), np.tile(sin, (2, 1))], 1).astype(np.float32)
    rank = np.tile(np.arange(EPG, 0, -1, dtype=np.float32)[None], (P, 1))
    return dict(masks=masks, levels=levels, decay=decay.astype(np.float32).reshape(P, -1), rope=rope, rank=rank)


def laid_out(x, c, ctx, c_ctx, ada_w, ada_b, norm1_g, norm2_g, final_g, ev_w_in, ev_shift_mu, rwkv_w0, rwkv_w2,
             rwkv_a0, rwkv_a2, rwkv_g2, rwkv_k_k, rwkv_k_a, rwkv_r_k, rwkv_lnx_w, rwkv_lnx_b, ev_w_out, mla_w_in,
             mla_q_norm_g, mla_w_uq, mla_kv_norm_g, mla_w_ukv, mla_w_o, moe_w_grp, moe_b_grp, moe_w_exp, moe_b_exp,
             moe_w_gate, moe_w_up, moe_w_down):
    import numpy as np

    def cols(v, n):
        v = np.reshape(v, -1)
        return np.concatenate([v, np.zeros(n * P - v.size, v.dtype)]).reshape(n, P).T

    def slabs(w, width):
        k, n = w.shape
        return w.reshape(k // P, P, n // width, width).transpose(2, 1, 0, 3).reshape(n // width, P, -1)

    vals = dict(c=c, c_ctx=c_ctx, norm1_g0=norm1_g[0], norm1_g1=norm1_g[1], norm2_g0=norm2_g[0], norm2_g1=norm2_g[1],
                final_g=final_g, ada_b0=ada_b[0], ada_b1=ada_b[1], mu0=ev_shift_mu[0, 0], mu1=ev_shift_mu[0, 1],
                w0_0=rwkv_w0[0, 0], w0_1=rwkv_w0[0, 1], a0_0=rwkv_a0[0, 0], a0_1=rwkv_a0[0, 1], k_k=rwkv_k_k,
                k_a=rwkv_k_a, r_k=rwkv_r_k, lnx_w=rwkv_lnx_w, lnx_b=rwkv_lnx_b, q_norm=mla_q_norm_g,
                kv_norm=mla_kv_norm_g)
    vec = np.concatenate([cols(vals[n], w) for n, (_, w) in VEC.items()], 1)
    hT = np.concatenate([ctx[0], x[0]], 0).T.reshape(DC, P, T).transpose(1, 0, 2).reshape(P, -1)
    g2 = np.concatenate([rwkv_g2[0], np.zeros((96, 512), rwkv_g2.dtype)], 0)
    lora = np.concatenate([rwkv_w2[0].reshape(P, 512), rwkv_a2[0].reshape(P, 512), g2[:P], g2[P:]], 1)[None]
    uq = mla_w_uq[0].reshape(-1, MH, 192)
    uq = np.concatenate([uq[:, :, :128].reshape(-1, 1024), uq[:, :, 128:].reshape(-1, 512)], 1)
    ukv = mla_w_ukv[0].reshape(-1, MH, 256)
    ukv = np.concatenate([ukv[:, :, :128].reshape(-1, 1024), ukv[:, :, 128:].reshape(-1, 1024)], 1)
    win = ev_w_in[0]
    mla_in = np.concatenate([mla_w_in[0], mla_w_in[0][:, 640:]], 1)
    e = 2 * NE

    def rows(w):
        w = w.reshape(e, w.shape[2] // P, P, w.shape[3])
        return w.transpose(0, 2, 1, 3).reshape(e, P, -1)

    expert = np.concatenate([rows(moe_w_gate), rows(moe_w_up), rows(moe_w_down)], 2)
    route_w = np.concatenate([moe_w_grp, moe_w_exp], 2).reshape(2, DC, P, NR).transpose(0, 2, 1, 3)
    return dict(vec=vec, hT=hT, ada=np.concatenate([slabs(ada_w[0], 512), slabs(ada_w[1], 512)], 0),
                win=slabs(win[:, :3072], 512), win6=slabs(win[:, 3072:], 416), lora=lora, wout=slabs(ev_w_out[0], 512),
                expert=expert, mla_in=slabs(mla_in, 768), mla_uq=slabs(uq, 1536), mla_ukv=slabs(ukv, 2048),
                mla_o=slabs(mla_w_o[0], 512), route_w=route_w,
                route_b=np.concatenate([moe_b_grp, moe_b_exp], 1), **tables())


def kernel(**inputs):
    import numpy as np
    import concourse.bacc as bacc
    from concourse.bass_utils import run_bass_kernel_spmd as run

    arrays = {n: np.ascontiguousarray(a) for n, a in laid_out(**{k: np.asarray(v) for k, v in inputs.items()}).items()}
    marks = {}
    for _ in range(2):
        nc = bacc.Bacc("TRN2", target_bir_lowering=False, num_devices=1)
        dram = {n: nc.dram_tensor("in_" + n, a.shape, mybir.dt.from_np(a.dtype), kind="ExternalInput").ap()
                for n, a in arrays.items()}
        dram["gates"] = nc.dram_tensor("gates", (NE, T), F32, kind="Internal").ap()
        out = nc.dram_tensor("out", (P, DC, TC), F32, kind="ExternalOutput").ap()
        marks = build(nc, dram, out, None, marks)
    r = run(nc, [{"in_" + n: a for n, a in arrays.items()}], core_ids=[0])
    o = r.results[0]["out"]
    return np.ascontiguousarray(o.transpose(2, 1, 0).reshape(1, TC, D))
```

```python
from contextlib import ExitStack
import math

import concourse.bass as bass
from concourse import mybir

F32 = mybir.dt.float32
U8 = mybir.dt.uint8
ALU = mybir.AluOpType
ACT = mybir.ActivationFunctionType
AX = mybir.AxisListType.X

P = 128
D = 1024
DC = D // P
TC = 256
T = 2 * TC
NT = T // P
EPS = 1e-6
RH = 4
NPAIR = 4
GN_EPS = 64e-5
MH = 8
NE, NG, EPG = 32, 4, 8
NR = NG + NE
CAP = 64
MLA_SCALE = (128 + 64) ** -0.5
LOG_DECAY = -math.exp(-0.5)

VEC, NV = {}, 0
for _name, _w in (("c", 8), ("c_ctx", 8), ("norm1_g0", 8), ("norm1_g1", 8), ("norm2_g0", 8), ("norm2_g1", 8),
                  ("final_g", 8), ("ada_b", 96), ("mu0", 16), ("mu1", 16), ("w0_0", 4),
                  ("w0_1", 4), ("a0_0", 4), ("a0_1", 4), ("k_k", 4), ("k_a", 4), ("r_k", 4), ("lnx_w", 4),
                  ("lnx_b", 4), ("q_norm", 3), ("kv_norm", 2)):
    VEC[_name] = (NV, _w)
    NV += _w
ADA_FIRST = 4
ADA_TURN = 5
MASKS = ("ident", "ones", "half_ones", "swap", "lt", "le", "gt", "ge", "eye2")
SLOT = 6144
LEVELS = (1, 2, 4, 8, 16, 32, 64)
ORDER = ((0, 1, 2, 3), (1, 0, 3, 2))


def stream_items():
    first = [("ada", n, 4096) for n in range(ADA_FIRST)] + [("win", n, 4096) for n in range(6)]
    first += [("win6", 0, 8 * 416), ("lora", 0, 2048)]
    items = [(a, i, w, n % 2) for n, (a, i, w) in enumerate(first)]
    items += [("ada", ADA_FIRST + ADA_TURN * t + i, 4096, i % 2) for t in range(NPAIR) for i in range(ADA_TURN)]
    items += [("wout", n, 4096, n % 2) for n in range(2)]
    items += [("expert", e, SLOT, e % 4) for e in range(NE)] + [("extra", x, SLOT, x % 2) for x in range(16)]
    mla = [("mla_in", 0, SLOT), ("mla_uq", 0, 4608), ("mla_ukv", 0, 4096), ("mla_o", 0, 4096), ("mla_o", 1, 4096)]
    items += [(a, i, w, n % 4) for n, (a, i, w) in enumerate(mla)]
    items += [("expert", NE + e, SLOT, e % 4) for e in range(NE)]
    items += [("extra", 16 + x, SLOT, x % 2) for x in range(8)]
    return items


def named(prefix, key):
    return f"ev:{prefix}{key[3:]}" if key.startswith("ev:") else prefix + key


class Layout:

    def __init__(self, sems, spare, marks):
        self.spare = spare
        self.sems, self.marks, self.new = sems, marks, {}
        self.count = {e: 0 for e in sems}
        self.loop = {e: None for e in sems}
        self.rotation, self.user = 0, {}
        self.waited, self.pending = {}, {}

    def did(self, engine, *keys):
        self.count[engine] += 1
        for key in keys:
            assert key not in self.new, key
            self.new[key] = (engine, self.loop[engine], self.count[engine])
        return self.sems[engine], 1

    def seen(self, eng, key, it=None, back=0):
        if not self.marks:
            return self.sems["pe"], 1
        engine, loop, n = self.marks[key]
        waiter, kind = str(eng.engine), None
        if loop is not None:
            base, per, times = self.marks["loop", engine, loop]
            if it is None:
                n += base + (times - 1) * per
            else:
                n, kind = n + base - back * per, loop
                assert n > 0, ("a wait below one", key, n, per)
        high = self.waited.get((waiter, engine, kind), 0)
        if kind is None:
            return self.sems[engine], n
        if high < n and self.pending.get(waiter) == engine:
            eng.sem_inc(self.spare, 1)
        self.pending[waiter] = engine
        self.waited[waiter, engine, kind] = n = max(n, high)
        return self.sems[engine], it * per + n

    def enter(self, engine, loop):
        self.loop[engine], base, self.count[engine] = loop, self.count[engine], 0
        self.waited = {}
        return base

    def leave(self, engine, base, times):
        loop, per = self.loop[engine], self.count[engine]
        self.new["loop", engine, loop] = (base, per, times)
        self.loop[engine], self.count[engine] = None, base + times * per
        self.waited = {}

    def bank(self, job):
        b, loop = self.rotation, self.loop["pe"]
        self.rotation = (b + 1) % 8
        before, back = self.user.get(b), 0
        if before is None and loop is not None:
            before, back = self.marks.get(("last", loop, b)), 1
        self.user[b] = job
        self.new["bank", job] = b
        if loop is not None:
            self.new["last", loop, b] = job
        return b, before, back

    def empty(self):
        self.rotation, self.user = 0, {}


def build(nc, dram, out, dbg, marks):
    items = stream_items()
    ctx = ExitStack()
    with ctx:
        def sb(name, shape, dt=F32):
            return ctx.enter_context(nc.sbuf_tensor(name, shape, dt))

        def sem(name):
            return ctx.enter_context(nc.semaphore(name))

        ring = sb("ring", [P, 4 * SLOT])
        xT_t = sb("xT", [P, DC * T])
        hm_t = sb("h_or_mix", [P, DC * T])
        feat_t = sb("features", [P, 8 * NPAIR * T])
        vec = sb("vec", [P, NV])
        mask_t = sb("masks", [P, len(MASKS) * P])
        level_t = sb("level_masks", [P, 2 * len(LEVELS) * P], U8)
        silu_c = sb("silu_c", [P, DC, 32])
        mods = sb("mods", [P, 2, 48, 2])
        gains = sb("gains", [P, 4, DC, 2])
        small = sb("small", [P, 26])
        row_int_t = sb("row_int", [P, 2, NT], mybir.dt.uint32)
        extra_of_t = sb("extra_of", [P, 17], mybir.dt.int32)
        gate_in = sb("gate_in", [P, 2, T])

        psum = [ctx.enter_context(nc.psum_tensor(f"bank{b}", [P, 512], F32)) for b in range(8)]

        sems = {e: sem(f"{e}_done") for e in ("pe", "act", "dve", "pool")}
        loaded = [sem(f"slot{s}_loaded") for s in range(4)]
        consts_in, tables_in, h_in, h_again = sem("consts_in"), sem("tables_in"), sem("h_in"), sem("h_again")
        router_in, rope_in = sem("router_in"), sem("rope_in")
        y_out = [sem(f"results_from_yt{i}") for i in range(4)]
        filled = sem("extra_blocks_filled")
        got_in = [sem(f"results_of_tile{t}") for t in range(NT)]
        stored, phase = sem("stored"), sem("phase")
        waited = sem("waited")
        L = Layout(sems, waited, marks)
        did, seen = L.did, L.seen
        block = ctx.enter_context(nc.Block())

        def V(name, j=None):
            a, w = VEC[name]
            return vec[:, a:a + w] if j is None else vec[:, a + j:a + j + 1]

        M = {n: mask_t[:, i * P:(i + 1) * P] for i, n in enumerate(MASKS)}
        level = level_t[:].rearrange("p (d n c) -> p d n c", d=2, c=P)
        xT = xT_t[:].rearrange("p (c t) -> p c t", t=T)
        hm = hm_t[:].rearrange("p (c t) -> p c t", t=T)
        mix = hm

        def part(t, off, *shape):
            n = math.prod(shape)
            v = t[:, off:off + n]
            if len(shape) == 2:
                v = v.rearrange("p (a b) -> p a b", b=shape[1])
            if len(shape) == 3:
                v = v.rearrange("p (a b c) -> p a b c", b=shape[1], c=shape[2])
            return v

        def slot(s, *shape):
            return part(ring, s * SLOT, *shape)

        r_t, kr_t, kk_t, v_t, a_t0, a_t1, lw_t0, lw_t1 = (part(feat_t, i * 2048, NPAIR, T) for i in range(8))
        a_t, lw_t = (a_t0, a_t1), (lw_t0, lw_t1)
        hT = part(feat_t, 0, DC, T)
        yT = part(feat_t, 4096, DC, T)
        WORK = 2 * SLOT

        turn, previous, last_in = {}, {}, {}
        uses = [0] * 4
        for a, i, w, s in items:
            uses[s] += 1
            turn[a, i] = (s, uses[s])
            previous[a, i] = last_in.get(s)
            last_in[s] = (a, i)

        def arrived(key):
            s, n = turn[key]
            return loaded[s], 16 * n

        def take(pe, job, it=None):
            b, before, back = L.bank(job)
            if before is not None:
                pe.wait_ge(*seen(pe, "ev:" + before, it, back))
            return psum[b]

        def bank(job):
            return psum[marks.get(("bank", job), 0)]

        barriers = {"pe": 0, "act": 0, "dve": 0, "pool": 0}

        def barrier(eng, name, label=None):
            barriers[name] += 1
            if label:
                L.new["barrier", label] = barriers[name]
            eng.drain().then_inc(phase, 1)
            eng.wait_ge(phase, 4 * barriers[name])
            if name == "pe":
                L.empty()

        SEGS = ((0, TC), (TC, T))

        def norm_bufs(at):
            return part(at[0], at[1], 2, T), part(at[0], at[1] + 2 * T, T)

        def norm_pe(pe, tag, n, chunks, at):
            sq, _ = norm_bufs(at)
            b = take(pe, tag)
            for k in range(chunks):
                pe.wait_ge(*seen(pe, f"{tag}.sq{k}"))
                pe.matmul(b[:, 0:n], M["ones"], sq[:, k % 2, 0:n], start=k == 0, stop=k == chunks - 1)\
                    .then_inc(*did("pe", f"{tag}.sum{k}"))

        def norm_act(act, tag, src, n, chunks, at, ready=()):
            sq, rt = norm_bufs(at)
            for k in range(chunks):
                for key in ready[k:k + 1]:
                    act.wait_ge(*seen(act, key))
                if k >= 2:
                    act.wait_ge(*seen(act, f"{tag}.sum{k - 2}"))
                act.activation(sq[:, k % 2, 0:n], src(k), ACT.Square).then_inc(*did("act", f"{tag}.sq{k}"))
            act.wait_ge(*seen(act, f"{tag}.sum{chunks - 1}"))
            act.activation(rt[:, 0:n], bank(tag)[:, 0:n], ACT.Sqrt, bias=small[:, 0:1], scale=1.0 / (chunks * P))\
                .then_inc(*did("act", "ev:" + tag))

        def norm_dve(dve, tag, src, dst, n, chunks, at):
            _, rt = norm_bufs(at)
            dve.wait_ge(*seen(dve, "ev:" + tag))
            dve.reciprocal(rt[:, 0:n], rt[:, 0:n]).then_inc(*did("dve", tag + ".inv"))
            dve.wait_ge(*seen(dve, tag + ".inv"))
            for k in range(chunks):
                dve.tensor_tensor(dst(k), src(k), rt[:, 0:n], ALU.mult).then_inc(*did("dve", f"{tag}.xr{k}"))

        def modulate_act(act, tag, layer, which, segs):
            for k in range(DC):
                act.wait_ge(*seen(act, f"{tag}.xr{k}"))
                for i, (a, b) in enumerate(segs):
                    seg = a // TC
                    act.activation(xT[:, k, a:b], xT[:, k, a:b], ACT.Identity,
                                   scale=gains[:, 2 * layer + which, k, seg:seg + 1],
                                   bias=mods[:, layer, 24 * which + k, seg:seg + 1])\
                        .then_inc(*did("act", *([f"{tag}.x{k}"] if i == len(segs) - 1 else [])))

        NORM = (ring, WORK)
        NORM2 = (feat_t, 11660)

        mods_flat = mods[:].rearrange("p l m c -> p (l m) c")
        ada_y = part(ring, 4096, 512)

        def ada_sum_pe(pe, key, s, count, it=None):
            b = take(pe, key, it)
            w = slot(s, DC, 512)
            pe.wait_ge(loaded[s], count)
            for q in range(2):
                for j in range(4):
                    mm = pe.matmul(b[32 * j:32 * j + 32, :], silu_c[:, 4 * q + j, :], w[:, 4 * q + j, :],
                                   start=q == 0, stop=q == 1)
            mm.then_inc(*did("pe", key))

        def ada_turn_pe(pe, key, it=None):
            b = take(pe, key + "t", it)
            pe.wait_ge(*seen(pe, "ev:" + key, it))
            for m in range(4):
                mm = pe.matmul(b[:, 2 * m:2 * m + 2], ada_y[:, m * P:(m + 1) * P], small[:, 24:26], start=True, stop=True)
            mm.then_inc(*did("pe", key + "t"))

        def ada_act(act, key, it=None):
            act.wait_ge(*seen(act, key, it))
            act.activation(ada_y, bank(key)[:, :], ACT.Copy).then_inc(*did("act", "ev:" + key))

        def ada_dve(dve, key, at, it=None):
            dve.wait_ge(*seen(dve, key + "t", it))
            cols = slice(at, at + 4) if it is None else bass.ds(it * (4 * ADA_TURN) + at, 4)
            bias = V("ada_b")[:, cols].unsqueeze(2).broadcast_to([P, 4, 2])
            dve.tensor_tensor(mods_flat[:, cols, :], bank(key + "t")[:, 0:8].rearrange("p (a b) -> p a b", b=2), bias,
                              ALU.add).then_inc(*did("dve", f"ev:{key}t"))

        def gain_dve(dve, layer, which, ready):
            dve.wait_ge(*seen(dve, ready))
            g = V(f"norm{which + 1}_g{layer}").unsqueeze(2).broadcast_to([P, DC, 2])
            dve.scalar_tensor_tensor(gains[:, 2 * layer + which], mods[:, layer, 24 * which + 8:24 * which + 16, :],
                                     1.0, g, ALU.add, ALU.mult).then_inc(*did("dve", f"gain{layer}.{which}"))

        def ada_loop_pe(pe, i, it):
            s, n = turn["ada", ADA_FIRST + i]
            ada_sum_pe(pe, f"A{i}", s, it * (16 * len(range(s, ADA_TURN, 2))) + 16 * n, it)

        def ada_loop_dve(dve, i, it):
            ada_dve(dve, f"A{i}", 4 * (ADA_FIRST + i), it)

        q_t = part(ring, WORK, 2, T)
        k_t = part(ring, WORK + 1024, 2, T)
        vtok = part(ring, WORK + 2048, NT, 512)
        g_t = part(ring, WORK + 4096, RH, T)
        decay = part(ring, WORK + 6144, RH, 768)
        scores = part(ring, WORK + 9216, NT, T)
        rtmp = part(ring, WORK + 11264, 2, T)

        def proj_pe(pe, job, w, k_n, m0, rhs, n, m=P, ready=None):
            b = take(pe, job)
            for k in range(k_n):
                if ready is not None:
                    pe.wait_ge(*seen(pe, ready(k)))
                mm = pe.matmul(b[0:m, 0:n], w[:, k, m0:m0 + m], rhs(k), start=k == 0, stop=k == k_n - 1)
            return mm

        def win_pe(pe, groups):
            for g in groups:
                key = ("win", g) if g < 6 else ("win6", 0)
                pe.wait_ge(*arrived(key))
                w = slot(turn[key][0], DC, 512 if g < 6 else 416)
                for j in range(4):
                    last = [f"used:{key[0]}{key[1]}"] if j == 3 else []
                    m = P if g < 6 or j < 3 else 32
                    if g == 1:
                        b = take(pe, f"win1.{j}")
                        for k in range(DC):
                            mm = pe.matmul(b[:, :], xT[:, k, j * P:(j + 1) * P], w[:, k, :],
                                           start=k == 0, stop=k == DC - 1)
                    else:
                        mm = proj_pe(pe, f"win{g}.{j}", w, DC, j * P, lambda k: xT[:, k, :], T, m,
                                     (lambda k: f"n1.x{k}") if g == 0 and j == 0 else None)
                    mm.then_inc(*did("pe", f"win{g}.{j}", *last))

        def ret_feat_act(act):
            act.wait_ge(*seen(act, "n1.sum7"))
            for j in range(4):
                act.wait_ge(*seen(act, f"win0.{j}"))
                dst, c = ((q_t, 64 ** -0.5) if j < 2 else (k_t, 1.0))
                act.activation(dst[:, j % 2, :], bank(f"win0.{j}")[:, :], ACT.Copy, scale=c)\
                    .then_inc(*did("act", f"ev:win0.{j}"))
            for j in range(4):
                act.wait_ge(*seen(act, f"win1.{j}"))
                act.activation(vtok[:, j, :], bank(f"win1.{j}")[:, :], ACT.Copy).then_inc(*did("act", f"ev:win1.{j}"))
            for j in range(4):
                act.wait_ge(*seen(act, f"win2.{j}"))
                act.activation(g_t[:, j, :], bank(f"win2.{j}")[:, :], ACT.Silu).then_inc(*did("act", f"ev:win2.{j}"))

        def ret_pe(pe):
            for h in range(RH):
                half = slice(64 * (h % 2), 64 * (h % 2) + 64)
                for J in range(NT):
                    i0 = 0 if J < 2 else TC
                    b = take(pe, f"sc{h}.{J}")
                    if h == 0 and J == 0:
                        pe.wait_ge(*seen(pe, "ev:win0.3"))
                    pe.matmul(b[:, i0:T], k_t[half, h // 2, J * P:(J + 1) * P], q_t[half, h // 2, i0:T],
                              start=True, stop=True).then_inc(*did("pe", f"sc{h}.{J}"))
                b = take(pe, f"ro{h}")
                for J in range(NT):
                    i0 = 0 if J < 2 else TC
                    pe.wait_ge(*seen(pe, f"ev:sc{h}.{J}"))
                    if h == 0 and J == 0:
                        pe.wait_ge(*seen(pe, "ev:win1.3"))
                    mm = pe.matmul(b[:, i0:T], vtok[:, J, h * P:(h + 1) * P], scores[:, J, i0:T],
                                   start=J == 0, stop=J == NT - 1)
                mm.then_inc(*did("pe", f"ro{h}"))
                b = take(pe, f"rs{h}")
                pe.wait_ge(*seen(pe, f"rsq{h}"))
                pe.matmul(b[:, :], M["ones"], rtmp[:, 0, :], start=True, stop=True).then_inc(*did("pe", f"rs{h}"))

        def ret_act(act):
            for h in range(RH):
                act.wait_ge(*seen(act, f"ro{h}"))
                if h:
                    act.wait_ge(*seen(act, f"rs{h - 1}"))
                act.activation(rtmp[:, 0, :], bank(f"ro{h}")[:, :], ACT.Square).then_inc(*did("act", f"rsq{h}"))
                act.activation(mix[:, h, :], bank(f"ro{h}")[:, :], ACT.Copy).then_inc(*did("act", f"ev:ro{h}"))
                act.wait_ge(*seen(act, f"rs{h}"))
                if h:
                    act.wait_ge(*seen(act, f"rmul{h - 1}"))
                act.activation(rtmp[:, 1, :], bank(f"rs{h}")[:, :], ACT.Sqrt, bias=small[:, 0:1], scale=1.0 / P)\
                    .then_inc(*did("act", f"ev:rs{h}"))

        def ret_dve(dve):
            dve.wait_ge(*seen(dve, "levels"))
            for h in range(RH):
                for J in range(NT):
                    dve.wait_ge(*seen(dve, f"sc{h}.{J}"))
                    if h:
                        dve.wait_ge(*seen(dve, f"ro{h - 1}"))
                    u = 128 - P * (J % 2)
                    b = bank(f"sc{h}.{J}")
                    if J < 2:
                        dve.tensor_tensor(scores[:, J, 0:TC], b[:, 0:TC], decay[:, h, u:u + TC], ALU.mult)\
                            .then_inc(*did("dve"))
                        table = decay[:, h, 384 + u:384 + u + TC]
                    else:
                        table = decay[:, h, u:u + TC]
                    dve.tensor_tensor(scores[:, J, TC:T], b[:, TC:T], table, ALU.mult)\
                        .then_inc(*did("dve", f"ev:sc{h}.{J}"))
                dve.wait_ge(*seen(dve, f"ev:rs{h}"))
                dve.reciprocal(rtmp[:, 1, :], rtmp[:, 1, :]).then_inc(*did("dve", f"rinv{h}"))
                dve.wait_ge(*seen(dve, f"rinv{h}"))
                dve.tensor_tensor(g_t[:, h, :], g_t[:, h, :], rtmp[:, 1, :], ALU.mult).then_inc(*did("dve", f"rmul{h}"))
                dve.wait_ge(*seen(dve, f"rmul{h}"))
                dve.tensor_tensor(mix[:, h, :], mix[:, h, :], g_t[:, h, :], ALU.mult).then_inc(*did("dve", f"ret{h}"))

        wd_t = part(xT_t, 0, T)
        SHIFTED = [(3, r_t), (4, kr_t), (5, v_t)]
        lora_tmp = part(ring, WORK, 4, T)

        def shift_dve(dve):
            one = small[:, 8:24]
            for g in range(3, 7):
                for j in range(4):
                    m = P if g < 6 or j < 3 else 32
                    c = 4 * (g - 3) + j
                    dst = (r_t, kr_t, v_t)[g - 3][:, j, :] if g < 6 else \
                        (lora_tmp[:, 0, :], lora_tmp[:, 1, :], gate_in[:, 0, :], gate_in[:, 1, :])[j]
                    d3 = dst[0:m].rearrange("p (s t) -> p s t", s=2)
                    b3 = bank(f"win{g}.{j}")[0:m, :].rearrange("p (s t) -> p s t", s=2)
                    dve.wait_ge(*seen(dve, f"win{g}.{j}"))
                    dve.tensor_scalar(d3, b3, one[0:m, c:c + 1], None, ALU.mult).then_inc(*did("dve", f"sh{c}a"))
                    dve.wait_ge(*seen(dve, f"sh{c}a"))
                    dve.scalar_tensor_tensor(d3[:, :, 1:], b3[:, :, 0:TC - 1], V("mu0", c)[0:m], d3[:, :, 1:],
                                             ALU.mult, ALU.add).then_inc(*did("dve", f"sh{c}b"))
                    dve.wait_ge(*seen(dve, f"sh{c}b"))
                    dve.scalar_tensor_tensor(d3[:, :, 0:TC - 1], b3[:, :, 1:], V("mu1", c)[0:m], d3[:, :, 0:TC - 1],
                                             ALU.mult, ALU.add).then_inc(*did("dve", f"ev:win{g}.{j}"))

        def lora_pe(pe):
            w = slot(turn["lora", 0][0], 4, 512)
            pe.wait_ge(*arrived(("lora", 0)))
            for d in range(2):
                rows = slice(64 * d, 64 * d + 64)
                for c in range(NPAIR):
                    for what, i in (("lw", 0), ("la", 1)):
                        b = take(pe, f"{what}{d}.{c}")
                        if d == 0 and c == 0:
                            pe.wait_ge(*seen(pe, "tanh" if i == 0 else "ev:win6.1"))
                        pe.matmul(b[:, :], w[rows, i, c * P:(c + 1) * P], lora_tmp[rows, i, :], start=True, stop=True)\
                            .then_inc(*did("pe", f"{what}{d}.{c}"))
            for c in range(NPAIR):
                b = take(pe, f"kn{c}")
                pe.wait_ge(*seen(pe, f"ksq{c}"))
                pe.matmul(b[:, :], M["half_ones"], lora_tmp[:, 2, :], start=True, stop=True)\
                    .then_inc(*did("pe", f"kn{c}"))

        def lora_act(act):
            act.wait_ge(*seen(act, "ev:win6.0"))
            act.activation(lora_tmp[:, 0, :], lora_tmp[:, 0, :], ACT.Tanh).then_inc(*did("act", "tanh"))
            act.wait_ge(*seen(act, "ev:win6.3"))
            act.activation(gate_in[:, 0, :], gate_in[:, 0, :], ACT.Sigmoid).then_inc(*did("act"))
            act.activation(gate_in[0:32, 1, :], gate_in[0:32, 1, :], ACT.Sigmoid).then_inc(*did("act", "gate_in"))
            for d in range(2):
                for c in range(NPAIR):
                    act.wait_ge(*seen(act, f"lw{d}.{c}"))
                    act.activation(lw_t[d][:, c, :], bank(f"lw{d}.{c}")[:, :], ACT.Sigmoid, bias=V(f"w0_{d}", c))\
                        .then_inc(*did("act", f"ev:lw{d}.{c}"))
                    act.wait_ge(*seen(act, f"la{d}.{c}"))
                    act.activation(a_t[d][:, c, :], bank(f"la{d}.{c}")[:, :], ACT.Sigmoid, bias=V(f"a0_{d}", c))\
                        .then_inc(*did("act", f"ev:la{d}.{c}"))
            for c in range(NPAIR):
                act.wait_ge(*seen(act, f"kk0.{c}"))
                if c:
                    act.wait_ge(*seen(act, f"kn{c - 1}"))
                act.activation(lora_tmp[:, 2, :], kk_t[:, c, :], ACT.Square).then_inc(*did("act", f"ksq{c}"))
                act.wait_ge(*seen(act, f"kn{c}"))
                if c:
                    act.wait_ge(*seen(act, f"kk{c - 1}"))
                act.activation(lora_tmp[:, 3, :], bank(f"kn{c}")[:, :], ACT.Sqrt).then_inc(*did("act", f"ev:kn{c}"))

        def lora_dve(dve):
            dve.wait_ge(*seen(dve, "ev:win6.3"))
            for c in range(NPAIR):
                dve.tensor_scalar(kk_t[:, c, :], kr_t[:, c, :], V("k_k", c), None, ALU.mult)\
                    .then_inc(*did("dve", f"kk0.{c}"))
            for c in range(NPAIR):
                dve.wait_ge(*seen(dve, f"ev:kn{c}"))
                dve.tensor_scalar(lora_tmp[:, 3, :], lora_tmp[:, 3, :], 1e-12, None, ALU.max)\
                    .then_inc(*did("dve", f"kmax{c}"))
                dve.wait_ge(*seen(dve, f"kmax{c}"))
                dve.reciprocal(lora_tmp[:, 3, :], lora_tmp[:, 3, :]).then_inc(*did("dve", f"kinv{c}"))
                dve.wait_ge(*seen(dve, f"kinv{c}"))
                dve.tensor_tensor(kk_t[:, c, :], kk_t[:, c, :], lora_tmp[:, 3, :], ALU.mult)\
                    .then_inc(*did("dve", f"kk{c}"))
            for d in range(2):
                dve.wait_ge(*seen(dve, f"ev:lw{d}.3"))
                dve.tensor_scalar(lw_t[d], lw_t[d], LOG_DECAY, None, ALU.mult).then_inc(*did("dve", f"logw{d}"))

        def gate_pe(pe):
            w = slot(turn["lora", 0][0], 4, 512)
            for c in range(NPAIR):
                b = take(pe, f"gt{c}")
                if c == 0:
                    pe.wait_ge(*seen(pe, "gate_in"))
                pe.matmul(b[:, :], w[:, 2, c * P:(c + 1) * P], gate_in[:, 0, :], start=True, stop=False)
                pe.matmul(b[:, :], w[0:32, 3, c * P:(c + 1) * P], gate_in[0:32, 1, :], start=False, stop=True)\
                    .then_inc(*did("pe", f"gt{c}", *(["used:lora0"] if c == NPAIR - 1 else [])))

        def gate_act(act):
            for c in range(NPAIR):
                act.wait_ge(*seen(act, f"gt{c}"))
                act.activation(mix[:, 4 + c, :], bank(f"gt{c}")[:, :], ACT.Copy).then_inc(*did("act", f"ev:gt{c}"))

        w0 = WORK
        KR = part(ring, w0, NT, 2, P)
        BE = part(ring, w0 + 1024, 2, T)
        AT = part(ring, w0 + 2048, 8, P)
        RE = part(ring, w0 + 3072, 8, P)
        RB = part(ring, w0 + 4096, 8, P)
        BT = part(ring, w0 + 5120, 8, P)
        TI = BT
        TI_T = part(ring, w0 + 6144, 8, P)
        YL = part(ring, w0 + 7168, 8, P)
        WZ = YL
        RHS = part(ring, w0 + 8192, 8, P)
        b_tok = part(ring, w0 + 9216, NT, P)
        e_tok = part(ring, w0 + 9728, NT, P)
        v_pair = part(ring, w0 + 10240, T)
        v_tok = part(ring, w0 + 10752, NT, P)
        GM = part(ring, w0 + 11264, NT, 64)
        FM = part(ring, w0 + 11520, NT, 64)
        SH = part(ring, w0 + 11776, NT, 64)
        mid = part(ring, w0 + 12032, 4)
        rest = part(ring, w0 + 12036, 4)
        dmid = part(ring, w0 + 12040, 4)
        drest = part(ring, w0 + 12044, 4)
        step_decay = part(ring, w0 + 12048, 4)
        Fc, e1, e2, e3, kt, akk, ysum, bsum = (part(xT_t, i * T, T) for i in range(8))
        QM = e1
        UNITS = [(t, h) for h in range(2) for t in range(NT)]

        def settled(eng):
            eng.sem_inc(waited, 1)

        def half(h):
            return slice(64 * h, 64 * h + 64)

        def four(m):
            return m.unsqueeze(1).broadcast_to([P, 4, P])

        def pair_pe(pe, d, it):
            k = lambda s: named(f"{d}.", s)
            sn = lambda s: seen(pe, k(s), it)
            dd = lambda s: did("pe", k(s))
            first = ORDER[d][0]
            ada_loop_pe(pe, 3 * d, it)
            if d == 0:
                b = take(pe, k("vt"), it)
                pe.wait_ge(*sn("v_pair"))
                for t in range(NT):
                    mm = pe.transpose(b[:, t * P:(t + 1) * P], v_pair[:, t * P:(t + 1) * P], M["ident"])
                mm.then_inc(*dd("vt"))
            for name, ready, src in (("kt", "kappa", lambda t: KR[:, t, 0, :]),
                                     ("bt", "beta", lambda t: BE[:, 0, t * P:(t + 1) * P]),
                                     ("et", "eta", lambda t: BE[:, 1, t * P:(t + 1) * P])):
                b = take(pe, k(name), it)
                pe.wait_ge(*sn(ready))
                for t in range(NT):
                    mm = pe.transpose(b[:, t * P:(t + 1) * P], src(t), M["ident"])
                mm.then_inc(*dd(name))
            beta = lambda t, h: BE[half(h), 0, t * P:(t + 1) * P]
            eta = lambda t, h: BE[half(h), 1, t * P:(t + 1) * P]
            kappa = lambda t, h: KR[half(h), t, 0, :]
            rho = lambda t, h: KR[half(h), t, 1, :]

            def gram(name, lhs, rhs):
                for g in range(2):
                    b = take(pe, k(f"{name}{g}"), it)
                    for u, (t, h) in enumerate(UNITS[4 * g:4 * g + 4]):
                        mm = pe.matmul(b[:, u * P:(u + 1) * P], lhs(t, h), rhs(t, h), start=True, stop=True)
                    mm.then_inc(*dd(f"{name}{g}"))

            gram("BT", eta, kappa)
            gram("AT", beta, kappa)
            ada_turn_pe(pe, f"A{3 * d}", it)
            b = take(pe, k("BV"), it)
            pe.wait_ge(*sn("ev:BT1"))
            pe.wait_ge(*seen(pe, "ev:0.vt", it))
            for u, (t, h) in enumerate(UNITS):
                mm = pe.matmul(b[:, u * 64:(u + 1) * 64], BT[:, u, :], v_tok[:, t, half(h)], start=True, stop=True)
            mm.then_inc(*dd("BV"))
            gram("A", kappa, beta)
            pe.wait_ge(*sn("rho"))
            gram("RE", eta, rho)
            gram("RB", beta, rho)
            for li in range(1, len(LEVELS)):
                for g in range(2):
                    b = take(pe, k(f"Y{li}.{g}"), it)
                    pe.wait_ge(*sn(f"T{li - 1}.{g}"))
                    for u in range(4 * g, 4 * g + 4):
                        mm = pe.matmul(b[:, (u % 4) * P:(u % 4 + 1) * P], AT[:, u, :], TI[:, u, :], start=True, stop=True)
                    mm.then_inc(*dd(f"Y{li}.{g}"))
                for g in range(2):
                    pe.wait_ge(*sn(f"ev:Y{li}.{g}"))
                    pe.wait_ge(*sn(f"TT{li - 1}.{g}"))
                    if li < len(LEVELS) - 1:
                        b = take(pe, k(f"U{li}.{g}"), it)
                        for u in range(4 * g, 4 * g + 4):
                            mm = pe.matmul(b[:, (u % 4) * P:(u % 4 + 1) * P], TI_T[:, u, :], YL[:, u, :],
                                           start=True, stop=True)
                        mm.then_inc(*dd(f"U{li}.{g}"))
                    b = take(pe, k(f"V{li}.{g}"), it)
                    for u in range(4 * g, 4 * g + 4):
                        mm = pe.matmul(b[:, (u % 4) * P:(u % 4 + 1) * P], YL[:, u, :], TI_T[:, u, :], start=True, stop=True)
                    mm.then_inc(*dd(f"V{li}.{g}"))
                if li == 2:
                    ada_loop_pe(pe, 3 * d + 1, it)
                if li == 3:
                    ada_turn_pe(pe, f"A{3 * d + 1}", it)
                if li == 4 and d == 0:
                    ada_loop_pe(pe, 2, it)
                if li == 5 and d == 0:
                    ada_turn_pe(pe, "A2", it)
            for g in range(2):
                b = take(pe, k(f"WZ{g}"), it)
                pe.wait_ge(*sn(f"TT{len(LEVELS) - 1}.{g}"))
                pe.wait_ge(*sn("ev:kt"))
                pe.wait_ge(*sn("ev:BV"))
                for u in range(4 * g, 4 * g + 4):
                    mm = pe.matmul(b[:, (u % 4) * P:(u % 4 + 1) * P], TI_T[:, u, :], RHS[:, u, :], start=True, stop=True)
                mm.then_inc(*dd(f"WZ{g}"))
            b = take(pe, k("GF"), it)
            pe.wait_ge(*sn("ev:WZ1"))
            for i in range(3):
                t = ORDER[d][i]
                for h in range(2):
                    u = 4 * h + t
                    if i:
                        pe.matmul(b[half(h), i * 64:(i + 1) * 64], WZ[:, u, 0:64], b_tok[:, t, half(h)],
                                  start=True, stop=True)
                    f = b[half(h), 256 + i * 64:256 + (i + 1) * 64]
                    pe.matmul(f, e_tok[:, t, half(h)], v_tok[:, t, half(h)], start=True, stop=False)
                    mm = pe.matmul(f, b_tok[:, t, half(h)], WZ[:, u, 64:128], start=False, stop=True)
            mm.then_inc(*dd("GF"))
            b = take(pe, k("Q"), it)
            pe.wait_ge(*sn("ev:RB1"))
            for t, h in UNITS:
                if t != first:
                    mm = pe.matmul(b[half(h), t * P:(t + 1) * P], WZ[:, 4 * h + t, 0:64], RB[:, 4 * h + t, :],
                                   start=True, stop=True)
            mm.then_inc(*dd("Q"))
            for i in (1, 2):
                b = take(pe, k(f"S{i}"), it)
                pe.wait_ge(*sn("ev:GF" if i == 1 else "ev:S1"))
                settled(pe)
                for h in range(2):
                    mm = pe.matmul(b[half(h), 0:64], GM[half(h), i, :], (FM[half(h), 0, :] if i == 1 else SH[half(h), i, :]),
                                   start=True, stop=True)
                mm.then_inc(*dd(f"S{i}"))
            b = take(pe, k("y"), it)
            pe.wait_ge(*sn("ev:Q"))
            pe.wait_ge(*sn("ev:S2"))
            for i in range(NT):
                t = ORDER[d][i]
                state = (None, FM[:, 0, :], SH[:, 2, :], SH[:, 3, :])[i]
                for h in range(2):
                    u, o = 4 * h + t, b[half(h), t * P:(t + 1) * P]
                    pe.matmul(o, v_tok[:, t, half(h)], RE[:, u, :], start=True, stop=False)
                    mm = pe.matmul(o, WZ[:, u, 64:128], RB[:, u, :], start=False, stop=i == 0)
                    if i:
                        mm = pe.matmul(o, state[half(h)], QM[half(h), t * P:(t + 1) * P], start=False, stop=True)
            mm.then_inc(*dd("y"))

        def pair_act(act, d, it):
            k = lambda s: named(f"{d}.", s)
            sn = lambda s: seen(act, k(s), it)
            dd = lambda s: did("act", k(s))
            if d == 0:
                act.wait_ge(*seen(act, "ev:1.y", it, 1))
                act.activation(v_pair, v_t[:, it, :], ACT.Copy).then_inc(*dd("v_pair"))
                act.wait_ge(*sn("vt"))
                act.activation(v_tok, bank(k("vt"))[:, :].rearrange("p (a b) -> p a b", b=P), ACT.Copy)\
                    .then_inc(*dd("ev:vt"))
            act.wait_ge(*sn("F"))
            for dst, src, sign, ready in (((e1, e1, 1.0, "E"), (e2, Fc, 1.0, "F"), (e3, Fc, -1.0, "F")) if d == 0 else
                                          ((e2, e1, -1.0, "E"), (e3, e1, 1.0, "E"), (e1, Fc, -1.0, "F"))):
                act.wait_ge(*sn(ready))
                name = "e1" if dst is e1 else "e2" if dst is e2 else "e3"
                if d == 1 and dst is e1:
                    act.wait_ge(*sn("e3"))
                act.activation(dst, src, ACT.Exp, scale=sign).then_inc(*dd(name))
            act.activation(part(ring, w0 + 12040, 8), part(ring, w0 + 12032, 8), ACT.Exp).then_inc(*dd("dmid"))
            ada_act(act, f"A{3 * d}", it)
            act.wait_ge(*sn("kt"))
            act.activation(RHS[:, :, 0:64].rearrange("p (h t) c -> p h t c", h=2),
                           bank(k("kt"))[:, :].rearrange("p (t h c) -> p h t c", h=2, c=64), ACT.Copy)\
                .then_inc(*dd("ev:kt"))
            for name, dst in (("bt", b_tok), ("et", e_tok)):
                act.wait_ge(*sn(name))
                act.activation(dst, bank(k(name))[:, :].rearrange("p (a b) -> p a b", b=P), ACT.Copy)\
                    .then_inc(*dd("ev:" + name))
            act.wait_ge(*sn("BV"))
            act.activation(RHS[:, :, 64:128], bank(k("BV"))[:, :].rearrange("p (u c) -> p u c", c=64), ACT.Copy)\
                .then_inc(*dd("ev:BV"))
            for li in range(1, len(LEVELS)):
                for g in range(2):
                    act.wait_ge(*sn(f"Y{li}.{g}"))
                    act.activation(YL[:, 4 * g:4 * g + 4, :],
                                   bank(k(f"Y{li}.{g}"))[:, :].rearrange("p (a b) -> p a b", b=P), ACT.Copy)\
                        .then_inc(*dd(f"ev:Y{li}.{g}"))
                if li == 2:
                    ada_act(act, f"A{3 * d + 1}", it)
                if li == 4 and d == 0:
                    ada_act(act, "A2", it)
            for g in range(2):
                act.wait_ge(*sn(f"WZ{g}"))
                act.activation(WZ[:, 4 * g:4 * g + 4, :], bank(k(f"WZ{g}"))[:, :].rearrange("p (a b) -> p a b", b=P),
                               ACT.Copy).then_inc(*dd(f"ev:WZ{g}"))

        def pair_pool(pool, d, it):
            k = lambda s: named(f"{d}.", s)
            pool.wait_ge(*seen(pool, *(("ev:1.y", it, 1) if d == 0 else ("ev:0.y", it))))
            settled(pool)
            for g in range(2):
                pool.tensor_copy(TI_T[:, 4 * g:4 * g + 4, :], four(M["ident"])).then_inc(*did("pool", k(f"TT_id{g}")))
            pool.wait_ge(*seen(pool, k("BV"), it))
            settled(pool)
            for g in range(2):
                pool.tensor_copy(TI[:, 4 * g:4 * g + 4, :], four(M["ident"])).then_inc(*did("pool", k(f"T_id{g}")))

        def pair_dve(dve, d, it):
            k = lambda s: named(f"{d}.", s)
            sn = lambda s: seen(dve, k(s), it)
            dd = lambda *s: did("dve", *[k(x) for x in s])
            r, kr, kk, a, lw = (t[:, it, :] for t in (r_t, kr_t, kk_t, a_t[d], lw_t[d]))
            f4 = Fc.rearrange("p (t c) -> p t c", c=P)
            dve.wait_ge(*seen(dve, *(("ev:1.y", it, 1) if d == 0 else ("ev:0.y", it))))
            for t in range(NT):
                dve.tensor_tensor_scan(Fc[:, t * P:(t + 1) * P], M["ones"], lw_t[d][:, it, t * P:(t + 1) * P], 0.0,
                                       ALU.mult, ALU.add).then_inc(*dd(f"scan{t}"))
            dve.tensor_tensor(akk, a, kk, ALU.mult).then_inc(*dd("akk"))
            ka = vec[:, bass.ds(VEC["k_a"][0] + it, 1)]
            dve.tensor_scalar(kt, a, 1.0, ka, ALU.subtract, ALU.mult).then_inc(*dd("kt1"))
            dve.wait_ge(*sn("scan3"))
            dve.tensor_copy(mid, f4[:, :, 63]).then_inc(*dd("mid"))
            dve.wait_ge(*sn("mid"))
            dve.tensor_tensor(rest, f4[:, :, P - 1], mid, ALU.subtract).then_inc(*dd("rest"))
            dve.wait_ge(*sn("rest"))
            dve.tensor_tensor(f4, f4, mid.unsqueeze(2).broadcast_to([P, NT, P]), ALU.subtract).then_inc(*dd("F"))
            dve.wait_ge(*sn("F"))
            dve.tensor_tensor(e1, Fc, lw, ALU.subtract).then_inc(*dd("E"))
            dve.wait_ge(*sn("kt1"))
            dve.scalar_tensor_tensor(kt, kt, 1.0, kr, ALU.add, ALU.mult).then_inc(*dd("kt2"))
            dve.wait_ge(*sn("kt2"))
            if d == 0:
                dve.tensor_tensor(bsum, kt, r, ALU.mult).then_inc(*dd("bsum"))
            r4, kk4 = (x.rearrange("p (t c) -> p t c", c=P) for x in (e2, e1))
            dve.wait_ge(*sn("e1"))
            dve.tensor_tensor(KR[:, :, 0, :], kk_t[:, it, :].rearrange("p (t c) -> p t c", c=P), kk4, ALU.mult)\
                .then_inc(*dd("kappa"))
            dve.wait_ge(*sn("e3"))
            dve.scalar_tensor_tensor(BE[:, 0, :], akk, -1.0, e3, ALU.mult, ALU.mult).then_inc(*dd("beta"))
            dve.tensor_tensor(BE[:, 1, :], kt, e3, ALU.mult).then_inc(*dd("eta"))
            dve.wait_ge(*sn("e2"))
            dve.tensor_tensor(KR[:, :, 1, :], r_t[:, it, :].rearrange("p (t c) -> p t c", c=P), r4, ALU.mult)\
                .then_inc(*dd("rho"))
            dve.wait_ge(*sn("dmid"))
            leave, come = (drest, dmid) if d == 0 else (dmid, drest)
            for i in range(3):
                x, y = ORDER[d][i], ORDER[d][i + 1]
                dve.tensor_tensor(step_decay[:, i:i + 1], leave[:, x:x + 1], come[:, y:y + 1], ALU.mult)\
                    .then_inc(*dd(f"dc{i}"))
            strict, incl = ("lt", "le") if d == 0 else ("gt", "ge")

            def v3(job):
                return bank(k(job))[:, :].rearrange("p (a b) -> p a b", b=P)

            def masked(name, dst, m, g):
                dve.wait_ge(*sn(f"{name}{g}"))
                dve.tensor_tensor(dst[:, 4 * g:4 * g + 4, :], v3(f"{name}{g}"), four(M[m]), ALU.mult)\
                    .then_inc(*dd(f"ev:{name}{g}"))

            for g in range(2):
                masked("BT", BT, strict, g)
            for g in range(2):
                masked("AT", AT, strict, g)
            for g in range(2):
                gs = slice(4 * g, 4 * g + 4)
                dve.wait_ge(*seen(dve, k(f"TT_id{g}"), it))
                dve.wait_ge(*sn(f"ev:AT{g}"))
                settled(dve)
                dve.copy_predicated(TI_T[:, gs, :], four(level[:, 1 - d, 0, :]), AT[:, gs, :]).then_inc(*dd(f"TT0.{g}"))
                dve.wait_ge(*seen(dve, k(f"T_id{g}"), it))
                dve.wait_ge(*sn(f"A{g}"))
                settled(dve)
                dve.copy_predicated(TI[:, gs, :], four(level[:, d, 0, :]), v3(f"A{g}")).then_inc(*dd(f"T0.{g}", f"ev:A{g}"))
            ada_loop_dve(dve, 3 * d, it)
            for g in range(2):
                masked("RE", RE, incl, g)
            for g in range(2):
                masked("RB", RB, incl, g)
            for li in range(1, len(LEVELS)):
                for g in range(2):
                    gs = slice(4 * g, 4 * g + 4)
                    if li < len(LEVELS) - 1:
                        dve.wait_ge(*sn(f"U{li}.{g}"))
                        settled(dve)
                        dve.copy_predicated(TI[:, gs, :], four(level[:, d, li, :]), v3(f"U{li}.{g}"))\
                            .then_inc(*dd(f"T{li}.{g}", f"ev:U{li}.{g}"))
                    dve.wait_ge(*sn(f"V{li}.{g}"))
                    settled(dve)
                    dve.copy_predicated(TI_T[:, gs, :], four(level[:, 1 - d, li, :]), v3(f"V{li}.{g}"))\
                        .then_inc(*dd(f"TT{li}.{g}", f"ev:V{li}.{g}"))
                if li == 3:
                    ada_loop_dve(dve, 3 * d + 1, it)
                if li == 5 and d == 0:
                    ada_loop_dve(dve, 2, it)
            dve.wait_ge(*sn("GF"))
            gf = bank(k("GF"))[:, :].rearrange("p (a b) -> p a b", b=64)
            dve.tensor_tensor(GM[:, 1:3, :], gf[:, 1:3, :], M["eye2"][:, 0:64].unsqueeze(1).broadcast_to([P, 2, 64]),
                              ALU.add).then_inc(*dd("GM"))
            dve.wait_ge(*sn("dc2"))
            dve.tensor_tensor(FM[:, 0:3, :], gf[:, 4:7, :], step_decay[:, 0:3].unsqueeze(2).broadcast_to([P, 3, 64]),
                              ALU.mult).then_inc(*dd("ev:GF"))
            dve.wait_ge(*sn("Q"))
            q0, q1 = (1, 4) if d == 0 else (0, 4)
            lots = [(1, 4)] if d == 0 else [(0, 1), (2, 4)]
            for n, (x, y) in enumerate(lots):
                dve.tensor_tensor(QM.rearrange("p (t c) -> p t c", c=P)[:, x:y, :], v3("Q")[:, x:y, :], KR[:, x:y, 1, :],
                                  ALU.add).then_inc(*dd(*(["ev:Q"] if n == len(lots) - 1 else [])))
            for i in (1, 2):
                dve.wait_ge(*sn(f"S{i}"))
                dve.wait_ge(*sn("ev:GF"))
                dve.scalar_tensor_tensor(SH[:, i + 1, :], bank(k(f"S{i}"))[:, 0:64], step_decay[:, i:i + 1],
                                         FM[:, i, :], ALU.mult, ALU.add).then_inc(*dd(f"ev:S{i}"))
            if d == 1:
                dve.tensor_tensor(kt, kt, r, ALU.mult).then_inc(*dd("bs1"))
                dve.wait_ge(*sn("bs1"))
                dve.tensor_tensor(r_t[:, it, :], bsum, kt, ALU.add).then_inc(*dd("bs2"))
            dve.wait_ge(*sn("y"))
            if d == 0:
                dve.tensor_copy(ysum, bank(k("y"))[:, :]).then_inc(*dd("ev:y"))
            else:
                dve.tensor_tensor(kk_t[:, it, :], bank(k("y"))[:, :], ysum, ALU.add).then_inc(*dd("ev:y"))

        def pair_loop(eng, name, body):
            base = L.enter(name, "pair")
            with eng.Fori(0, NPAIR) as it:
                for d in range(2):
                    body(eng, d, it)
            L.leave(name, base, NPAIR)

        post = part(ring, WORK, 4, T)

        def post_pe(pe):
            for c in range(NPAIR):
                for name, ready, src in (("pm", None, kk_t[:, c, :]), ("pv", f"psq{c}", post[:, 0, :]),
                                         ("pb", f"prk{c}", post[:, 1, :])):
                    b = take(pe, f"{name}{c}")
                    if ready:
                        pe.wait_ge(*seen(pe, ready))
                    pe.matmul(b[:, :], M["half_ones"], src, start=True, stop=True).then_inc(*did("pe", f"{name}{c}"))

        def post_act(act):
            for c in range(NPAIR):
                act.wait_ge(*seen(act, f"ev:pm{c}"))
                if c:
                    act.wait_ge(*seen(act, f"pv{c - 1}"))
                act.activation(post[:, 0, :], kk_t[:, c, :], ACT.Square).then_inc(*did("act", f"psq{c}"))
                act.wait_ge(*seen(act, f"pv{c}"))
                if c:
                    act.wait_ge(*seen(act, f"pn{c - 1}"))
                act.activation(post[:, 2, :], bank(f"pv{c}")[:, :], ACT.Sqrt, bias=small[:, 1:2], scale=1.0 / 64)\
                    .then_inc(*did("act", f"ev:pv{c}"))

        def post_dve(dve):
            for c in range(NPAIR):
                y = kk_t[:, c, :]
                if c:
                    dve.wait_ge(*seen(dve, f"pb{c - 1}"))
                dve.tensor_scalar(post[:, 1, :], r_t[:, c, :], V("r_k", c), None, ALU.mult).then_inc(*did("dve", f"prk{c}"))
                dve.wait_ge(*seen(dve, f"pm{c}"))
                dve.scalar_tensor_tensor(y, bank(f"pm{c}")[:, :], -1.0 / 64, y, ALU.mult, ALU.add)\
                    .then_inc(*did("dve", f"ev:pm{c}"))
                dve.wait_ge(*seen(dve, f"pb{c}"))
                dve.tensor_tensor(v_t[:, c, :], bank(f"pb{c}")[:, :], v_t[:, c, :], ALU.mult)\
                    .then_inc(*did("dve", f"ev:pb{c}"))
                dve.wait_ge(*seen(dve, f"ev:pv{c}"))
                dve.reciprocal(post[:, 2, :], post[:, 2, :]).then_inc(*did("dve", f"pinv{c}"))
                dve.wait_ge(*seen(dve, f"pinv{c}"))
                dve.tensor_tensor(y, y, post[:, 2, :], ALU.mult).then_inc(*did("dve", f"pn{c}"))
                dve.wait_ge(*seen(dve, f"pn{c}"))
                dve.tensor_scalar(y, y, V("lnx_w", c), V("lnx_b", c), ALU.mult, ALU.add).then_inc(*did("dve", f"pl{c}"))
                dve.wait_ge(*seen(dve, f"pl{c}"))
                dve.tensor_tensor(y, y, v_t[:, c, :], ALU.add).then_inc(*did("dve", f"py{c}"))
                dve.wait_ge(*seen(dve, f"py{c}"))
                dve.tensor_tensor(mix[:, 4 + c, :], mix[:, 4 + c, :], y, ALU.mult).then_inc(*did("dve", f"mix{c}"))

        def wout_pe(pe, array, tag, a, ready):
            for g in range(2):
                key = (array, g)
                pe.wait_ge(*arrived(key))
                w = slot(turn[key][0], DC, 512)
                for j in range(4):
                    if g == 0 and j == 0:
                        pe.wait_ge(*seen(pe, ready))
                    mm = proj_pe(pe, f"{tag}.{4 * g + j}", w, DC, j * P, lambda k: mix[:, k, a:T], T - a)
                    mm.then_inc(*did("pe", f"{tag}.{4 * g + j}", *([f"used:{array}{g}"] if j == 3 else [])))

        def residual_dve(dve, tag, layer, m, a, h):
            for c in range(DC):
                dve.wait_ge(*seen(dve, f"{tag}.{c}"))
                for x in range(a, T, TC):
                    dve.scalar_tensor_tensor(h[:, c, x:x + TC], bank(f"{tag}.{c}")[:, x - a:x - a + TC],
                                             mods[:, layer, 8 * m + c, x // TC:x // TC + 1], h[:, c, x:x + TC],
                                             ALU.mult, ALU.add)\
                        .then_inc(*did("dve", *([f"ev:{tag}.{c}", f"{tag}.h{c}"] if x == T - TC else [])))

        route_w = part(feat_t, 8192, DC, NR)
        logits = part(feat_t, 8480, NT, NR)
        route = part(feat_t, 8624, 24, NT * EPG)
        chosen_by = part(feat_t, 9392, 2, NT * NE)
        either = part(feat_t, 9648, NT, NE)
        place = part(feat_t, 9776, NT, NE)
        beyond = part(feat_t, 9904, NT, NE)
        count = part(feat_t, 10032, NE)
        extras = part(feat_t, 10064, NE)
        so_far = part(feat_t, 10096, NE)
        wide_t = part(feat_t, 10128, 16 * NE)
        tab = part(feat_t, 10640, 192)
        rank, first_row, limits, ordinals, slots0 = (tab[:, x:y] for x, y in ((0, 8), (8, 40), (40, 48), (48, 64), (64, 192)))
        route_b = part(feat_t, 10832, NR)
        row_of = part(feat_t, 10868, 2, NT)
        share = part(feat_t, 10876, 2, NT)
        row_int = row_int_t[:]
        extra_of = extra_of_t[:, 0:16]
        n_extra = extra_of_t[:, 16:17]
        rows_now = part(feat_t, 10884, P)
        sel_a = part(feat_t, 11012, NT, P)
        sel = part(feat_t, 11524, 2, NT * P)
        sil = part(feat_t, 12548, P)
        hid_t = part(feat_t, 12676, P)
        hid = part(feat_t, 12804, 2, CAP)
        xg = part(feat_t, 4096, 2, DC * P)
        yt = part(feat_t, 6144, 4, 512)
        x_tok = part(hm_t, 0, NT, D)
        got = (part(hm_t, 0, NT, D), part(feat_t, 4096, NT, D))

        def route_pe(pe, l, a):
            tag, nt = f"m{l}", (T - a) // P
            b = take(pe, tag + ".logits")
            pe.wait_ge(router_in, 48 * (l + 1))
            for t in range(nt):
                for k in range(DC):
                    if t == 0:
                        pe.wait_ge(*seen(pe, f"n2{l}.x{k}"))
                    pe.matmul(b[:, t * NR:(t + 1) * NR], xT[:, k, a + t * P:a + (t + 1) * P], route_w[:, k, :],
                              start=k == 0, stop=False)
                mm = pe.matmul(b[:, t * NR:(t + 1) * NR], M["ones"][0:1, :], route_b[0:1, :], start=False, stop=True)
            mm.then_inc(*did("pe", tag + ".logits"))
            for t in range(nt):
                for g in range(2):
                    b = take(pe, f"{tag}.xt{t}.{g}")
                    for c in range(4):
                        mm = pe.transpose(b[:, c * P:(c + 1) * P], xT[:, 4 * g + c, a + t * P:a + (t + 1) * P], M["ident"])
                    mm.then_inc(*did("pe", f"{tag}.xt{t}.{g}"))
            b = take(pe, tag + ".place")
            pe.wait_ge(*seen(pe, tag + ".either"))
            for t in range(nt):
                for j in range(t):
                    pe.matmul(b[:, t * NE:(t + 1) * NE], M["ones"], either[:, j, :], start=j == 0, stop=False)
                pe.matmul(b[:, t * NE:(t + 1) * NE], M["lt"], either[:, t, :], start=t == 0, stop=True)
            for j in range(nt):
                mm = pe.matmul(b[:, NT * NE:(NT + 1) * NE], M["ones"], either[:, j, :], start=j == 0, stop=j == nt - 1)
            mm.then_inc(*did("pe", tag + ".place"))
            gather_pe(pe, l, a, f"m{l}.", 0, None)

        def route_dve(dve, l, a):
            tag, nt = f"m{l}", (T - a) // P
            n = [0]

            def link(ins):
                n[0] += 1
                ins.then_inc(*did("dve", f"{tag}.route{n[0]}"))
                dve.wait_ge(*seen(dve, f"{tag}.route{n[0]}"))

            def row(i, w):
                return route[:, i, 0:nt * w].rearrange("p (t w) -> p t w", w=w)

            def wide(x, w):
                return x.broadcast_to([P, nt, w])

            lg, one = logits[:, 0:nt, :], lambda i: row(i, 1)

            def first_of(dst, x, top, w, i):
                link(dve.tensor_tensor(row(i, w), x, wide(top, w), ALU.is_equal))
                link(dve.tensor_tensor(row(i, w), row(i, w),
                                       rank[:, EPG - w:EPG].unsqueeze(1).broadcast_to([P, nt, w]), ALU.mult))
                link(dve.tensor_reduce(one(i + 1), row(i, w), AX, ALU.max))
                link(dve.tensor_tensor(dst, row(i, w), wide(one(i + 1), w), ALU.is_equal))

            dve.wait_ge(*seen(dve, tag + ".logits"))
            dve.tensor_copy(lg, bank(tag + ".logits")[:, 0:nt * NR].rearrange("p (t r) -> p t r", r=NR))\
                .then_inc(*did("dve", f"ev:{tag}.logits"))
            dve.wait_ge(*seen(dve, f"ev:{tag}.logits"))
            groups, experts = lg[:, :, 0:NG], lg[:, :, NG:NR]
            link(dve.tensor_reduce(one(0), groups, AX, ALU.max))
            link(dve.tensor_tensor(row(1, NG), groups, wide(one(0), NG), ALU.subtract))
            first_of(row(2, NG), groups, one(0), NG, 3)
            chosen = row(5, EPG)
            for g in range(NG):
                x = experts[:, :, g * EPG:(g + 1) * EPG]
                oh = wide(row(2, NG)[:, :, g:g + 1], EPG)
                link(dve.tensor_tensor(chosen if g == 0 else row(6, EPG), x, oh, ALU.mult))
                if g:
                    link(dve.tensor_tensor(chosen, chosen, row(6, EPG), ALU.add))
            link(dve.tensor_reduce(one(7), chosen, AX, ALU.max))
            first_of(row(8, EPG), chosen, one(7), EPG, 9)
            link(dve.scalar_tensor_tensor(row(11, EPG), row(8, EPG), -3e38, chosen, ALU.mult, ALU.add))
            link(dve.tensor_reduce(one(12), row(11, EPG), AX, ALU.max))
            first_of(row(13, EPG), row(11, EPG), one(12), EPG, 14)
            dve.tensor_tensor(one(16), one(12), one(7), ALU.subtract).then_inc(*did("dve", tag + ".gap"))
            chosen_at = [chosen_by[:, k, 0:nt * NE].rearrange("p (t g e) -> p t g e", g=NG, e=EPG) for k in range(2)]
            by = [chosen_by[:, k, 0:nt * NE].rearrange("p (t e) -> p t e", e=NE) for k in range(2)]
            for k, i in enumerate((8, 13)):
                link(dve.tensor_tensor(chosen_at[k], row(2, NG).unsqueeze(3).broadcast_to([P, nt, NG, EPG]),
                                       row(i, EPG).unsqueeze(2).broadcast_to([P, nt, NG, EPG]), ALU.mult))
            dve.tensor_tensor(either[:, 0:nt, :], by[0], by[1], ALU.add).then_inc(*did("dve", tag + ".either"))
            dve.wait_ge(*seen(dve, tag + ".exps"))
            link(dve.tensor_reduce(one(17), row(1, NG), AX, ALU.add))
            link(dve.tensor_scalar(one(18), one(16), 1.0, None, ALU.add))
            link(dve.tensor_tensor(one(17), one(17), one(18), ALU.mult))
            link(dve.reciprocal(share[:, 0, 0:nt], route[:, 17, 0:nt]))
            link(dve.tensor_tensor(share[:, 1, 0:nt], share[:, 0, 0:nt], route[:, 16, 0:nt], ALU.mult))
            dve.wait_ge(*seen(dve, tag + ".place"))
            b = bank(tag + ".place")
            link(dve.tensor_copy(place[:, 0:nt, :], b[:, 0:nt * NE].rearrange("p (t e) -> p t e", e=NE)))
            dve.tensor_copy(count, b[:, NT * NE:(NT + 1) * NE]).then_inc(*did("dve", f"ev:{tag}.place"))
            dve.wait_ge(*seen(dve, f"ev:{tag}.place"))
            link(dve.tensor_tensor(wide_t[:, 0:8 * NE].rearrange("p (e m) -> p e m", m=8),
                                   count.unsqueeze(2).broadcast_to([P, NE, 8]),
                                   limits.unsqueeze(1).broadcast_to([P, NE, 8]), ALU.is_gt))
            link(dve.tensor_reduce(extras, wide_t[:, 0:8 * NE].rearrange("p (e m) -> p e m", m=8), AX, ALU.add))
            link(dve.tensor_tensor_scan(so_far, M["ones"][:, 0:NE], extras, 0.0, ALU.mult, ALU.add))
            link(dve.tensor_copy(n_extra, so_far[:, NE - 1:NE]))
            w3 = wide_t.rearrange("p (x e) -> p x e", e=NE)
            link(dve.tensor_tensor(w3, so_far.unsqueeze(1).broadcast_to([P, 16, NE]),
                                   ordinals.unsqueeze(2).broadcast_to([P, 16, NE]), ALU.is_le))
            link(dve.tensor_reduce(route[:, 0, 0:16], w3, AX, ALU.add))
            link(dve.tensor_scalar(route[:, 0, 0:16], route[:, 0, 0:16], NE - 1.0, None, ALU.min))
            dve.tensor_copy(extra_of, route[:, 0, 0:16]).then_inc(*did("dve", tag + ".extras"))
            link(dve.tensor_tensor(so_far, so_far, extras, ALU.subtract))
            link(dve.tensor_scalar(so_far, so_far, float(CAP), float(CAP * (NE - 1)), ALU.mult, ALU.add))
            link(dve.tensor_tensor(so_far, so_far, first_row, ALU.subtract))
            link(dve.tensor_scalar(beyond[:, 0:nt, :], place[:, 0:nt, :], float(CAP), None, ALU.is_ge))
            link(dve.tensor_tensor(beyond[:, 0:nt, :], beyond[:, 0:nt, :], so_far.unsqueeze(1).broadcast_to([P, nt, NE]),
                                   ALU.mult))
            link(dve.tensor_tensor(place[:, 0:nt, :], place[:, 0:nt, :], first_row.unsqueeze(1).broadcast_to([P, nt, NE]),
                                   ALU.add))
            link(dve.tensor_tensor(place[:, 0:nt, :], place[:, 0:nt, :], beyond[:, 0:nt, :], ALU.add))
            for k in range(2):
                link(dve.tensor_tensor(beyond[:, 0:nt, :], place[:, 0:nt, :], by[k], ALU.mult))
                link(dve.tensor_reduce(row_of[:, k, 0:nt], beyond[:, 0:nt, :], AX, ALU.add))
            dve.tensor_copy(row_int, row_of).then_inc(*did("dve", tag + ".rows"))
            dve.tensor_copy(rows_now, slots0).then_inc(*did("dve", tag + ".now"))
            select_dve(dve, l, a, f"m{l}.", 0, None, (f"m{l}.now", None, 0))

        def route_act(act, l, a):
            tag, nt = f"m{l}", (T - a) // P
            for t in range(nt):
                for g in range(2):
                    act.wait_ge(*seen(act, f"{tag}.xt{t}.{g}"))
                    act.activation(x_tok[:, t, 512 * g:512 * g + 512], bank(f"{tag}.xt{t}.{g}")[:, :], ACT.Copy)\
                        .then_inc(*did("act", f"ev:{tag}.xt{t}.{g}"))
            act.wait_ge(*seen(act, tag + ".gap"))
            act.activation(route[:, 1, 0:nt * NG], route[:, 1, 0:nt * NG], ACT.Exp).then_inc(*did("act"))
            act.activation(route[:, 16, 0:nt], route[:, 16, 0:nt], ACT.Exp).then_inc(*did("act", tag + ".exps"))
            for half in range(2):
                take_in_act(act, f"m{l}.", half, 0, None)

        def select_dve(dve, l, a, prefix, par, it, ready):
            nt, k_ = (T - a) // P, lambda x: named(prefix, x)
            s3 = sel[:, par, 0:nt * P].rearrange("p (t c) -> p t c", c=P)
            now = rows_now.unsqueeze(1).broadcast_to([P, nt, P])
            dve.wait_ge(*seen(dve, *ready))
            for k, dst in ((0, sel_a[:, 0:nt, :]), (1, s3)):
                dve.tensor_tensor(dst, row_of[:, k, 0:nt].unsqueeze(2).broadcast_to([P, nt, P]), now, ALU.is_equal)\
                    .then_inc(*did("dve", k_(f"sel{k}")))
            dve.wait_ge(*seen(dve, k_("sel1"), it))
            dve.tensor_tensor(s3, s3, sel_a[:, 0:nt, :], ALU.add).then_inc(*did("dve", k_("sel")))
            dve.tensor_scalar(rows_now, rows_now, float(P), None, ALU.add).then_inc(*did("dve", k_("next")))

        def gather_part(pe, l, a, b, half, par, chunks):
            nt = (T - a) // P
            for c in chunks:
                for t in range(nt):
                    mm = pe.matmul(b[:, c * P:(c + 1) * P], x_tok[:, t, (4 * half + c) * P:(4 * half + c + 1) * P],
                                   sel[:, par, t * P:(t + 1) * P], start=t == 0, stop=t == nt - 1)
            return mm

        def gather_pe(pe, l, a, prefix, par, it):
            k_ = lambda x: named(prefix, x)
            for half in range(2):
                b = take(pe, k_(f"xg{half}"), it)
                if half == 0:
                    pe.wait_ge(*seen(pe, k_("sel"), it))
                    if it is None:
                        pe.wait_ge(*seen(pe, f"ev:m{l}.xt{(T - a) // P - 1}.1"))
                gather_part(pe, l, a, b, half, par, range(4)).then_inc(*did("pe", k_(f"xg{half}")))

        def take_in_act(act, prefix, half, par, it):
            k_ = lambda x: named(prefix, x)
            act.wait_ge(*seen(act, k_(f"xg{half}"), it))
            act.activation(xg[:, par, 512 * half:512 * half + 512], bank(k_(f"xg{half}"))[:, :], ACT.Copy)\
                .then_inc(*did("act", k_(f"ev:xg{half}")))

        def hidden_pe(pe, prefix, s, par, it, turn_, ready):
            k_ = lambda x: named(prefix, x)
            w = part(ring, s * SLOT, 2, DC * 256).rearrange("p a (k n) -> p a k n", n=256)
            b = take(pe, k_("gu"), it)
            pe.wait_ge(loaded[s], it * 16 + 16 * turn_)
            if ready is not None:
                pe.wait_ge(*seen(pe, *ready))
            x = xg[:, par, :].rearrange("p (k j c) -> p k j c", j=2, c=CAP)
            for k in range(DC):
                for g in range(2):
                    mm = pe.matmul(b[64 * g:64 * g + 64, 0:256].rearrange("p (a n) -> p a n", n=P), x[:, k, s % 2, :],
                                   w[:, :, k, g * P:(g + 1) * P], start=k == 0, stop=k == DC - 1)
            mm.then_inc(*did("pe", k_("gu")))

        def hidden_act(act, prefix, it):
            k_ = lambda x: named(prefix, x)
            act.wait_ge(*seen(act, k_("gu"), it))
            act.activation(sil, bank(k_("gu"))[:, 0:P], ACT.Silu).then_inc(*did("act", k_("sil")))

        def hidden_dve(dve, prefix, it):
            k_ = lambda x: named(prefix, x)
            dve.wait_ge(*seen(dve, k_("sil"), it))
            dve.tensor_tensor(hid_t, bank(k_("gu"))[:, P:2 * P], sil, ALU.mult).then_inc(*did("dve", k_("ev:gu")))

        def turn_pe(pe, prefix, it):
            k_ = lambda x: named(prefix, x)
            b = take(pe, k_("ht"), it)
            pe.wait_ge(*seen(pe, k_("ev:gu"), it))
            pe.transpose(b[:, 0:P], hid_t, M["ident"]).then_inc(*did("pe", k_("ht")))

        def turn_act(act, prefix, it):
            k_ = lambda x: named(prefix, x)
            act.wait_ge(*seen(act, k_("ht"), it))
            act.activation(hid, bank(k_("ht"))[:, 0:P].rearrange("p (h c) -> p h c", c=CAP), ACT.Copy)\
                .then_inc(*did("act", k_("ev:ht")))

        def down_pe(pe, prefix, s, it):
            k_ = lambda x: named(prefix, x)
            down = part(ring, s * SLOT + 4096, 2, D)
            b = take(pe, k_("down"), it)
            pe.wait_ge(*seen(pe, k_("ev:ht"), it))
            for hc in range(2):
                for g in range(2):
                    mm = pe.matmul(b[64 * g:64 * g + 64, :], hid[:, hc, :], down[:, hc, 512 * g:512 * g + 512],
                                   start=hc == 0, stop=hc == 1)
            mm.then_inc(*did("pe", k_("down")))

        def down_dve(dve, prefix, s, it, out_turn):
            k_ = lambda x: named(prefix, x)
            dve.wait_ge(*seen(dve, k_("down"), it))
            dve.wait_ge(y_out[s], it * 32 + 32 * out_turn)
            dve.tensor_copy(yt[:, s, :], bank(k_("down"))[:, :]).then_inc(*did("dve", k_("ev:down")))

        def expert_pe(pe, l, a, s, it, first_turn):
            me, before, par = f"e{l}.{s}.", f"e{l}.{(s - 1) % 4}.", s // 2
            hidden_pe(pe, me, s, par, it, first_turn,
                      None if s % 2 else (named(before, "ev:xg1"), it, 0 if s else 1))
            b = take(pe, named(me, f"xg{s % 2}"), it)
            if s % 2 == 0:
                pe.wait_ge(*seen(pe, named(me, "sel"), it))
            gather_part(pe, l, a, b, s % 2, 1 - par, range(2))
            turn_pe(pe, me, it)
            gather_part(pe, l, a, b, s % 2, 1 - par, range(2, 4)).then_inc(*did("pe", named(me, f"xg{s % 2}")))
            down_pe(pe, me, s, it)

        def expert_act(act, l, s, it):
            me = f"e{l}.{s}."
            hidden_act(act, me, it)
            turn_act(act, me, it)
            take_in_act(act, me, s % 2, 1 - s // 2, it)

        def expert_dve(dve, l, a, s, it):
            me, before = f"e{l}.{s}.", f"e{l}.{(s - 2) % 4}."
            if s % 2 == 0:
                select_dve(dve, l, a, me, 1 - s // 2, it, (named(before, "next"), it, 0 if s else 1))
            hidden_dve(dve, me, it)
            down_dve(dve, me, s, it, out_base[l][s])

        def expert_loop(eng, name, l, body):
            base = L.enter(name, f"experts{l}")
            with eng.Fori(0, NE // 4) as it:
                for s in range(4):
                    body(s, it)
            L.leave(name, base, NE // 4)

        n_extras = [16, 8]
        out_base, extra_base = [(1, 1, 1, 1)], []
        for l in range(2):
            extra_base.append(tuple(x + NE // 4 for x in out_base[l]))
            out_base.append(tuple(x + (n_extras[l] // 2 if s < 2 else 0) for s, x in enumerate(extra_base[l])))

        def extra_loop(eng, name, l, body):
            n = eng.value_load(n_extra[0:1, :], min_val=0, max_val=16)
            base = L.enter(name, f"extras{l}")
            with eng.Fori(0, n_extras[l] // 2) as it:
                with eng.If(n > it * 2):
                    body(it)
                with eng.Else():
                    eng.drain()
                    eng.sem_inc(sems[name], max(L.count[name], 1))
            L.leave(name, base, n_extras[l] // 2)

        def extra_pe(pe, l, a, it):
            for s in range(2):
                me = f"x{l}.{s}."
                hidden_pe(pe, me, s, 0, it, turn["extra", 16 * l + s][1],
                          None if s else (named(f"x{l}.0.", "ev:xg1"), it, 1))
                turn_pe(pe, me, it)
                down_pe(pe, me, s, it)
            gather_pe(pe, l, a, f"x{l}.0.", 0, it)

        def extra_act(act, l, it):
            for s in range(2):
                hidden_act(act, f"x{l}.{s}.", it)
                turn_act(act, f"x{l}.{s}.", it)
            for half in range(2):
                take_in_act(act, f"x{l}.0.", half, 0, it)

        def extra_dve(dve, l, a, it):
            dve.wait_ge(*seen(dve, f"x{l}.0.xg1", it, 1))
            select_dve(dve, l, a, f"x{l}.0.", 0, it, (f"x{l}.0.next", it, 1))
            for s in range(2):
                hidden_dve(dve, f"x{l}.{s}.", it)
                down_dve(dve, f"x{l}.{s}.", s, it, extra_base[l][s])

        def mixed_pe(pe, l, a):
            nt = (T - a) // P
            for c in range(DC):
                b = take(pe, f"z{l}.{c}")
                for t in range(nt):
                    if c == 0:
                        pe.wait_ge(*seen(pe, f"z{l}.y{t}"))
                    mm = pe.transpose(b[:, t * P:(t + 1) * P], got[0][:, t, c * P:(c + 1) * P], M["ident"])
                mm.then_inc(*did("pe", f"z{l}.{c}"))

        def mixed_act(act, l, a):
            for t in range((T - a) // P):
                act.wait_ge(got_in[t], 32 * (l + 1))
                act.activation(got[0][:, t, :], got[0][:, t, :], ACT.Copy, scale=share[:, 0, t:t + 1])\
                    .then_inc(*did("act", f"z{l}.a{t}"))

        def mixed_dve(dve, l, a):
            for t in range((T - a) // P):
                dve.wait_ge(got_in[t], 32 * (l + 1))
                dve.wait_ge(*seen(dve, f"z{l}.a{t}"))
                dve.scalar_tensor_tensor(got[0][:, t, :], got[1][:, t, :], share[:, 1, t:t + 1], got[0][:, t, :],
                                         ALU.mult, ALU.add).then_inc(*did("dve", f"z{l}.y{t}"))
            residual_dve(dve, f"z{l}", l, 5, a, hT)

        def mixed_pool(pool, l, a):
            for i in range(4):
                pool.wait_ge(y_out[i], 32 * out_base[l + 1][i])
            for t in range((T - a) // P):
                for k in range(2):
                    pool.indirect_dma_start(out=got[k][:, t, :], out_offset=None, in_=dram["results"],
                                            in_offset=bass.IndirectOffsetOnAxis(ap=row_int[:, k, t:t + 1], axis=0))\
                        .then_inc(got_in[t], 16)

        F0 = 8192
        cq = part(feat_t, F0, 3, TC)
        ckv = part(feat_t, F0 + 768, 2, T)
        kpe = part(feat_t, F0 + 1792, T)
        qn = part(feat_t, F0 + 2304, MH, TC)
        qpe = part(feat_t, F0 + 4352, 4, TC)
        rope = part(feat_t, F0 + 5376, 2, TC)
        pmax = part(feat_t, F0 + 5888, 16)
        psum_ = part(feat_t, F0 + 5904, 16)
        kn = yT
        val = part(xT_t, 0, NT, D)
        prob = part(feat_t, F0 + 6144, 2, T)
        rope_tmp = part(feat_t, F0 + 7168, T)

        def mla_pe(pe):
            w = slot(turn["mla_in", 0][0], DC, 768)
            pe.wait_ge(*arrived(("mla_in", 0)))
            for j in range(6):
                a = TC if j < 3 else 0
                mm = proj_pe(pe, f"mi{j}", w, DC, j * P, lambda k: xT[:, k, a:T], T - a, P,
                             (lambda k: f"n11.x{k}") if j == 0 else None)
                mm.then_inc(*did("pe", f"mi{j}", *(["used:mla_in0"] if j == 5 else [])))
            b = take(pe, "kswap")
            pe.wait_ge(*seen(pe, "ev:mi5"))
            pe.matmul(b[:, 0:TC], M["swap"], kpe[:, TC:T], start=True, stop=True).then_inc(*did("pe", "kswap"))
            norm_pe(pe, "nq", TC, 3, (hm_t, 0))
            norm_pe(pe, "nkv", T, 2, (hm_t, 1536))
            w = slot(turn["mla_uq", 0][0], 3, 1536)
            pe.wait_ge(*arrived(("mla_uq", 0)))
            for j in range(12):
                mm = proj_pe(pe, f"uq{j}", w, 3, j * P, lambda k: cq[:, k, :], TC, P,
                             (lambda k: f"cq{k}") if j == 0 else None)
                mm.then_inc(*did("pe", f"uq{j}", *(["used:mla_uq0"] if j == 11 else [])))
            for j in range(4):
                b = take(pe, f"qswap{j}")
                pe.wait_ge(*seen(pe, f"ev:uq{8 + j}"))
                pe.matmul(b[:, 0:TC], M["swap"], qpe[:, j, :], start=True, stop=True).then_inc(*did("pe", f"qswap{j}"))
            w = slot(turn["mla_ukv", 0][0], 2, 2048)
            pe.wait_ge(*arrived(("mla_ukv", 0)))
            for j in range(8):
                proj_pe(pe, f"uk{j}", w, 2, j * P, lambda k: ckv[:, k, :], T, P,
                        (lambda k: f"ckv{k}") if j == 0 else None).then_inc(*did("pe", f"uk{j}"))
            for t in range(NT):
                for g in range(2):
                    b = take(pe, f"uv{t}.{g}")
                    for k in range(2):
                        mm = pe.matmul(b[:, :], ckv[:, k, t * P:(t + 1) * P], w[:, k, 1024 + 512 * g:1536 + 512 * g],
                                       start=k == 0, stop=k == 1)
                    mm.then_inc(*did("pe", f"uv{t}.{g}", *(["used:mla_ukv0"] if t == 3 and g == 1 else [])))
            for h in range(MH + 1):
                if h < MH:
                    for qt in range(2):
                        qs = slice(qt * P, (qt + 1) * P)
                        b = take(pe, f"s{h}.{qt}")
                        if h == 0:
                            pe.wait_ge(*seen(pe, "ev:uk7"))
                            pe.wait_ge(*seen(pe, "qpe3"))
                        pe.matmul(b[:, :], qn[:, h, qs], kn[:, h, :], start=True, stop=False)
                        pe.matmul(b[:, :], qpe[half(h % 2), h // 2, qs], kpe[half(h % 2), :], start=False, stop=True)\
                            .then_inc(*did("pe", f"s{h}.{qt}"))
                if h:
                    g = h - 1
                    for kp in range(2):
                        b = take(pe, f"pt{g}.{kp}")
                        for i in range(2):
                            for qt in range(2):
                                if kp == 0 and i == 0:
                                    pe.wait_ge(*seen(pe, f"p{g}.{qt}"))
                                mm = pe.transpose(b[:, (2 * i + qt) * P:(2 * i + qt + 1) * P],
                                                  prob_of(g)[:, qt, (2 * kp + i) * P:(2 * kp + i + 1) * P], M["ident"])
                        mm.then_inc(*did("pe", f"pt{g}.{kp}"))
                    b = take(pe, f"o{g}")
                    for kt_ in range(NT):
                        pe.wait_ge(*seen(pe, f"ev:pt{g}.{kt_ // 2}"))
                        if g == 0 and kt_ == 0:
                            pe.wait_ge(*seen(pe, "ev:uv3.1"))
                        mm = pe.matmul(b[:, 0:TC], val[:, kt_, g * P:(g + 1) * P], prob_T[:, kt_, :],
                                       start=kt_ == 0, stop=kt_ == NT - 1)
                    mm.then_inc(*did("pe", f"o{g}"))

        mix_lo = hm_t[:].rearrange("p (c t) -> p c t", t=T)[:, :, 0:TC]
        prob_T = mix_lo[:, 4:8, :]

        def prob_of(h):
            return prob

        def mla_act(act):
            for j in range(6):
                act.wait_ge(*seen(act, f"mi{j}"))
                dst = cq[:, j, :] if j < 3 else ckv[:, j - 3, :] if j < 5 else kpe[:, :]
                act.activation(dst, bank(f"mi{j}")[:, 0:(TC if j < 3 else T)], ACT.Copy).then_inc(*did("act", f"ev:mi{j}"))
            norm_act(act, "nq", lambda k: cq[:, k, :], TC, 3, (hm_t, 0), ["ev:mi0", "ev:mi1", "ev:mi2"])
            norm_act(act, "nkv", lambda k: ckv[:, k, :], T, 2, (hm_t, 1536), ["ev:mi3", "ev:mi4"])
            for j in range(12):
                act.wait_ge(*seen(act, f"uq{j}"))
                dst = qn[:, j, :] if j < 8 else qpe[:, j - 8, :]
                act.activation(dst, bank(f"uq{j}")[:, 0:TC], ACT.Copy).then_inc(*did("act", f"ev:uq{j}"))
            for t in range(NT):
                for g in range(2):
                    act.wait_ge(*seen(act, f"uv{t}.{g}"))
                    act.activation(val[:, t, 512 * g:512 * g + 512], bank(f"uv{t}.{g}")[:, :], ACT.Copy)\
                        .then_inc(*did("act", f"ev:uv{t}.{g}"))
            for h in range(MH):
                for qt in range(2):
                    i = 2 * h + qt
                    act.wait_ge(*seen(act, f"max{h}.{qt}"))
                    if h:
                        act.wait_ge(*seen(act, f"pt{h - 1}.1"))
                    act.activation(prob[:, qt, :], bank(f"s{h}.{qt}")[:, :], ACT.Exp, bias=pmax[:, i:i + 1],
                                   scale=MLA_SCALE, accum_out=psum_[:, i:i + 1]).then_inc(*did("act", f"ev:s{h}.{qt}"))

        def rope_dve(dve, x, job, key, tmp, at):
            dve.wait_ge(*seen(dve, job))
            dve.tensor_tensor(tmp, bank(job)[:, 0:TC], rope[:, 1, :], ALU.mult).then_inc(*did("dve", "ev:" + job))
            dve.tensor_tensor(x, x, rope[:, 0, :], ALU.mult).then_inc(*did("dve", key + ".c"))
            dve.wait_ge(*seen(dve, key + ".c"))
            dve.tensor_tensor(x, x, tmp, ALU.add).then_inc(*did("dve", key))

        def mla_dve(dve):
            dve.wait_ge(rope_in, 16)
            rope_dve(dve, kpe[:, TC:T], "kswap", "kpe", rope_tmp[:, 0:TC], 0)
            for tag, x, n, chunks, g, at in (("nq", cq, TC, 3, "q_norm", 0), ("nkv", ckv, T, 2, "kv_norm", 1536)):
                norm_dve(dve, tag, lambda k: x[:, k, :], lambda k: x[:, k, :], n, chunks, (hm_t, at))
                for k in range(chunks):
                    dve.wait_ge(*seen(dve, f"{tag}.xr{k}"))
                    dve.tensor_scalar(x[:, k, :], x[:, k, :], V(g, k), None, ALU.mult)\
                        .then_inc(*did("dve", f"{'cq' if tag == 'nq' else 'ckv'}{k}"))
            for j in range(4):
                if j:
                    dve.wait_ge(*seen(dve, f"qpe{j - 1}"))
                rope_dve(dve, qpe[:, j, :], f"qswap{j}", f"qpe{j}", rope_tmp[:, 0:TC], 0)
            for j in range(8):
                dve.wait_ge(*seen(dve, f"uk{j}"))
                dve.tensor_copy(kn[:, j, :], bank(f"uk{j}")[:, :]).then_inc(*did("dve", f"ev:uk{j}"))
            def head_end(h):
                for qt in range(2):
                    i = 2 * h + qt
                    dve.wait_ge(*seen(dve, f"ev:s{h}.{qt}"))
                    dve.reciprocal(psum_[:, i:i + 1], psum_[:, i:i + 1]).then_inc(*did("dve", f"ri{h}.{qt}"))
                    dve.wait_ge(*seen(dve, f"ri{h}.{qt}"))
                    dve.tensor_scalar(prob[:, qt, :], prob[:, qt, :], psum_[:, i:i + 1], None, ALU.mult)\
                        .then_inc(*did("dve", f"p{h}.{qt}"))
                for kp in range(2):
                    dve.wait_ge(*seen(dve, f"pt{h}.{kp}"))
                    if h:
                        dve.wait_ge(*seen(dve, f"o{h - 1}"))
                    dve.tensor_copy(prob_T[:, 2 * kp:2 * kp + 2, :],
                                    bank(f"pt{h}.{kp}")[:, :].rearrange("p (a b) -> p a b", b=TC))\
                        .then_inc(*did("dve", f"ev:pt{h}.{kp}"))
                dve.wait_ge(*seen(dve, f"o{h}"))
                dve.tensor_copy(mix[:, h, TC:T], bank(f"o{h}")[:, 0:TC]).then_inc(*did("dve", f"ev:o{h}"))

            for h in range(MH + 1):
                if h < MH:
                    for qt in range(2):
                        i = 2 * h + qt
                        dve.wait_ge(*seen(dve, f"s{h}.{qt}"))
                        dve.tensor_reduce(pmax[:, i:i + 1], bank(f"s{h}.{qt}")[:, :], AX, ALU.max, negate=True)\
                            .then_inc(*did("dve", f"mx{h}.{qt}"))
                        dve.wait_ge(*seen(dve, f"mx{h}.{qt}"))
                        dve.tensor_scalar(pmax[:, i:i + 1], pmax[:, i:i + 1], MLA_SCALE, None, ALU.mult)\
                            .then_inc(*did("dve", f"max{h}.{qt}"))
                if h:
                    head_end(h - 1)

        def experts_pe(pe, l, a):
            expert_loop(pe, "pe", l, lambda s, it: expert_pe(pe, l, a, s, it, turn["expert", NE * l + s][1]))
            barrier(pe, "pe", f"experts{l}")
            extra_loop(pe, "pe", l, lambda it: extra_pe(pe, l, a, it))
            barrier(pe, "pe", f"extras{l}")
            mixed_pe(pe, l, a)

        def experts_act(act, l, a):
            expert_loop(act, "act", l, lambda s, it: expert_act(act, l, s, it))
            barrier(act, "act")
            extra_loop(act, "act", l, lambda it: extra_act(act, l, it))
            barrier(act, "act")
            mixed_act(act, l, a)

        def experts_dve(dve, l, a):
            expert_loop(dve, "dve", l, lambda s, it: expert_dve(dve, l, a, s, it))
            barrier(dve, "dve")
            extra_loop(dve, "dve", l, lambda it: extra_dve(dve, l, a, it))
            barrier(dve, "dve")
            mixed_dve(dve, l, a)

        @block.tensor
        def _(pe):
            pe.wait_ge(consts_in, 16 * N_CONST)
            pe.wait_ge(*seen(pe, "silu_c"))
            pe.wait_ge(*seen(pe, "sum32"))
            for g in range(ADA_FIRST):
                ada_sum_pe(pe, f"ada{g}", g % 2, 16 * turn["ada", g][1])
                ada_turn_pe(pe, f"ada{g}")
            norm_pe(pe, "n1", T, DC, NORM)
            win_pe(pe, range(3))
            ret_pe(pe)
            barrier(pe, "pe")
            win_pe(pe, range(3, 7))
            lora_pe(pe)
            gate_pe(pe)
            barrier(pe, "pe")
            pair_loop(pe, "pe", pair_pe)
            barrier(pe, "pe")
            post_pe(pe)
            wout_pe(pe, "wout", "wo", 0, "mix3")
            norm_pe(pe, "n20", T, DC, NORM)
            route_pe(pe, 0, 0)
            barrier(pe, "pe")
            experts_pe(pe, 0, 0)
            norm_pe(pe, "n11", T, DC, NORM2)
            mla_pe(pe)
            wout_pe(pe, "mla_o", "mo", TC, f"ev:o{MH - 1}")
            norm_pe(pe, "n21", TC, DC, NORM2)
            route_pe(pe, 1, TC)
            barrier(pe, "pe")
            experts_pe(pe, 1, TC)
            norm_pe(pe, "nf", TC, DC, NORM2)

        @block.scalar
        def _(act):
            act.wait_ge(consts_in, 16 * N_CONST)
            act.wait_ge(*seen(act, "silu0"))
            for i, name in enumerate(("c_ctx", "c")):
                act.activation(silu_c[:, :, i], V(name), ACT.Silu).then_inc(*did("act", *(["silu_c"] if i else [])))
            for g in range(ADA_FIRST):
                ada_act(act, f"ada{g}")
            act.wait_ge(h_in, 16)
            act.wait_ge(*seen(act, "eps"))
            norm_act(act, "n1", lambda k: hm[:, k, :], T, DC, NORM)
            act.wait_ge(*seen(act, "gain0.0"))
            modulate_act(act, "n1", 0, 0, SEGS)
            ret_feat_act(act)
            ret_act(act)
            barrier(act, "act")
            lora_act(act)
            gate_act(act)
            barrier(act, "act")
            pair_loop(act, "act", pair_act)
            barrier(act, "act")
            post_act(act)
            norm_act(act, "n20", lambda k: hT[:, k, :], T, DC, NORM, [f"wo.h{k}" for k in range(DC)])
            modulate_act(act, "n20", 0, 1, SEGS)
            route_act(act, 0, 0)
            barrier(act, "act")
            experts_act(act, 0, 0)
            norm_act(act, "n11", lambda k: hT[:, k, :], T, DC, NORM2, [f"z0.h{k}" for k in range(DC)])
            modulate_act(act, "n11", 1, 0, SEGS)
            mla_act(act)
            norm_act(act, "n21", lambda k: hT[:, k, TC:T], TC, DC, NORM2, [f"mo.h{k}" for k in range(DC)])
            modulate_act(act, "n21", 1, 1, SEGS[1:])
            route_act(act, 1, TC)
            barrier(act, "act")
            experts_act(act, 1, TC)
            norm_act(act, "nf", lambda k: hT[:, k, TC:T], TC, DC, NORM2, [f"z1.h{k}" for k in range(DC)])

        @block.vector
        def _(dve):
            dve.memset(small[:, 0:1], EPS).then_inc(*did("dve"))
            dve.memset(small[:, 1:2], GN_EPS).then_inc(*did("dve", "eps"))
            dve.memset(silu_c[:], 0.0).then_inc(*did("dve", "silu0"))
            dve.wait_ge(consts_in, 16 * N_CONST)
            dve.tensor_tensor(small[:, 24:26], M["eye2"][:, 0:2], M["eye2"][:, 32:34], ALU.add)\
                .then_inc(*did("dve", "sum32"))
            dve.tensor_tensor(small[:, 8:24], V("mu0"), V("mu1"), ALU.add).then_inc(*did("dve", "mu"))
            dve.wait_ge(*seen(dve, "mu"))
            dve.tensor_scalar(small[:, 8:24], small[:, 8:24], -1.0, 1.0, ALU.mult, ALU.add).then_inc(*did("dve", "one_mu"))
            dve.wait_ge(*seen(dve, "one_mu"))
            for g in range(ADA_FIRST):
                ada_dve(dve, f"ada{g}", 4 * g)
            gain_dve(dve, 0, 0, f"ev:ada{ADA_FIRST - 1}t")
            dve.wait_ge(h_in, 16)
            norm_dve(dve, "n1", lambda k: hm[:, k, :], lambda k: xT[:, k, :], T, DC, NORM)
            dve.wait_ge(tables_in, 32)
            ret_dve(dve)
            barrier(dve, "dve")
            shift_dve(dve)
            lora_dve(dve)
            barrier(dve, "dve")
            pair_loop(dve, "dve", pair_dve)
            barrier(dve, "dve")
            for layer, which in ((0, 1), (1, 0), (1, 1)):
                gain_dve(dve, layer, which, f"ev:A{ADA_TURN - 1}t")
            post_dve(dve)
            dve.wait_ge(h_again, 16)
            residual_dve(dve, "wo", 0, 2, 0, hT)
            norm_dve(dve, "n20", lambda k: hT[:, k, :], lambda k: xT[:, k, :], T, DC, NORM)
            dve.wait_ge(router_in, 48)
            route_dve(dve, 0, 0)
            barrier(dve, "dve")
            experts_dve(dve, 0, 0)
            norm_dve(dve, "n11", lambda k: hT[:, k, :], lambda k: xT[:, k, :], T, DC, NORM2)
            mla_dve(dve)
            residual_dve(dve, "mo", 1, 2, TC, hT)
            norm_dve(dve, "n21", lambda k: hT[:, k, TC:T], lambda k: xT[:, k, TC:T], TC, DC, NORM2)
            dve.wait_ge(router_in, 96)
            route_dve(dve, 1, TC)
            barrier(dve, "dve")
            experts_dve(dve, 1, TC)
            norm_dve(dve, "nf", lambda k: hT[:, k, TC:T], lambda k: xT[:, k, 0:TC], TC, DC, NORM2)
            for k in range(DC):
                dve.wait_ge(*seen(dve, f"nf.xr{k}"))
                dve.tensor_scalar(xT[:, k, 0:TC], xT[:, k, 0:TC], V("final_g", k), None, ALU.mult)\
                    .then_inc(*did("dve", f"out{k}"))

        @block.gpsimd
        def _(pool):
            pool.wait_ge(tables_in, 32)
            pool.tensor_copy(level_t[:], part(ring, WORK + 9216, 2 * len(LEVELS) * P)).then_inc(*did("pool", "levels"))
            barrier(pool, "pool")
            barrier(pool, "pool")
            pair_loop(pool, "pool", pair_pool)
            barrier(pool, "pool")
            for l, a in ((0, 0), (1, TC)):
                for _ in range(3):
                    barrier(pool, "pool")
                mixed_pool(pool, l, a)

        @block.sync
        def _(sp):
            sp.dma_start(vec[:], dram["vec"]).then_inc(consts_in, 16)
            sp.dma_start(mask_t[:], dram["masks"]).then_inc(consts_in, 16)
            sp.dma_start(hm_t[:], dram["hT"]).then_inc(h_in, 16)

            def load(key):
                a, i = key
                before = previous[key]
                if before is not None:
                    sp.wait_ge(*seen(sp, f"used:{before[0]}{before[1]}"))
                s, n = turn[key]
                w = next(w for x, j, w, _ in items if (x, j) == key)
                sp.dma_start(ring[:, s * SLOT:s * SLOT + w], dram[a][i]).then_inc(loaded[s], 16)

            def passed(label):
                return phase, 4 * marks.get(("barrier", label), 1)

            def store(block, s):
                for g in range(2):
                    sp.dma_start(dram["results"][block, 512 * g:512 * g + 512], yt[64 * g:64 * g + 64, s, :])\
                        .then_inc(y_out[s], 16)

            for s in range(4):
                sp.sem_inc(y_out[s], 32)
            order = [(a, i) for a, i, _, _ in items]
            for l in range(2):
                start = 0 if l == 0 else order.index(("extra", 15)) + 1
                for key in order[start:order.index(("expert", NE * l))]:
                    if key == ("ada", 2):
                        sp.dma_start(part(ring, WORK + 9216, 2 * len(LEVELS) * P), dram["levels"]).then_inc(tables_in, 16)
                        sp.dma_start(part(ring, WORK + 6144, RH * 768), dram["decay"]).then_inc(tables_in, 16)
                    if key[0] == "ada" and key[1] > ADA_FIRST:
                        continue
                    if key == ("ada", ADA_FIRST):
                        for i in range(2):
                            sp.dma_start(dram["results"][(NE + 8 * i) * CAP:(NE + 8 + 8 * i) * CAP, :],
                                         dram["hT"].rearrange("p (a b) -> (p a) b", b=D)).then_inc(filled, 16)
                        sp.wait_ge(*seen(sp, "used:lora0"))
                        sp.wait_ge(*seen(sp, "used:win60"))
                        with sp.Fori(0, NPAIR) as it:
                            for i in range(ADA_TURN):
                                sp.wait_ge(*seen(sp, *((f"A{i - 2}", it) if i > 1 else
                                                       (f"A{ADA_TURN - 1 - (ADA_TURN - 1 - i) % 2}", it, 1))))
                                sp.dma_start(slot(i % 2, 4096), dram["ada"][bass.ds(it * ADA_TURN + (ADA_FIRST + i), 1)]
                                             .rearrange("o p n -> (o p) n")).then_inc(loaded[i % 2], 16)
                        continue
                    if key == ("wout", 1):
                        sp.wait_ge(*seen(sp, "mix3"))
                        sp.dma_start(part(feat_t, 0, DC * T), dram["hT"]).then_inc(h_again, 16)
                        sp.dma_start(route_w, dram["route_w"][0]).then_inc(router_in, 16)
                        sp.dma_start(route_b[0:1, :], dram["route_b"][0:1]).then_inc(router_in, 16)
                        sp.dma_start(tab, dram["tab"]).then_inc(router_in, 16)
                    if key == ("mla_in", 0):
                        sp.wait_ge(*passed("extras0"))
                        sp.dma_start(rope, dram["rope"]).then_inc(rope_in, 16)
                    load(key)
                if l:
                    sp.wait_ge(*seen(sp, "ev:o7"))
                    sp.wait_ge(*seen(sp, "mo.7"))
                    sp.dma_start(route_w, dram["route_w"][1]).then_inc(router_in, 16)
                    sp.dma_start(route_b[0:1, :], dram["route_b"][1:2]).then_inc(router_in, 16)
                    sp.dma_start(tab, dram["tab"]).then_inc(router_in, 16)
                else:
                    sp.wait_ge(filled, 32)
                for s in range(4):
                    if l == 0 and s == 2:
                        sp.wait_ge(*seen(sp, "n20.x7"))
                    load(("expert", NE * l + s))
                with sp.Fori(0, NE // 4 - 1) as it:
                    for s in range(4):
                        sp.wait_ge(*seen(sp, f"e{l}.{s}.down", it))
                        sp.dma_start(slot(s, SLOT), dram["expert"][bass.ds(it * 4 + (NE * l + 4 + s), 1)]
                                     .rearrange("o p n -> (o p) n")).then_inc(loaded[s], 16)
                        sp.wait_ge(*seen(sp, f"ev:e{l}.{s}.down", it))
                        store(bass.ds(it * (4 * CAP) + s * CAP, CAP), s)
                for s in range(4):
                    sp.wait_ge(*seen(sp, f"ev:e{l}.{s}.down"))
                    store(slice((NE - 4 + s) * CAP, (NE - 3 + s) * CAP), s)
                n = sp.value_load(n_extra[0:1, :], min_val=0, max_val=16)
                with sp.Fori(0, n_extras[l] // 2) as it:
                    with sp.If(n > it * 2):
                        for s in range(2):
                            e = sp.value_load(extra_of[0:1, bass.ds(it * 2 + s, 1)], min_val=0, max_val=NE - 1)
                            sp.wait_ge(*seen(sp, f"x{l}.{s}.down", it, 1))
                            sp.dma_start(slot(s, SLOT), dram["expert"][bass.ds(e + NE * l, 1)]
                                         .rearrange("o p n -> (o p) n")).then_inc(loaded[s], 16)
                        for s in range(2):
                            sp.wait_ge(*seen(sp, f"ev:x{l}.{s}.down", it))
                            store(bass.ds(it * (2 * CAP) + (NE + s) * CAP, CAP), s)
                    with sp.Else():
                        for s in range(2):
                            sp.sem_inc(loaded[s], 16)
                            sp.sem_inc(y_out[s], 32)
                for s in range(4):
                    sp.wait_ge(y_out[s], 32 * out_base[l + 1][s])
            for k in range(DC):
                sp.wait_ge(*seen(sp, f"out{k}"))
                sp.dma_start(out[:, k, :], xT[:, k, 0:TC]).then_inc(stored, 16)
            sp.wait_ge(stored, 16 * DC)

        for i in range(ADA_TURN):
            L.new[f"used:ada{ADA_FIRST + ADA_TURN * (NPAIR - 1) + i}"] = L.new[f"A{i}"]
        for i in range(ADA_FIRST):
            L.new[f"used:ada{i}"] = L.new[f"ada{i}"]
        for l in range(2):
            for s in range(4):
                L.new[f"used:expert{NE * l + NE - 4 + s}"] = L.new[f"e{l}.{s}.down"]
            for s in range(2):
                L.new[f"used:extra{16 * l + n_extras[l] - 2 + s}"] = L.new[f"x{l}.{s}.down"]
    return L.new


N_CONST = 2


def tables():
    import numpy as np

    i = np.arange(P)
    p, c = i[:, None], i[None, :]
    swap = ((p // 32 == c // 32) & ((p - c) % 32 == 16)).astype(np.float32)
    masks = dict(ident=p == c, ones=np.ones((P, P)), half_ones=p // 64 == c // 64, swap=swap, lt=p < c, le=p <= c,
                 gt=p > c, ge=p >= c, eye2=p % 64 == c % 64)
    masks = np.concatenate([np.asarray(masks[n], np.float32) for n in MASKS], 1)
    low = [((p // (2 * n) == c // (2 * n)) & (p // n % 2 == 1) & (c // n % 2 == 0)) for n in LEVELS]
    levels = np.concatenate([np.concatenate(low, 1), np.concatenate([m.T for m in low], 1)], 1).astype(np.float32)
    decay = np.zeros((P, RH, 768), np.float64)
    u, w = np.arange(-128, 256), np.arange(128, 512)
    for h in range(RH):
        lg = math.log1p(-2.0 ** (-5 - h))
        decay[:, h, :384] = np.exp(lg * np.abs(u[None] - p))
        decay[:, h, 384:] = np.exp(lg * (w[None] - p)) + np.exp(lg * (512 - w[None] + p))
    t = np.arange(TC)
    freq = (10000.0 ** (-np.arange(16, dtype=np.float32) / 16)).astype(np.float32)
    row, col = (t // 64).astype(np.float32)[None] * freq[:, None], (t % 64).astype(np.float32)[None] * freq[:, None]
    cos = np.concatenate([np.cos(row)] * 2 + [np.cos(col)] * 2, 0)
    sin = np.concatenate([-np.sin(row), np.sin(row), -np.sin(col), np.sin(col)], 0)
    rope = np.stack([np.tile(cos, (2, 1)), np.tile(sin, (2, 1))], 1).astype(np.float32)
    tab = np.concatenate([np.arange(EPG, 0, -1), CAP * np.arange(NE), CAP * (1 + np.arange(8)), np.arange(16),
                          np.arange(2 * CAP)]).astype(np.float32)
    tab = np.tile(tab[None], (P, 1))
    return dict(masks=masks, levels=levels, decay=decay.astype(np.float32).reshape(P, -1), rope=rope, tab=tab)


def laid_out(x, c, ctx, c_ctx, ada_w, ada_b, norm1_g, norm2_g, final_g, ev_w_in, ev_shift_mu, rwkv_w0, rwkv_w2,
             rwkv_a0, rwkv_a2, rwkv_g2, rwkv_k_k, rwkv_k_a, rwkv_r_k, rwkv_lnx_w, rwkv_lnx_b, ev_w_out, mla_w_in,
             mla_q_norm_g, mla_w_uq, mla_kv_norm_g, mla_w_ukv, mla_w_o, moe_w_grp, moe_b_grp, moe_w_exp, moe_b_exp,
             moe_w_gate, moe_w_up, moe_w_down):
    import numpy as np

    def cols(v, n):
        v = np.reshape(v, -1)
        return np.concatenate([v, np.zeros(n * P - v.size, v.dtype)]).reshape(n, P).T

    def slabs(w, width):
        k, n = w.shape
        return w.reshape(k // P, P, n // width, width).transpose(2, 1, 0, 3).reshape(n // width, P, -1)

    vals = dict(c=c, c_ctx=c_ctx, norm1_g0=norm1_g[0], norm1_g1=norm1_g[1], norm2_g0=norm2_g[0], norm2_g1=norm2_g[1],
                final_g=final_g, ada_b=ada_b.reshape(-1), mu0=ev_shift_mu[0, 0], mu1=ev_shift_mu[0, 1],
                w0_0=rwkv_w0[0, 0], w0_1=rwkv_w0[0, 1], a0_0=rwkv_a0[0, 0], a0_1=rwkv_a0[0, 1], k_k=rwkv_k_k,
                k_a=rwkv_k_a, r_k=rwkv_r_k, lnx_w=rwkv_lnx_w, lnx_b=rwkv_lnx_b, q_norm=mla_q_norm_g,
                kv_norm=mla_kv_norm_g)
    vec = np.concatenate([cols(vals[n], w) for n, (_, w) in VEC.items()], 1)
    hT = np.concatenate([ctx[0], x[0]], 0).T.reshape(DC, P, T).transpose(1, 0, 2).reshape(P, -1)
    g2 = np.concatenate([rwkv_g2[0], np.zeros((96, 512), rwkv_g2.dtype)], 0)
    lora = np.concatenate([rwkv_w2[0].reshape(P, 512), rwkv_a2[0].reshape(P, 512), g2[:P], g2[P:]], 1)[None]
    uq = mla_w_uq[0].reshape(-1, MH, 192)
    uq = np.concatenate([uq[:, :, :128].reshape(-1, 1024), uq[:, :, 128:].reshape(-1, 512)], 1)
    ukv = mla_w_ukv[0].reshape(-1, MH, 256)
    ukv = np.concatenate([ukv[:, :, :128].reshape(-1, 1024), ukv[:, :, 128:].reshape(-1, 1024)], 1)
    win = ev_w_in[0]
    mla_in = np.concatenate([mla_w_in[0], mla_w_in[0][:, 640:]], 1)
    e = 2 * NE

    def rows(w):
        w = w.reshape(e, w.shape[2] // P, P, w.shape[3])
        return w.transpose(0, 2, 1, 3).reshape(e, P, -1)

    expert = np.concatenate([rows(moe_w_gate), rows(moe_w_up), rows(moe_w_down)], 2)
    route_w = np.concatenate([moe_w_grp, moe_w_exp], 2).reshape(2, DC, P, NR).transpose(0, 2, 1, 3)
    return dict(vec=vec, hT=hT, ada=np.concatenate([slabs(ada_w[0], 512), slabs(ada_w[1], 512)], 0),
                win=slabs(win[:, :3072], 512), win6=slabs(win[:, 3072:], 416), lora=lora, wout=slabs(ev_w_out[0], 512),
                expert=expert, mla_in=slabs(mla_in, 768), mla_uq=slabs(uq, 1536), mla_ukv=slabs(ukv, 2048),
                mla_o=slabs(mla_w_o[0], 512), route_w=route_w,
                route_b=np.concatenate([moe_b_grp, moe_b_exp], 1), **tables())


def kernel(**inputs):
    import numpy as np
    import concourse.bacc as bacc
    from concourse.bass_utils import run_bass_kernel_spmd as run

    arrays = {n: np.ascontiguousarray(a) for n, a in laid_out(**{k: np.asarray(v) for k, v in inputs.items()}).items()}
    marks = {}
    for _ in range(2):
        nc = bacc.Bacc("TRN2", target_bir_lowering=False, num_devices=1)
        dram = {n: nc.dram_tensor("in_" + n, a.shape, mybir.dt.from_np(a.dtype), kind="ExternalInput").ap()
                for n, a in arrays.items()}
        dram["results"] = nc.dram_tensor("results", ((NE + 16) * CAP, D), F32, kind="Internal").ap()
        out = nc.dram_tensor("out", (P, DC, TC), F32, kind="ExternalOutput").ap()
        marks = build(nc, dram, out, None, marks)
    r = run(nc, [{"in_" + n: a for n, a in arrays.items()}], core_ids=[0])
    o = r.results[0]["out"]
    return np.ascontiguousarray(o.transpose(2, 1, 0).reshape(1, TC, D))
```

```python
from contextlib import ExitStack
import math

import concourse.bass as bass
from concourse import mybir

F32 = mybir.dt.float32
U8 = mybir.dt.uint8
ALU = mybir.AluOpType
ACT = mybir.ActivationFunctionType
AX = mybir.AxisListType.X

P = 128
D = 1024
DC = D // P
TC = 256
T = 2 * TC
NT = T // P
EPS = 1e-6
RH = 4
NPAIR = 4
GN_EPS = 64e-5
MH = 8
NE, NG, EPG = 32, 4, 8
NR = NG + NE
CAP = 64
MLA_SCALE = (128 + 64) ** -0.5
LOG_DECAY = -math.exp(-0.5)

VEC, NV = {}, 0
for _name, _w in (("c", 8), ("c_ctx", 8), ("norm1_g0", 8), ("norm1_g1", 8), ("norm2_g0", 8), ("norm2_g1", 8),
                  ("final_g", 8), ("ada_b", 96), ("mu0", 16), ("mu1", 16), ("w0_0", 4),
                  ("w0_1", 4), ("a0_0", 4), ("a0_1", 4), ("k_k", 4), ("k_a", 4), ("r_k", 4), ("lnx_w", 4),
                  ("lnx_b", 4), ("q_norm", 3), ("kv_norm", 2)):
    VEC[_name] = (NV, _w)
    NV += _w
ADA_FIRST = 4
ADA_TURN = 5
MASKS = ("ident", "ones", "half_ones", "swap", "lt", "le", "gt", "ge", "eye2")
SLOT = 6144
LEVELS = (1, 2, 4, 8, 16, 32, 64)
ORDER = ((0, 1, 2, 3), (1, 0, 3, 2))


EXTRA_ITEMS = (18, 10)


def stream_items():
    first = [("ada", n, 4096) for n in range(ADA_FIRST)] + [("win", n, 4096) for n in range(6)]
    first += [("win6", 0, 8 * 416), ("lora", 0, 2048)]
    items = [(a, i, w, n % 2) for n, (a, i, w) in enumerate(first)]
    items += [("ada", ADA_FIRST + ADA_TURN * t + i, 4096, i % 2) for t in range(NPAIR) for i in range(ADA_TURN)]
    items += [("wout", n, 4096, n % 2) for n in range(2)]
    items += [("expert", e, SLOT, e % 4) for e in range(NE)] + [("extra", x, SLOT, x % 2) for x in range(EXTRA_ITEMS[0])]
    items += [("mla_in", 0, SLOT, 2), ("mla_uq", 0, 4608, 3), ("mla_ukv", 0, 4096, 0)]
    items += [("mla_o", 0, 4096, 2), ("mla_o", 1, 4096, 3)]
    items += [("expert", NE + e, SLOT, e % 4) for e in range(NE)]
    items += [("extra", EXTRA_ITEMS[0] + x, SLOT, x % 2) for x in range(EXTRA_ITEMS[1])]
    return items


def named(prefix, key):
    return f"ev:{prefix}{key[3:]}" if key.startswith("ev:") else prefix + key


class Layout:

    def __init__(self, sems, spare, marks):
        self.spare = spare
        self.sems, self.marks, self.new = sems, marks, {}
        self.count = {e: 0 for e in sems}
        self.loop = {e: None for e in sems}
        self.rotation, self.user = 0, {}
        self.waited, self.pending = {}, {}

    def did(self, engine, *keys):
        self.count[engine] += 1
        for key in keys:
            assert key not in self.new, key
            self.new[key] = (engine, self.loop[engine], self.count[engine])
        return self.sems[engine], 1

    def seen(self, eng, key, it=None, back=0):
        if not self.marks:
            return self.sems["pe"], 1
        engine, loop, n = self.marks[key]
        waiter, kind = str(eng.engine), None
        if loop is not None:
            base, per, times = self.marks["loop", engine, loop]
            if it is None:
                n += base + (times - 1) * per
            else:
                n, kind = n + base - back * per, loop
                assert n > 0, ("a wait below one", key, n, per)
        high = self.waited.get((waiter, engine, kind), 0)
        if kind is None:
            return self.sems[engine], n
        if high < n and self.pending.get(waiter) == engine:
            eng.sem_inc(self.spare, 1)
        self.pending[waiter] = engine
        self.waited[waiter, engine, kind] = n = max(n, high)
        return self.sems[engine], it * per + n

    def enter(self, engine, loop):
        self.loop[engine], base, self.count[engine] = loop, self.count[engine], 0
        self.waited = {}
        return base

    def leave(self, engine, base, times):
        loop, per = self.loop[engine], self.count[engine]
        self.new["loop", engine, loop] = (base, per, times)
        self.loop[engine], self.count[engine] = None, base + times * per
        self.waited = {}

    def bank(self, job):
        b, loop = self.rotation, self.loop["pe"]
        self.rotation = (b + 1) % 8
        before, back = self.user.get(b), 0
        if before is None and loop is not None:
            before, back = self.marks.get(("last", loop, b)), 1
        self.user[b] = job
        self.new["bank", job] = b
        if loop is not None:
            self.new["last", loop, b] = job
        return b, before, back

    def empty(self):
        self.rotation, self.user = 0, {}


def build(nc, dram, out, marks):
    items = stream_items()
    ctx = ExitStack()
    with ctx:
        def sb(name, shape, dt=F32):
            return ctx.enter_context(nc.sbuf_tensor(name, shape, dt))

        def sem(name):
            return ctx.enter_context(nc.semaphore(name))

        ring = sb("ring", [P, 4 * SLOT])
        xT_t = sb("xT", [P, DC * T])
        hm_t = sb("h_or_mix", [P, DC * T])
        feat_t = sb("features", [P, 8 * NPAIR * T])
        vec = sb("vec", [P, NV])
        mask_t = sb("masks", [P, len(MASKS) * P])
        level_t = sb("level_masks", [P, 2 * len(LEVELS) * P], U8)
        silu_c = sb("silu_c", [P, DC, 32])
        mods = sb("mods", [P, 2, 48, 2])
        gains = sb("gains", [P, 4, DC, 2])
        small = sb("small", [P, 26])
        row_int_t = sb("row_int", [P, 2, NT], mybir.dt.uint32)
        extra_of_t = sb("extra_of", [P, 19], mybir.dt.int32)
        gate_in = sb("gate_in", [P, 2, T])

        psum = [ctx.enter_context(nc.psum_tensor(f"bank{b}", [P, 512], F32)) for b in range(8)]

        sems = {e: sem(f"{e}_done") for e in ("pe", "act", "dve", "pool")}
        loaded = [sem(f"slot{s}_loaded") for s in range(4)]
        consts_in, tables_in, h_in, h_again = sem("consts_in"), sem("tables_in"), sem("h_in"), sem("h_again")
        router_in, rope_in = sem("router_in"), sem("rope_in")
        y_out = [sem(f"results_from_yt{i}") for i in range(4)]
        filled = sem("extra_blocks_filled")
        got_in = [sem(f"results_of_tile{t}") for t in range(NT)]
        stored, phase = sem("stored"), sem("phase")
        waited = sem("waited")
        L = Layout(sems, waited, marks)
        did, seen = L.did, L.seen
        block = ctx.enter_context(nc.Block())

        def V(name, j=None):
            a, w = VEC[name]
            return vec[:, a:a + w] if j is None else vec[:, a + j:a + j + 1]

        M = {n: mask_t[:, i * P:(i + 1) * P] for i, n in enumerate(MASKS)}
        level = level_t[:].rearrange("p (d n c) -> p d n c", d=2, c=P)
        xT = xT_t[:].rearrange("p (c t) -> p c t", t=T)
        hm = hm_t[:].rearrange("p (c t) -> p c t", t=T)
        mix = hm

        def part(t, off, *shape):
            n = math.prod(shape)
            v = t[:, off:off + n]
            if len(shape) == 2:
                v = v.rearrange("p (a b) -> p a b", b=shape[1])
            if len(shape) == 3:
                v = v.rearrange("p (a b c) -> p a b c", b=shape[1], c=shape[2])
            return v

        def slot(s, *shape):
            return part(ring, s * SLOT, *shape)

        r_t, kr_t, kk_t, v_t, a_t0, a_t1, lw_t0, lw_t1 = (part(feat_t, i * 2048, NPAIR, T) for i in range(8))
        a_t, lw_t = (a_t0, a_t1), (lw_t0, lw_t1)
        hT = part(feat_t, 0, DC, T)
        WORK = 2 * SLOT

        turn, previous, last_in = {}, {}, {}
        uses = [0] * 4
        for a, i, w, s in items:
            uses[s] += 1
            turn[a, i] = (s, uses[s])
            previous[a, i] = last_in.get(s)
            last_in[s] = (a, i)

        def arrived(key):
            s, n = turn[key]
            return loaded[s], 16 * n

        def take(pe, job, it=None):
            b, before, back = L.bank(job)
            if before is not None:
                pe.wait_ge(*seen(pe, "ev:" + before, it, back))
            return psum[b]

        def bank(job):
            return psum[marks.get(("bank", job), 0)]

        barriers = {"pe": 0, "act": 0, "dve": 0, "pool": 0}

        def barrier(eng, name, label=None):
            barriers[name] += 1
            if label:
                L.new["barrier", label] = barriers[name]
            eng.drain().then_inc(phase, 1)
            eng.wait_ge(phase, 4 * barriers[name])
            if name == "pe":
                L.empty()

        SEGS = ((0, TC), (TC, T))

        def norm_bufs(at):
            return part(at[0], at[1], 2, T), part(at[0], at[1] + 2 * T, T)

        def norm_pe(pe, tag, n, chunks, at):
            sq, _ = norm_bufs(at)
            b = take(pe, tag)
            for k in range(chunks):
                pe.wait_ge(*seen(pe, f"{tag}.sq{k}"))
                pe.matmul(b[:, 0:n], M["ones"], sq[:, k % 2, 0:n], start=k == 0, stop=k == chunks - 1)\
                    .then_inc(*did("pe", f"{tag}.sum{k}"))

        def norm_act(act, tag, src, n, chunks, at, ready=()):
            sq, rt = norm_bufs(at)
            for k in range(chunks):
                for key in ready[k:k + 1]:
                    act.wait_ge(*seen(act, key))
                if k >= 2:
                    act.wait_ge(*seen(act, f"{tag}.sum{k - 2}"))
                act.activation(sq[:, k % 2, 0:n], src(k), ACT.Square).then_inc(*did("act", f"{tag}.sq{k}"))
            act.wait_ge(*seen(act, f"{tag}.sum{chunks - 1}"))
            act.activation(rt[:, 0:n], bank(tag)[:, 0:n], ACT.Sqrt, bias=small[:, 0:1], scale=1.0 / (chunks * P))\
                .then_inc(*did("act", "ev:" + tag))

        def norm_dve(dve, tag, src, dst, n, chunks, at):
            _, rt = norm_bufs(at)
            dve.wait_ge(*seen(dve, "ev:" + tag))
            dve.reciprocal(rt[:, 0:n], rt[:, 0:n]).then_inc(*did("dve", tag + ".inv"))
            dve.wait_ge(*seen(dve, tag + ".inv"))
            for k in range(chunks):
                dve.tensor_tensor(dst(k), src(k), rt[:, 0:n], ALU.mult).then_inc(*did("dve", f"{tag}.xr{k}"))

        def modulate_act(act, tag, layer, which, segs):
            for k in range(BY_ACT):
                act.wait_ge(*seen(act, f"{tag}.xr{k}"))
                for i, (a, b) in enumerate(segs):
                    seg = a // TC
                    act.activation(xT[:, k, a:b], xT[:, k, a:b], ACT.Identity,
                                   scale=gains[:, 2 * layer + which, k, seg:seg + 1],
                                   bias=mods[:, layer, 24 * which + k, seg:seg + 1])\
                        .then_inc(*did("act", *([f"{tag}.x{k}"] if i == len(segs) - 1 else [])))

        def modulate_dve(dve, tag, layer, which, segs):
            dve.wait_ge(*seen(dve, f"gain{layer}.{which}"))
            for k in range(BY_ACT, DC):
                dve.wait_ge(*seen(dve, f"{tag}.xr{k}"))
                for i, (a, b) in enumerate(segs):
                    seg = a // TC
                    dve.tensor_scalar(xT[:, k, a:b], xT[:, k, a:b], gains[:, 2 * layer + which, k, seg:seg + 1],
                                      mods[:, layer, 24 * which + k, seg:seg + 1], ALU.mult, ALU.add)\
                        .then_inc(*did("dve", *([f"{tag}.x{k}"] if i == len(segs) - 1 else [])))

        BY_ACT = 6
        NORM = (ring, WORK)
        NORM2 = (feat_t, 11660)

        mods_flat = mods[:].rearrange("p l m c -> p (l m) c")
        ada_y = part(ring, 4096, 512)

        def ada_sum_pe(pe, key, s, count, it=None):
            b = take(pe, key, it)
            w = slot(s, DC, 512)
            pe.wait_ge(loaded[s], count)
            for q in range(2):
                for j in range(4):
                    mm = pe.matmul(b[32 * j:32 * j + 32, :], silu_c[:, 4 * q + j, :], w[:, 4 * q + j, :],
                                   start=q == 0, stop=q == 1)
            mm.then_inc(*did("pe", key))

        def ada_turn_pe(pe, key, it=None):
            b = take(pe, key + "t", it)
            pe.wait_ge(*seen(pe, "ev:" + key, it))
            for m in range(4):
                mm = pe.matmul(b[:, 2 * m:2 * m + 2], ada_y[:, m * P:(m + 1) * P], small[:, 24:26], start=True, stop=True)
            mm.then_inc(*did("pe", key + "t"))

        def ada_act(act, key, it=None):
            act.wait_ge(*seen(act, key, it))
            act.activation(ada_y, bank(key)[:, :], ACT.Copy).then_inc(*did("act", "ev:" + key))

        def ada_dve(dve, key, at, it=None):
            dve.wait_ge(*seen(dve, key + "t", it))
            cols = slice(at, at + 4) if it is None else bass.ds(it * (4 * ADA_TURN) + at, 4)
            bias = V("ada_b")[:, cols].unsqueeze(2).broadcast_to([P, 4, 2])
            dve.tensor_tensor(mods_flat[:, cols, :], bank(key + "t")[:, 0:8].rearrange("p (a b) -> p a b", b=2), bias,
                              ALU.add).then_inc(*did("dve", f"ev:{key}t"))

        def gain_dve(dve, layer, which, ready):
            dve.wait_ge(*seen(dve, ready))
            g = V(f"norm{which + 1}_g{layer}").unsqueeze(2).broadcast_to([P, DC, 2])
            dve.scalar_tensor_tensor(gains[:, 2 * layer + which], mods[:, layer, 24 * which + 8:24 * which + 16, :],
                                     1.0, g, ALU.add, ALU.mult).then_inc(*did("dve", f"gain{layer}.{which}"))

        def ada_loop_pe(pe, i, it):
            s, n = turn["ada", ADA_FIRST + i]
            ada_sum_pe(pe, f"A{i}", s, it * (16 * len(range(s, ADA_TURN, 2))) + 16 * n, it)

        def ada_loop_dve(dve, i, it):
            ada_dve(dve, f"A{i}", 4 * (ADA_FIRST + i), it)

        q_t = part(ring, WORK, 2, T)
        k_t = part(ring, WORK + 1024, 2, T)
        vtok = part(ring, WORK + 2048, NT, 512)
        g_t = part(ring, WORK + 4096, RH, T)
        decay = part(ring, WORK + 6144, RH, 768)
        scores = part(ring, WORK + 9216, NT, T)
        rtmp = part(ring, WORK + 11264, 2, T)

        def proj_pe(pe, job, w, k_n, m0, rhs, n, m=P, ready=None):
            b = take(pe, job)
            for k in range(k_n):
                if ready is not None:
                    pe.wait_ge(*seen(pe, ready(k)))
                mm = pe.matmul(b[0:m, 0:n], w[:, k, m0:m0 + m], rhs(k), start=k == 0, stop=k == k_n - 1)
            return mm

        def win_pe(pe, g, j):
            key = ("win", g) if g < 6 else ("win6", 0)
            if j == 0:
                pe.wait_ge(*arrived(key))
            w = slot(turn[key][0], DC, 512 if g < 6 else 416)
            last = [f"used:{key[0]}{key[1]}"] if j == 3 else []
            m = P if g < 6 or j < 3 else 32
            if g == 1:
                b = take(pe, f"win1.{j}")
                for k in range(DC):
                    mm = pe.matmul(b[:, :], xT[:, k, j * P:(j + 1) * P], w[:, k, :], start=k == 0, stop=k == DC - 1)
            else:
                mm = proj_pe(pe, f"win{g}.{j}", w, DC, j * P, lambda k: xT[:, k, :], T, m,
                             (lambda k: f"n1.x{k}") if g == 0 and j == 0 else None)
            mm.then_inc(*did("pe", f"win{g}.{j}", *last))

        def ret_feat_act(act):
            act.wait_ge(*seen(act, "n1.sum7"))
            for j in range(4):
                act.wait_ge(*seen(act, f"win0.{j}"))
                dst, c = ((q_t, 64 ** -0.5) if j < 2 else (k_t, 1.0))
                act.activation(dst[:, j % 2, :], bank(f"win0.{j}")[:, :], ACT.Copy, scale=c)\
                    .then_inc(*did("act", f"ev:win0.{j}"))
            for j in range(4):
                act.wait_ge(*seen(act, f"win1.{j}"))
                act.activation(vtok[:, j, :], bank(f"win1.{j}")[:, :], ACT.Copy).then_inc(*did("act", f"ev:win1.{j}"))
            for j in range(4):
                act.wait_ge(*seen(act, f"win2.{j}"))
                act.activation(g_t[:, j, :], bank(f"win2.{j}")[:, :], ACT.Silu).then_inc(*did("act", f"ev:win2.{j}"))

        def ret_pe(pe):
            for h in range(RH):
                half = slice(64 * (h % 2), 64 * (h % 2) + 64)
                for J in range(NT):
                    i0 = 0 if J < 2 else TC
                    b = take(pe, f"sc{h}.{J}")
                    if h == 0 and J == 0:
                        pe.wait_ge(*seen(pe, "ev:win0.3"))
                    pe.matmul(b[:, i0:T], k_t[half, h // 2, J * P:(J + 1) * P], q_t[half, h // 2, i0:T],
                              start=True, stop=True).then_inc(*did("pe", f"sc{h}.{J}"))
                win_pe(pe, 3, h)
                b = take(pe, f"ro{h}")
                for J in range(NT):
                    i0 = 0 if J < 2 else TC
                    pe.wait_ge(*seen(pe, f"ev:sc{h}.{J}"))
                    if h == 0 and J == 0:
                        pe.wait_ge(*seen(pe, "ev:win1.3"))
                    mm = pe.matmul(b[:, i0:T], vtok[:, J, h * P:(h + 1) * P], scores[:, J, i0:T],
                                   start=J == 0, stop=J == NT - 1)
                mm.then_inc(*did("pe", f"ro{h}"))
                win_pe(pe, 4, h)
                b = take(pe, f"rs{h}")
                pe.wait_ge(*seen(pe, f"rsq{h}"))
                pe.matmul(b[:, :], M["ones"], rtmp[:, 0, :], start=True, stop=True).then_inc(*did("pe", f"rs{h}"))

        def ret_act(act):
            for h in range(RH):
                act.wait_ge(*seen(act, f"ro{h}"))
                if h:
                    act.wait_ge(*seen(act, f"rs{h - 1}"))
                act.activation(rtmp[:, 0, :], bank(f"ro{h}")[:, :], ACT.Square).then_inc(*did("act", f"rsq{h}"))
                act.activation(mix[:, h, :], bank(f"ro{h}")[:, :], ACT.Copy).then_inc(*did("act", f"ev:ro{h}"))
                act.wait_ge(*seen(act, f"rs{h}"))
                if h:
                    act.wait_ge(*seen(act, f"rmul{h - 1}"))
                act.activation(rtmp[:, 1, :], bank(f"rs{h}")[:, :], ACT.Sqrt, bias=small[:, 0:1], scale=1.0 / P)\
                    .then_inc(*did("act", f"ev:rs{h}"))

        def ret_dve(dve):
            dve.wait_ge(*seen(dve, "levels"))
            for h in range(RH):
                for J in range(NT):
                    dve.wait_ge(*seen(dve, f"sc{h}.{J}"))
                    if h:
                        dve.wait_ge(*seen(dve, f"ro{h - 1}"))
                    u = 128 - P * (J % 2)
                    b = bank(f"sc{h}.{J}")
                    if J < 2:
                        dve.tensor_tensor(scores[:, J, 0:TC], b[:, 0:TC], decay[:, h, u:u + TC], ALU.mult)\
                            .then_inc(*did("dve"))
                        table = decay[:, h, 384 + u:384 + u + TC]
                    else:
                        table = decay[:, h, u:u + TC]
                    dve.tensor_tensor(scores[:, J, TC:T], b[:, TC:T], table, ALU.mult)\
                        .then_inc(*did("dve", f"ev:sc{h}.{J}"))
                shift_dve(dve, 3, h)
                shift_dve(dve, 4, h)
                dve.wait_ge(*seen(dve, f"ev:rs{h}"))
                dve.reciprocal(rtmp[:, 1, :], rtmp[:, 1, :]).then_inc(*did("dve", f"rinv{h}"))
                dve.wait_ge(*seen(dve, f"rinv{h}"))
                dve.tensor_tensor(g_t[:, h, :], g_t[:, h, :], rtmp[:, 1, :], ALU.mult).then_inc(*did("dve", f"rmul{h}"))
                dve.wait_ge(*seen(dve, f"rmul{h}"))
                dve.tensor_tensor(mix[:, h, :], mix[:, h, :], g_t[:, h, :], ALU.mult).then_inc(*did("dve", f"ret{h}"))

        lora_tmp = part(ring, WORK, 2, T)

        def shift_dve(dve, g, j):
            one = small[:, 8:24]
            m = P if g < 6 or j < 3 else 32
            c = 4 * (g - 3) + j
            dst = (r_t, kr_t, v_t)[g - 3][:, j, :] if g < 6 else \
                (lora_tmp[:, 0, :], lora_tmp[:, 1, :], gate_in[:, 0, :], gate_in[:, 1, :])[j]
            d3 = dst[0:m].rearrange("p (s t) -> p s t", s=2)
            b3 = bank(f"win{g}.{j}")[0:m, :].rearrange("p (s t) -> p s t", s=2)
            dve.wait_ge(*seen(dve, f"win{g}.{j}"))
            dve.tensor_scalar(d3, b3, one[0:m, c:c + 1], None, ALU.mult).then_inc(*did("dve", f"sh{c}a"))
            dve.wait_ge(*seen(dve, f"sh{c}a"))
            dve.scalar_tensor_tensor(d3[:, :, 1:], b3[:, :, 0:TC - 1], V("mu0", c)[0:m], d3[:, :, 1:],
                                     ALU.mult, ALU.add).then_inc(*did("dve", f"sh{c}b"))
            dve.wait_ge(*seen(dve, f"sh{c}b"))
            dve.scalar_tensor_tensor(d3[:, :, 0:TC - 1], b3[:, :, 1:], V("mu1", c)[0:m], d3[:, :, 0:TC - 1],
                                     ALU.mult, ALU.add).then_inc(*did("dve", f"ev:win{g}.{j}"))

        def lora_pe(pe):
            w = slot(turn["lora", 0][0], 4, 512)
            pe.wait_ge(*arrived(("lora", 0)))
            for d in range(2):
                rows = slice(64 * d, 64 * d + 64)
                for c in range(NPAIR):
                    for what, i in (("lw", 0), ("la", 1)):
                        b = take(pe, f"{what}{d}.{c}")
                        if d == 0 and c == 0:
                            pe.wait_ge(*seen(pe, "tanh" if i == 0 else "ev:win6.1"))
                        pe.matmul(b[:, :], w[rows, i, c * P:(c + 1) * P], lora_tmp[rows, i, :], start=True, stop=True)\
                            .then_inc(*did("pe", f"{what}{d}.{c}"))

        def lora_act(act):
            act.wait_ge(*seen(act, "ev:win6.0"))
            act.activation(lora_tmp[:, 0, :], lora_tmp[:, 0, :], ACT.Tanh).then_inc(*did("act", "tanh"))
            act.wait_ge(*seen(act, "ev:win6.3"))
            act.activation(gate_in[:, 0, :], gate_in[:, 0, :], ACT.Sigmoid).then_inc(*did("act"))
            act.activation(gate_in[0:32, 1, :], gate_in[0:32, 1, :], ACT.Sigmoid).then_inc(*did("act", "gate_in"))
            for d in range(2):
                for c in range(NPAIR):
                    act.wait_ge(*seen(act, f"lw{d}.{c}"))
                    if d == 1 and c == 0:
                        act.wait_ge(*seen(act, f"kk{NPAIR - 1}"))
                    act.activation(lw_t[d][:, c, :], bank(f"lw{d}.{c}")[:, :], ACT.Sigmoid, bias=V(f"w0_{d}", c))\
                        .then_inc(*did("act", f"ev:lw{d}.{c}"))
                    act.wait_ge(*seen(act, f"la{d}.{c}"))
                    act.activation(a_t[d][:, c, :], bank(f"la{d}.{c}")[:, :], ACT.Sigmoid, bias=V(f"a0_{d}", c))\
                        .then_inc(*did("act", f"ev:la{d}.{c}"))

        def kk_pe(pe):
            for c in range(NPAIR):
                b = take(pe, f"kn{c}")
                pe.wait_ge(*seen(pe, f"ksq{c}"))
                pe.matmul(b[:, :], M["half_ones"], lw_t[1][:, c, :], start=True, stop=True).then_inc(*did("pe", f"kn{c}"))

        def kk_act(act):
            for c in range(NPAIR):
                act.wait_ge(*seen(act, f"kk0.{c}"))
                act.activation(lw_t[1][:, c, :], kk_t[:, c, :], ACT.Square).then_inc(*did("act", f"ksq{c}"))
            for c in range(NPAIR):
                act.wait_ge(*seen(act, f"kn{c}"))
                act.activation(a_t[1][:, c, :], bank(f"kn{c}")[:, :], ACT.Sqrt).then_inc(*did("act", f"ev:kn{c}"))

        def kk_scale_dve(dve):
            for c in range(NPAIR):
                dve.tensor_scalar(kk_t[:, c, :], kr_t[:, c, :], V("k_k", c), None, ALU.mult)\
                    .then_inc(*did("dve", f"kk0.{c}"))

        def kk_dve(dve, c):
            dve.wait_ge(*seen(dve, f"ev:kn{c}"))
            root = a_t[1][:, c, :]
            dve.tensor_scalar(root, root, 1e-12, None, ALU.max).then_inc(*did("dve", f"kmax{c}"))
            dve.wait_ge(*seen(dve, f"kmax{c}"))
            dve.reciprocal(root, root).then_inc(*did("dve", f"kinv{c}"))
            dve.wait_ge(*seen(dve, f"kinv{c}"))
            dve.tensor_tensor(kk_t[:, c, :], kk_t[:, c, :], root, ALU.mult).then_inc(*did("dve", f"kk{c}"))

        def gate_pe(pe):
            w = slot(turn["lora", 0][0], 4, 512)
            for c in range(NPAIR):
                b = take(pe, f"gt{c}")
                if c == 0:
                    pe.wait_ge(*seen(pe, "gate_in"))
                pe.matmul(b[:, :], w[:, 2, c * P:(c + 1) * P], gate_in[:, 0, :], start=True, stop=False)
                pe.matmul(b[:, :], w[0:32, 3, c * P:(c + 1) * P], gate_in[0:32, 1, :], start=False, stop=True)\
                    .then_inc(*did("pe", f"gt{c}", *(["used:lora0"] if c == NPAIR - 1 else [])))

        def gate_act(act):
            for c in range(NPAIR):
                act.wait_ge(*seen(act, f"gt{c}"))
                act.activation(mix[:, 4 + c, :], bank(f"gt{c}")[:, :], ACT.Copy).then_inc(*did("act", f"ev:gt{c}"))

        w0 = WORK
        KRs = (part(ring, w0, NT, 2, P), part(ring, SLOT + 4096, NT, 2, P))
        BEs = (part(ring, w0 + 1024, 2, T), part(ring, SLOT + 5120, 2, T))
        AT = part(ring, w0 + 2048, 8, P)
        RE = part(ring, w0 + 3072, 8, P)
        RB = part(ring, w0 + 4096, 8, P)
        BT = part(ring, w0 + 5120, 8, P)
        TI = BT
        TI_T = part(ring, w0 + 6144, 8, P)
        YL = part(ring, w0 + 7168, 8, P)
        WZ = YL
        RHS = part(ring, w0 + 8192, 8, P)
        b_tok = part(ring, w0 + 9216, NT, P)
        e_tok = part(ring, w0 + 9728, NT, P)
        v_pair = part(ring, w0 + 10240, T)
        v_tok = part(ring, w0 + 10752, NT, P)
        GM = part(ring, w0 + 11264, NT, 64)
        FM = part(ring, w0 + 11520, NT, 64)
        SH = part(ring, w0 + 11776, NT, 64)
        edges = tuple(part(ring, w0 + 12032 + 20 * d, 20) for d in range(2))
        mids, rests, edge_exps, step_decays = ([e[:, x:y] for e in edges] for x, y in ((0, 4), (4, 8), (8, 16), (16, 20)))
        Fc, e1, e2, e3, kt, akk, ysum, bsum = (part(xT_t, i * T, T) for i in range(8))
        QM = e1
        UNITS = [(t, h) for h in range(2) for t in range(NT)]

        def settled(eng):
            eng.sem_inc(waited, 1)

        def half(h):
            return slice(64 * h, 64 * h + 64)

        def four(m):
            return m.unsqueeze(1).broadcast_to([P, 4, P])

        def pair_pe(pe, d, it):
            k = lambda s: named(f"{d}.", s)
            sn = lambda s: seen(pe, k(s), it)
            dd = lambda s: did("pe", k(s))
            first, KR, BE, back = ORDER[d][0], KRs[d], BEs[d], 1 - d
            ready = lambda s: seen(pe, f"P{d}.{s}", it, back)
            ada_loop_pe(pe, 3 * d, it)
            if d == 0:
                b = take(pe, k("vt"), it)
                pe.wait_ge(*ready("v_pair"))
                for t in range(NT):
                    mm = pe.transpose(b[:, t * P:(t + 1) * P], v_pair[:, t * P:(t + 1) * P], M["ident"])
                mm.then_inc(*dd("vt"))
            for name, src_key, src in (("kt", "kappa", lambda t: KR[:, t, 0, :]),
                                     ("bt", "beta", lambda t: BE[:, 0, t * P:(t + 1) * P]),
                                     ("et", "eta", lambda t: BE[:, 1, t * P:(t + 1) * P])):
                b = take(pe, k(name), it)
                pe.wait_ge(*ready(src_key))
                for t in range(NT):
                    mm = pe.transpose(b[:, t * P:(t + 1) * P], src(t), M["ident"])
                mm.then_inc(*dd(name))
            beta = lambda t, h: BE[half(h), 0, t * P:(t + 1) * P]
            eta = lambda t, h: BE[half(h), 1, t * P:(t + 1) * P]
            kappa = lambda t, h: KR[half(h), t, 0, :]
            rho = lambda t, h: KR[half(h), t, 1, :]

            def gram(name, lhs, rhs):
                for g in range(2):
                    b = take(pe, k(f"{name}{g}"), it)
                    for u, (t, h) in enumerate(UNITS[4 * g:4 * g + 4]):
                        mm = pe.matmul(b[:, u * P:(u + 1) * P], lhs(t, h), rhs(t, h), start=True, stop=True)
                    mm.then_inc(*dd(f"{name}{g}"))

            gram("BT", eta, kappa)
            gram("AT", beta, kappa)
            ada_turn_pe(pe, f"A{3 * d}", it)
            b = take(pe, k("BV"), it)
            pe.wait_ge(*sn("ev:BT1"))
            pe.wait_ge(*seen(pe, "ev:0.vt", it))
            for u, (t, h) in enumerate(UNITS):
                mm = pe.matmul(b[:, u * 64:(u + 1) * 64], BT[:, u, :], v_tok[:, t, half(h)], start=True, stop=True)
            mm.then_inc(*dd("BV"))
            gram("A", kappa, beta)
            pe.wait_ge(*ready("rho"))
            gram("RE", eta, rho)
            gram("RB", beta, rho)
            for li in range(1, len(LEVELS)):
                for g in range(2):
                    b = take(pe, k(f"Y{li}.{g}"), it)
                    pe.wait_ge(*sn(f"T{li - 1}.{g}"))
                    for u in range(4 * g, 4 * g + 4):
                        mm = pe.matmul(b[:, (u % 4) * P:(u % 4 + 1) * P], AT[:, u, :], TI[:, u, :], start=True, stop=True)
                    mm.then_inc(*dd(f"Y{li}.{g}"))
                for g in range(2):
                    pe.wait_ge(*sn(f"ev:Y{li}.{g}"))
                    pe.wait_ge(*sn(f"TT{li - 1}.{g}"))
                    if li < len(LEVELS) - 1:
                        b = take(pe, k(f"U{li}.{g}"), it)
                        for u in range(4 * g, 4 * g + 4):
                            mm = pe.matmul(b[:, (u % 4) * P:(u % 4 + 1) * P], TI_T[:, u, :], YL[:, u, :],
                                           start=True, stop=True)
                        mm.then_inc(*dd(f"U{li}.{g}"))
                    b = take(pe, k(f"V{li}.{g}"), it)
                    for u in range(4 * g, 4 * g + 4):
                        mm = pe.matmul(b[:, (u % 4) * P:(u % 4 + 1) * P], YL[:, u, :], TI_T[:, u, :], start=True, stop=True)
                    mm.then_inc(*dd(f"V{li}.{g}"))
                if li == 2:
                    ada_loop_pe(pe, 3 * d + 1, it)
                if li == 3:
                    ada_turn_pe(pe, f"A{3 * d + 1}", it)
                if li == 4 and d == 0:
                    ada_loop_pe(pe, 2, it)
                if li == 5 and d == 0:
                    ada_turn_pe(pe, "A2", it)
            for g in range(2):
                b = take(pe, k(f"WZ{g}"), it)
                pe.wait_ge(*sn(f"TT{len(LEVELS) - 1}.{g}"))
                pe.wait_ge(*sn("ev:kt"))
                pe.wait_ge(*sn("ev:BV"))
                for u in range(4 * g, 4 * g + 4):
                    mm = pe.matmul(b[:, (u % 4) * P:(u % 4 + 1) * P], TI_T[:, u, :], RHS[:, u, :], start=True, stop=True)
                mm.then_inc(*dd(f"WZ{g}"))
            b = take(pe, k("GF"), it)
            pe.wait_ge(*sn("ev:WZ1"))
            for i in range(3):
                t = ORDER[d][i]
                for h in range(2):
                    u = 4 * h + t
                    if i:
                        pe.matmul(b[half(h), i * 64:(i + 1) * 64], WZ[:, u, 0:64], b_tok[:, t, half(h)],
                                  start=True, stop=True)
                    f = b[half(h), 256 + i * 64:256 + (i + 1) * 64]
                    pe.matmul(f, e_tok[:, t, half(h)], v_tok[:, t, half(h)], start=True, stop=False)
                    mm = pe.matmul(f, b_tok[:, t, half(h)], WZ[:, u, 64:128], start=False, stop=True)
            mm.then_inc(*dd("GF"))
            b = take(pe, k("Q"), it)
            pe.wait_ge(*sn("ev:RB1"))
            for t, h in UNITS:
                if t != first:
                    mm = pe.matmul(b[half(h), t * P:(t + 1) * P], WZ[:, 4 * h + t, 0:64], RB[:, 4 * h + t, :],
                                   start=True, stop=True)
            mm.then_inc(*dd("Q"))
            for i in (1, 2):
                b = take(pe, k(f"S{i}"), it)
                pe.wait_ge(*sn("ev:GF" if i == 1 else "ev:S1"))
                settled(pe)
                for h in range(2):
                    mm = pe.matmul(b[half(h), 0:64], GM[half(h), i, :], (FM[half(h), 0, :] if i == 1 else SH[half(h), i, :]),
                                   start=True, stop=True)
                mm.then_inc(*dd(f"S{i}"))
            b = take(pe, k("y"), it)
            pe.wait_ge(*sn("ev:Q"))
            pe.wait_ge(*sn("ev:S2"))
            for i in range(NT):
                t = ORDER[d][i]
                state = (None, FM[:, 0, :], SH[:, 2, :], SH[:, 3, :])[i]
                for h in range(2):
                    u, o = 4 * h + t, b[half(h), t * P:(t + 1) * P]
                    pe.matmul(o, v_tok[:, t, half(h)], RE[:, u, :], start=True, stop=False)
                    mm = pe.matmul(o, WZ[:, u, 64:128], RB[:, u, :], start=False, stop=i == 0)
                    if i:
                        mm = pe.matmul(o, state[half(h)], QM[half(h), t * P:(t + 1) * P], start=False, stop=True)
            mm.then_inc(*dd("y"))

        def prep_act(act, d, step, it, prefix):
            sn = lambda x: seen(act, prefix + x, it)
            if step == 0 and d == 0:
                src = v_t[:, 0, :] if it is None else feat_t[:, bass.ds(it * T + (3 * NPAIR * T + T), T)]
                act.activation(v_pair, src, ACT.Copy).then_inc(*did("act", prefix + "v_pair"))
            if step == 0:
                act.wait_ge(*sn("E"))
            if step == 2 and d == 1:
                act.wait_ge(*sn("exp1"))
            dst, src, sign = (((e2, Fc, 1.0), (e3, Fc, -1.0), (e1, e1, 1.0)) if d == 0 else
                              ((e2, e1, -1.0), (e3, e1, 1.0), (e1, Fc, -1.0)))[step]
            act.activation(dst, src, ACT.Exp, scale=sign * LOG_DECAY).then_inc(*did("act", f"{prefix}exp{step}"))
            if step == 2:
                act.activation(edge_exps[d], edges[d][:, 0:8], ACT.Exp, scale=LOG_DECAY).then_inc(*did("act", prefix + "edges"))

        def pair_act(act, d, it):
            k = lambda s: named(f"{d}.", s)
            sn = lambda s: seen(act, k(s), it)
            dd = lambda s: did("act", k(s))
            if d == 0:
                act.wait_ge(*sn("vt"))
                act.activation(v_tok, bank(k("vt"))[:, :].rearrange("p (a b) -> p a b", b=P), ACT.Copy)\
                    .then_inc(*dd("ev:vt"))
            ada_act(act, f"A{3 * d}", it)
            act.wait_ge(*sn("kt"))
            act.activation(RHS[:, :, 0:64].rearrange("p (h t) c -> p h t c", h=2),
                           bank(k("kt"))[:, :].rearrange("p (t h c) -> p h t c", h=2, c=64), ACT.Copy)\
                .then_inc(*dd("ev:kt"))
            for name, dst in (("bt", b_tok), ("et", e_tok)):
                act.wait_ge(*sn(name))
                act.activation(dst, bank(k(name))[:, :].rearrange("p (a b) -> p a b", b=P), ACT.Copy)\
                    .then_inc(*dd("ev:" + name))
            act.wait_ge(*sn("BV"))
            act.activation(RHS[:, :, 64:128], bank(k("BV"))[:, :].rearrange("p (u c) -> p u c", c=64), ACT.Copy)\
                .then_inc(*dd("ev:BV"))
            for li in range(1, len(LEVELS)):
                for g in range(2):
                    act.wait_ge(*sn(f"Y{li}.{g}"))
                    act.activation(YL[:, 4 * g:4 * g + 4, :],
                                   bank(k(f"Y{li}.{g}"))[:, :].rearrange("p (a b) -> p a b", b=P), ACT.Copy)\
                        .then_inc(*dd(f"ev:Y{li}.{g}"))
                if li in (2, 3, 4):
                    prep_act(act, 1 - d, li - 2, it, f"P{1 - d}.")
                if li == 2:
                    ada_act(act, f"A{3 * d + 1}", it)
                if li == 4 and d == 0:
                    ada_act(act, "A2", it)
            for g in range(2):
                act.wait_ge(*sn(f"WZ{g}"))
                act.activation(WZ[:, 4 * g:4 * g + 4, :], bank(k(f"WZ{g}"))[:, :].rearrange("p (a b) -> p a b", b=P),
                               ACT.Copy).then_inc(*dd(f"ev:WZ{g}"))

        def pair_pool(pool, d, it):
            k = lambda s: named(f"{d}.", s)
            pool.wait_ge(*seen(pool, *(("ev:1.WZ1", it, 1) if d == 0 else ("ev:0.WZ1", it))))
            settled(pool)
            for g in range(2):
                pool.tensor_copy(TI_T[:, 4 * g:4 * g + 4, :], four(M["ident"])).then_inc(*did("pool", k(f"TT_id{g}")))
            pool.wait_ge(*seen(pool, k("BV"), it))
            settled(pool)
            for g in range(2):
                pool.tensor_copy(TI[:, 4 * g:4 * g + 4, :], four(M["ident"])).then_inc(*did("pool", k(f"T_id{g}")))

        def prep_dve(dve, d, step, it, prefix):
            sn = lambda x: seen(dve, prefix + x, it)
            dd = lambda *x: did("dve", *[prefix + y for y in x])
            KR, BE, mid, rest = KRs[d], BEs[d], mids[d], rests[d]

            def row(i):
                if it is None:
                    return feat_t[:, i * NPAIR * T:i * NPAIR * T + T]
                return feat_t[:, bass.ds(it * T + (i * NPAIR * T + (1 - d) * T), T)]

            def tiles(x):
                return x.rearrange("p (t c) -> p t c", c=P)

            r, kr, kk, a, lw = row(0), row(1), row(2), row(4 + d), row(6 + d)
            if step == 1:
                for t in range(NT):
                    lw1 = feat_t[:, t * P + (6 + d) * NPAIR * T:(t + 1) * P + (6 + d) * NPAIR * T] if it is None else \
                        feat_t[:, bass.ds(it * T + ((6 + d) * NPAIR * T + (1 - d) * T + t * P), P)]
                    dve.tensor_tensor_scan(Fc[:, t * P:(t + 1) * P], M["ones"], lw1, 0.0,
                                           ALU.mult, ALU.add).then_inc(*dd(f"scan{t}"))
                dve.wait_ge(*sn("scan3"))
                dve.tensor_copy(mid, tiles(Fc)[:, :, 63]).then_inc(*dd("mid"))
                dve.wait_ge(*sn("mid"))
                dve.tensor_tensor(rest, tiles(Fc)[:, :, P - 1], mid, ALU.subtract).then_inc(*dd("rest"))
                dve.wait_ge(*sn("rest"))
                dve.tensor_tensor(tiles(Fc), tiles(Fc), mid.unsqueeze(2).broadcast_to([P, NT, P]), ALU.subtract)\
                    .then_inc(*dd("F"))
                dve.wait_ge(*sn("F"))
                dve.tensor_tensor(e1, Fc, lw, ALU.subtract).then_inc(*dd("E"))
            if step == 2:
                dve.tensor_tensor(akk, a, kk, ALU.mult).then_inc(*dd("akk"))
                ka = V("k_a", 0) if it is None else vec[:, bass.ds(VEC["k_a"][0] + (1 - d) + it, 1)]
                dve.tensor_scalar(kt, a, 1.0, ka, ALU.subtract, ALU.mult).then_inc(*dd("kt1"))
            if step == 3:
                dve.wait_ge(*sn("kt1"))
                dve.scalar_tensor_tensor(kt, kt, 1.0, kr, ALU.add, ALU.mult).then_inc(*dd("kt2"))
            if step == 4:
                dve.wait_ge(*sn("kt2"))
                if d == 0:
                    dve.tensor_tensor(bsum, kt, r, ALU.mult).then_inc(*dd("bsum"))
            if step == 5:
                dve.wait_ge(*sn("exp2"))
                for_kappa, for_beta, for_rho = e1, e3, e2
                dve.tensor_tensor(KR[:, :, 0, :], tiles(kk), tiles(for_kappa), ALU.mult).then_inc(*dd("kappa"))
                dve.scalar_tensor_tensor(BE[:, 0, :], akk, -1.0, for_beta, ALU.mult, ALU.mult).then_inc(*dd("beta"))
                dve.tensor_tensor(BE[:, 1, :], kt, for_beta, ALU.mult).then_inc(*dd("eta"))
                dve.tensor_tensor(KR[:, :, 1, :], tiles(r), tiles(for_rho), ALU.mult).then_inc(*dd("rho"))
                dve.wait_ge(*sn("edges"))
                dmid, drest = edge_exps[d][:, 0:4], edge_exps[d][:, 4:8]
                leave, come = (drest, dmid) if d == 0 else (dmid, drest)
                for i in range(3):
                    x, y = ORDER[d][i], ORDER[d][i + 1]
                    dve.tensor_tensor(step_decays[d][:, i:i + 1], leave[:, x:x + 1], come[:, y:y + 1], ALU.mult)\
                        .then_inc(*dd(f"dc{i}"))

        def pair_dve(dve, d, it):
            k = lambda s: named(f"{d}.", s)
            sn = lambda s: seen(dve, k(s), it)
            dd = lambda *s: did("dve", *[k(x) for x in s])
            KR, step_decay = KRs[d], step_decays[d]
            strict, incl = ("lt", "le") if d == 0 else ("gt", "ge")

            def v3(job):
                return bank(k(job))[:, :].rearrange("p (a b) -> p a b", b=P)

            def masked(name, dst, m, g):
                dve.wait_ge(*sn(f"{name}{g}"))
                dve.tensor_tensor(dst[:, 4 * g:4 * g + 4, :], v3(f"{name}{g}"), four(M[m]), ALU.mult)\
                    .then_inc(*dd(f"ev:{name}{g}"))

            for g in range(2):
                masked("BT", BT, strict, g)
            for g in range(2):
                masked("AT", AT, strict, g)
            for g in range(2):
                gs = slice(4 * g, 4 * g + 4)
                dve.wait_ge(*seen(dve, k(f"TT_id{g}"), it))
                dve.wait_ge(*sn(f"ev:AT{g}"))
                settled(dve)
                dve.copy_predicated(TI_T[:, gs, :], four(level[:, 1 - d, 0, :]), AT[:, gs, :]).then_inc(*dd(f"TT0.{g}"))
                dve.wait_ge(*seen(dve, k(f"T_id{g}"), it))
                dve.wait_ge(*sn(f"A{g}"))
                settled(dve)
                dve.copy_predicated(TI[:, gs, :], four(level[:, d, 0, :]), v3(f"A{g}")).then_inc(*dd(f"T0.{g}", f"ev:A{g}"))
            ada_loop_dve(dve, 3 * d, it)
            for g in range(2):
                masked("RE", RE, incl, g)
            for g in range(2):
                masked("RB", RB, incl, g)
            for li in range(1, len(LEVELS)):
                for g in range(2):
                    gs = slice(4 * g, 4 * g + 4)
                    if li < len(LEVELS) - 1:
                        dve.wait_ge(*sn(f"U{li}.{g}"))
                        settled(dve)
                        dve.copy_predicated(TI[:, gs, :], four(level[:, d, li, :]), v3(f"U{li}.{g}"))\
                            .then_inc(*dd(f"T{li}.{g}", f"ev:U{li}.{g}"))
                    dve.wait_ge(*sn(f"V{li}.{g}"))
                    settled(dve)
                    dve.copy_predicated(TI_T[:, gs, :], four(level[:, 1 - d, li, :]), v3(f"V{li}.{g}"))\
                        .then_inc(*dd(f"TT{li}.{g}", f"ev:V{li}.{g}"))
                if li < 6:
                    prep_dve(dve, 1 - d, li, it, f"P{1 - d}.")
                if li == 3:
                    ada_loop_dve(dve, 3 * d + 1, it)
                if li == 5 and d == 0:
                    ada_loop_dve(dve, 2, it)
            dve.wait_ge(*sn("GF"))
            gf = bank(k("GF"))[:, :].rearrange("p (a b) -> p a b", b=64)
            dve.tensor_tensor(GM[:, 1:3, :], gf[:, 1:3, :], M["eye2"][:, 0:64].unsqueeze(1).broadcast_to([P, 2, 64]),
                              ALU.add).then_inc(*dd("GM"))
            dve.wait_ge(*seen(dve, f"P{d}.dc2", it, 1 - d))
            dve.tensor_tensor(FM[:, 0:3, :], gf[:, 4:7, :], step_decay[:, 0:3].unsqueeze(2).broadcast_to([P, 3, 64]),
                              ALU.mult).then_inc(*dd("ev:GF"))
            dve.wait_ge(*sn("Q"))
            lots = [(1, 4)] if d == 0 else [(0, 1), (2, 4)]
            for n, (x, y) in enumerate(lots):
                dve.tensor_tensor(QM.rearrange("p (t c) -> p t c", c=P)[:, x:y, :], v3("Q")[:, x:y, :], KR[:, x:y, 1, :],
                                  ALU.add).then_inc(*dd(*(["ev:Q"] if n == len(lots) - 1 else [])))
            for i in (1, 2):
                dve.wait_ge(*sn(f"S{i}"))
                dve.wait_ge(*sn("ev:GF"))
                dve.scalar_tensor_tensor(SH[:, i + 1, :], bank(k(f"S{i}"))[:, 0:64], step_decay[:, i:i + 1],
                                         FM[:, i, :], ALU.mult, ALU.add).then_inc(*dd(f"ev:S{i}"))
            if d == 0:
                dve.tensor_tensor(kt, kt, r_t[:, it, :], ALU.mult).then_inc(*dd("bs1"))
                dve.wait_ge(*sn("bs1"))
                dve.tensor_tensor(r_t[:, it, :], bsum, kt, ALU.add).then_inc(*dd("bs2"))
            dve.wait_ge(*sn("y"))
            if d == 0:
                dve.tensor_copy(ysum, bank(k("y"))[:, :]).then_inc(*dd("ev:y"))
            else:
                dve.tensor_tensor(kk_t[:, it, :], bank(k("y"))[:, :], ysum, ALU.add).then_inc(*dd("ev:y"))

        def pair_loop(eng, name, body):
            base = L.enter(name, "pair")
            with eng.Fori(0, NPAIR) as it:
                for d in range(2):
                    body(eng, d, it)
            L.leave(name, base, NPAIR)

        post = tuple(part(ring, WORK + 3 * T * c, 3, T) for c in range(NPAIR))

        def post_pe(pe):
            for name, key in (("pb", "prk"), ("pm", None), ("pv", "psq")):
                for c in range(NPAIR):
                    b = take(pe, f"{name}{c}")
                    if key:
                        pe.wait_ge(*seen(pe, f"{key}{c}"))
                    src = {"pb": post[c][:, 1, :], "pm": kk_t[:, c, :], "pv": post[c][:, 0, :]}[name]
                    pe.matmul(b[:, :], M["half_ones"], src, start=True, stop=True).then_inc(*did("pe", f"{name}{c}"))

        def post_act(act):
            for c in range(NPAIR):
                act.activation(post[c][:, 1, :], r_t[:, c, :], ACT.Copy, scale=V("r_k", c)).then_inc(*did("act", f"prk{c}"))
            for c in range(NPAIR):
                act.wait_ge(*seen(act, f"ev:pm{c}"))
                act.activation(post[c][:, 0, :], kk_t[:, c, :], ACT.Square).then_inc(*did("act", f"psq{c}"))
            for c in range(NPAIR):
                act.wait_ge(*seen(act, f"pv{c}"))
                act.activation(post[c][:, 2, :], bank(f"pv{c}")[:, :], ACT.Sqrt, bias=small[:, 1:2], scale=1.0 / 64)\
                    .then_inc(*did("act", f"ev:pv{c}"))
            for c in range(NPAIR):
                act.wait_ge(*seen(act, f"pn{c}"))
                act.activation(kk_t[:, c, :], kk_t[:, c, :], ACT.Identity, scale=V("lnx_w", c), bias=V("lnx_b", c))\
                    .then_inc(*did("act", f"pl{c}"))

        def post_dve(dve):
            for c in range(NPAIR):
                y = kk_t[:, c, :]
                dve.wait_ge(*seen(dve, f"pm{c}"))
                dve.scalar_tensor_tensor(y, bank(f"pm{c}")[:, :], -1.0 / 64, y, ALU.mult, ALU.add)\
                    .then_inc(*did("dve", f"ev:pm{c}"))
            for c in range(NPAIR):
                dve.wait_ge(*seen(dve, f"pb{c}"))
                dve.tensor_tensor(v_t[:, c, :], bank(f"pb{c}")[:, :], v_t[:, c, :], ALU.mult)\
                    .then_inc(*did("dve", f"ev:pb{c}"))

            def finish(c):
                y = kk_t[:, c, :]
                dve.wait_ge(*seen(dve, f"pl{c}"))
                dve.tensor_tensor(y, y, v_t[:, c, :], ALU.add).then_inc(*did("dve", f"py{c}"))
                dve.wait_ge(*seen(dve, f"py{c}"))
                dve.tensor_tensor(mix[:, 4 + c, :], mix[:, 4 + c, :], y, ALU.mult).then_inc(*did("dve", f"mix{c}"))

            for c in range(NPAIR):
                y = kk_t[:, c, :]
                dve.wait_ge(*seen(dve, f"ev:pv{c}"))
                dve.reciprocal(post[c][:, 2, :], post[c][:, 2, :]).then_inc(*did("dve", f"pinv{c}"))
                dve.wait_ge(*seen(dve, f"pinv{c}"))
                dve.tensor_tensor(y, y, post[c][:, 2, :], ALU.mult).then_inc(*did("dve", f"pn{c}"))
                if c:
                    finish(c - 1)
            finish(NPAIR - 1)

        def wout_pe(pe, array, tag, a, ready):
            for g in range(2):
                key = (array, g)
                pe.wait_ge(*arrived(key))
                w = slot(turn[key][0], DC, 512)
                banks = {}
                for ks in ((range(4), range(4, DC)) if g == 0 else (range(DC),)):
                    for j in range(4):
                        if ks[0] == 0:
                            banks[j] = take(pe, f"{tag}.{4 * g + j}")
                        for k in ks:
                            if g == 0 and j == 0 and ready(k):
                                pe.wait_ge(*seen(pe, ready(k)))
                            mm = pe.matmul(banks[j][:, 0:T - a], w[:, k, j * P:(j + 1) * P], mix[:, k, a:T],
                                           start=k == 0, stop=k == DC - 1)
                        if ks[-1] == DC - 1:
                            mm.then_inc(*did("pe", f"{tag}.{4 * g + j}", *([f"used:{array}{g}"] if j == 3 else [])))

        def residual_dve(dve, tag, layer, m, a, h):
            for c in range(DC):
                dve.wait_ge(*seen(dve, f"{tag}.{c}"))
                for x in range(a, T, TC):
                    dve.scalar_tensor_tensor(h[:, c, x:x + TC], bank(f"{tag}.{c}")[:, x - a:x - a + TC],
                                             mods[:, layer, 8 * m + c, x // TC:x // TC + 1], h[:, c, x:x + TC],
                                             ALU.mult, ALU.add)\
                        .then_inc(*did("dve", *([f"ev:{tag}.{c}", f"{tag}.h{c}"] if x == T - TC else [])))

        route_w = part(feat_t, 8192, DC, NR)
        logits = part(feat_t, 8480, NT, NR)
        route = part(feat_t, 8624, 24, NT * EPG)
        chosen_by = part(feat_t, 9392, 2, NT * NE)
        either = part(feat_t, 9648, NT, NE)
        place = part(feat_t, 9776, NT, NE)
        beyond = part(feat_t, 9904, NT, NE)
        count = part(feat_t, 10032, NE)
        extras = part(feat_t, 10064, NE)
        so_far = part(feat_t, 10096, NE)
        wide_t = part(feat_t, 10128, 16 * NE)
        tab = part(feat_t, 10640, 192)
        rank, first_row, limits, ordinals, slots0 = (tab[:, x:y] for x, y in ((0, 8), (8, 40), (40, 48), (48, 64), (64, 192)))
        route_b = part(feat_t, 10832, NR)
        row_of = part(feat_t, 10868, 2, NT)
        share = part(feat_t, 10876, 2, NT)
        row_int = row_int_t[:]
        extra_of = extra_of_t[:, 0:18]
        n_extra = extra_of_t[:, 18:19]
        rows_now = part(feat_t, 10884, P)
        sel_a = part(feat_t, 11012, NT, P)
        sel = part(feat_t, 11524, 2, NT * P)
        sil = part(feat_t, 12548, P)
        hid_t = part(feat_t, 12676, P)
        hid = part(feat_t, 12804, 2, CAP)
        ahead = part(feat_t, 12932, NE)
        xg = part(feat_t, 4096, 2, DC * P)
        yt = part(feat_t, 6144, 4, 512)
        x_tok = part(hm_t, 0, NT, D)
        got = (part(hm_t, 0, NT, D), part(feat_t, 4096, NT, D))

        def route_pe(pe, l, a):
            tag, nt = f"m{l}", (T - a) // P
            banks = [take(pe, f"{tag}.logits{t}") for t in range(nt)]
            pe.wait_ge(router_in, 48 * (l + 1))
            for k in range(DC):
                pe.wait_ge(*seen(pe, f"n2{l}.x{k}"))
                for t in range(nt):
                    pe.matmul(banks[t][:, 0:NR], xT[:, k, a + t * P:a + (t + 1) * P], route_w[:, k, :],
                              start=k == 0, stop=False)
            for t in range(nt):
                pe.matmul(banks[t][:, 0:NR], M["ones"][0:1, :], route_b[0:1, :], start=False, stop=True)\
                    .then_inc(*did("pe", f"{tag}.logits{t}"))
            for t in range(nt):
                for g in range(2):
                    b = take(pe, f"{tag}.xt{t}.{g}")
                    for c in range(4):
                        mm = pe.transpose(b[:, c * P:(c + 1) * P], xT[:, 4 * g + c, a + t * P:a + (t + 1) * P], M["ident"])
                    mm.then_inc(*did("pe", f"{tag}.xt{t}.{g}"))
            b = take(pe, tag + ".place")
            pe.wait_ge(*seen(pe, tag + ".either"))
            for t in range(nt):
                for j in range(t):
                    pe.matmul(b[:, t * NE:(t + 1) * NE], M["ones"], either[:, j, :], start=j == 0, stop=False)
                pe.matmul(b[:, t * NE:(t + 1) * NE], M["lt"], either[:, t, :], start=t == 0, stop=True)
            for j in range(nt):
                mm = pe.matmul(b[:, NT * NE:(NT + 1) * NE], M["ones"], either[:, j, :], start=j == 0, stop=j == nt - 1)
            mm.then_inc(*did("pe", tag + ".place"))
            gather_pe(pe, l, a, f"m{l}.", 0, None)

        def route_dve(dve, l, a):
            tag, nt = f"m{l}", (T - a) // P
            n = [0]

            def link(ins):
                n[0] += 1
                ins.then_inc(*did("dve", f"{tag}.route{n[0]}"))
                dve.wait_ge(*seen(dve, f"{tag}.route{n[0]}"))

            def row(i, w):
                return route[:, i, 0:nt * w].rearrange("p (t w) -> p t w", w=w)

            def wide(x, w):
                return x.broadcast_to([P, nt, w])

            lg, one = logits[:, 0:nt, :], lambda i: row(i, 1)

            def first_of(dst, x, top, w, i):
                link(dve.tensor_tensor(row(i, w), x, wide(top, w), ALU.is_equal))
                link(dve.tensor_tensor(row(i, w), row(i, w),
                                       rank[:, EPG - w:EPG].unsqueeze(1).broadcast_to([P, nt, w]), ALU.mult))
                link(dve.tensor_reduce(one(i + 1), row(i, w), AX, ALU.max))
                link(dve.tensor_tensor(dst, row(i, w), wide(one(i + 1), w), ALU.is_equal))

            for t in range(nt):
                dve.wait_ge(*seen(dve, f"{tag}.logits{t}"))
                dve.tensor_copy(lg[:, t, :], bank(f"{tag}.logits{t}")[:, 0:NR]).then_inc(*did("dve", f"ev:{tag}.logits{t}"))
            dve.wait_ge(*seen(dve, f"ev:{tag}.logits{nt - 1}"))
            groups, experts = lg[:, :, 0:NG], lg[:, :, NG:NR]
            link(dve.tensor_reduce(one(0), groups, AX, ALU.max))
            link(dve.tensor_tensor(row(1, NG), groups, wide(one(0), NG), ALU.subtract))
            first_of(row(2, NG), groups, one(0), NG, 3)
            chosen = row(5, EPG)
            for g in range(NG):
                x = experts[:, :, g * EPG:(g + 1) * EPG]
                oh = wide(row(2, NG)[:, :, g:g + 1], EPG)
                link(dve.tensor_tensor(chosen if g == 0 else row(6, EPG), x, oh, ALU.mult))
                if g:
                    link(dve.tensor_tensor(chosen, chosen, row(6, EPG), ALU.add))
            link(dve.tensor_reduce(one(7), chosen, AX, ALU.max))
            first_of(row(8, EPG), chosen, one(7), EPG, 9)
            link(dve.scalar_tensor_tensor(row(11, EPG), row(8, EPG), -3e38, chosen, ALU.mult, ALU.add))
            link(dve.tensor_reduce(one(12), row(11, EPG), AX, ALU.max))
            first_of(row(13, EPG), row(11, EPG), one(12), EPG, 14)
            dve.tensor_tensor(one(16), one(12), one(7), ALU.subtract).then_inc(*did("dve", tag + ".gap"))
            chosen_at = [chosen_by[:, k, 0:nt * NE].rearrange("p (t g e) -> p t g e", g=NG, e=EPG) for k in range(2)]
            by = [chosen_by[:, k, 0:nt * NE].rearrange("p (t e) -> p t e", e=NE) for k in range(2)]
            for k, i in enumerate((8, 13)):
                link(dve.tensor_tensor(chosen_at[k], row(2, NG).unsqueeze(3).broadcast_to([P, nt, NG, EPG]),
                                       row(i, EPG).unsqueeze(2).broadcast_to([P, nt, NG, EPG]), ALU.mult))
            dve.tensor_tensor(either[:, 0:nt, :], by[0], by[1], ALU.add).then_inc(*did("dve", tag + ".either"))
            dve.wait_ge(*seen(dve, tag + ".exps"))
            link(dve.tensor_reduce(one(17), row(1, NG), AX, ALU.add))
            link(dve.tensor_scalar(one(18), one(16), 1.0, None, ALU.add))
            link(dve.tensor_tensor(one(17), one(17), one(18), ALU.mult))
            link(dve.reciprocal(share[:, 0, 0:nt], route[:, 17, 0:nt]))
            link(dve.tensor_tensor(share[:, 1, 0:nt], share[:, 0, 0:nt], route[:, 16, 0:nt], ALU.mult))
            dve.wait_ge(*seen(dve, tag + ".place"))
            b = bank(tag + ".place")
            link(dve.tensor_copy(place[:, 0:nt, :], b[:, 0:nt * NE].rearrange("p (t e) -> p t e", e=NE)))
            dve.tensor_copy(count, b[:, NT * NE:(NT + 1) * NE]).then_inc(*did("dve", f"ev:{tag}.place"))
            dve.wait_ge(*seen(dve, f"ev:{tag}.place"))
            link(dve.tensor_tensor(wide_t[:, 0:8 * NE].rearrange("p (e m) -> p e m", m=8),
                                   count.unsqueeze(2).broadcast_to([P, NE, 8]),
                                   limits.unsqueeze(1).broadcast_to([P, NE, 8]), ALU.is_gt))
            link(dve.tensor_reduce(extras, wide_t[:, 0:8 * NE].rearrange("p (e m) -> p e m", m=8), AX, ALU.add))
            link(dve.tensor_tensor_scan(so_far, M["ones"][:, 0:NE], extras, 0.0, ALU.mult, ALU.add))
            link(dve.tensor_tensor(ahead, so_far, extras, ALU.subtract))
            link(dve.tensor_scalar(ahead, ahead, float(CAP), float(CAP * (NE - 1)), ALU.mult, ALU.add))
            link(dve.tensor_tensor(ahead, ahead, first_row, ALU.subtract))
            link(dve.tensor_scalar(beyond[:, 0:nt, :], place[:, 0:nt, :], float(CAP), None, ALU.is_ge))
            link(dve.tensor_tensor(beyond[:, 0:nt, :], beyond[:, 0:nt, :], ahead.unsqueeze(1).broadcast_to([P, nt, NE]),
                                   ALU.mult))
            link(dve.tensor_tensor(place[:, 0:nt, :], place[:, 0:nt, :], first_row.unsqueeze(1).broadcast_to([P, nt, NE]),
                                   ALU.add))
            link(dve.tensor_tensor(place[:, 0:nt, :], place[:, 0:nt, :], beyond[:, 0:nt, :], ALU.add))
            for k in range(2):
                link(dve.tensor_tensor(beyond[:, 0:nt, :], place[:, 0:nt, :], by[k], ALU.mult))
                link(dve.tensor_reduce(row_of[:, k, 0:nt], beyond[:, 0:nt, :], AX, ALU.add))
            dve.tensor_copy(row_int, row_of).then_inc(*did("dve", tag + ".rows"))
            dve.tensor_copy(rows_now, slots0).then_inc(*did("dve", tag + ".now"))
            select_dve(dve, l, a, f"m{l}.", 0, None, (f"m{l}.now", None, 0))
            link(dve.tensor_copy(n_extra, so_far[:, NE - 1:NE]))
            w3 = wide_t.rearrange("p (x e) -> p x e", e=NE)
            link(dve.tensor_tensor(w3, so_far.unsqueeze(1).broadcast_to([P, 16, NE]),
                                   ordinals.unsqueeze(2).broadcast_to([P, 16, NE]), ALU.is_le))
            link(dve.tensor_reduce(route[:, 0, 0:16], w3, AX, ALU.add))
            link(dve.tensor_scalar(route[:, 0, 0:16], route[:, 0, 0:16], NE - 1.0, None, ALU.min))
            dve.tensor_copy(extra_of[:, 0:16], route[:, 0, 0:16]).then_inc(*did("dve", tag + ".extras"))

        def route_act(act, l, a):
            tag, nt = f"m{l}", (T - a) // P
            for t in range(nt):
                for g in range(2):
                    act.wait_ge(*seen(act, f"{tag}.xt{t}.{g}"))
                    act.activation(x_tok[:, t, 512 * g:512 * g + 512], bank(f"{tag}.xt{t}.{g}")[:, :], ACT.Copy)\
                        .then_inc(*did("act", f"ev:{tag}.xt{t}.{g}"))
            act.wait_ge(*seen(act, tag + ".gap"))
            act.activation(route[:, 1, 0:nt * NG], route[:, 1, 0:nt * NG], ACT.Exp).then_inc(*did("act"))
            act.activation(route[:, 16, 0:nt], route[:, 16, 0:nt], ACT.Exp).then_inc(*did("act", tag + ".exps"))
            for half in range(2):
                take_in_act(act, f"m{l}.", half, 0, None)

        def select_dve(dve, l, a, prefix, par, it, ready):
            nt, k_ = (T - a) // P, lambda x: named(prefix, x)
            s3 = sel[:, par, 0:nt * P].rearrange("p (t c) -> p t c", c=P)
            now = rows_now.unsqueeze(1).broadcast_to([P, nt, P])
            dve.wait_ge(*seen(dve, *ready))
            for k, dst in ((0, sel_a[:, 0:nt, :]), (1, s3)):
                dve.tensor_tensor(dst, row_of[:, k, 0:nt].unsqueeze(2).broadcast_to([P, nt, P]), now, ALU.is_equal)\
                    .then_inc(*did("dve", k_(f"sel{k}")))
            dve.wait_ge(*seen(dve, k_("sel1"), it))
            dve.tensor_tensor(s3, s3, sel_a[:, 0:nt, :], ALU.add).then_inc(*did("dve", k_("sel")))
            dve.tensor_scalar(rows_now, rows_now, float(P), None, ALU.add).then_inc(*did("dve", k_("next")))

        def gather_part(pe, l, a, b, half, par, chunks):
            nt = (T - a) // P
            for c in chunks:
                for t in range(nt):
                    mm = pe.matmul(b[:, c * P:(c + 1) * P], x_tok[:, t, (4 * half + c) * P:(4 * half + c + 1) * P],
                                   sel[:, par, t * P:(t + 1) * P], start=t == 0, stop=t == nt - 1)
            return mm

        def gather_pe(pe, l, a, prefix, par, it):
            k_ = lambda x: named(prefix, x)
            for half in range(2):
                b = take(pe, k_(f"xg{half}"), it)
                if half == 0:
                    pe.wait_ge(*seen(pe, k_("sel"), it))
                    if it is None:
                        pe.wait_ge(*seen(pe, f"ev:m{l}.xt{(T - a) // P - 1}.1"))
                gather_part(pe, l, a, b, half, par, range(4)).then_inc(*did("pe", k_(f"xg{half}")))

        def take_in_act(act, prefix, half, par, it):
            k_ = lambda x: named(prefix, x)
            act.wait_ge(*seen(act, k_(f"xg{half}"), it))
            act.activation(xg[:, par, 512 * half:512 * half + 512], bank(k_(f"xg{half}"))[:, :], ACT.Copy)\
                .then_inc(*did("act", k_(f"ev:xg{half}")))

        def hidden_pe(pe, prefix, s, par, it, turn_, ready):
            k_ = lambda x: named(prefix, x)
            w = part(ring, s * SLOT, 2, DC * 256).rearrange("p a (k n) -> p a k n", n=256)
            b = take(pe, k_("gu"), it)
            pe.wait_ge(loaded[s], it * 16 + 16 * turn_)
            if ready is not None:
                pe.wait_ge(*seen(pe, *ready))
            x = xg[:, par, :].rearrange("p (k j c) -> p k j c", j=2, c=CAP)
            for k in range(DC):
                for g in range(2):
                    mm = pe.matmul(b[64 * g:64 * g + 64, 0:256].rearrange("p (a n) -> p a n", n=P), x[:, k, s % 2, :],
                                   w[:, :, k, g * P:(g + 1) * P], start=k == 0, stop=k == DC - 1)
            mm.then_inc(*did("pe", k_("gu")))

        def hidden_act(act, prefix, it):
            k_ = lambda x: named(prefix, x)
            act.wait_ge(*seen(act, k_("gu"), it))
            act.activation(sil, bank(k_("gu"))[:, 0:P], ACT.Silu).then_inc(*did("act", k_("sil")))

        def hidden_dve(dve, prefix, it):
            k_ = lambda x: named(prefix, x)
            dve.wait_ge(*seen(dve, k_("sil"), it))
            dve.tensor_tensor(hid_t, bank(k_("gu"))[:, P:2 * P], sil, ALU.mult).then_inc(*did("dve", k_("ev:gu")))

        def turn_pe(pe, prefix, it):
            k_ = lambda x: named(prefix, x)
            b = take(pe, k_("ht"), it)
            pe.wait_ge(*seen(pe, k_("ev:gu"), it))
            pe.transpose(b[:, 0:P], hid_t, M["ident"]).then_inc(*did("pe", k_("ht")))

        def turn_act(act, prefix, it):
            k_ = lambda x: named(prefix, x)
            act.wait_ge(*seen(act, k_("ht"), it))
            act.activation(hid, bank(k_("ht"))[:, 0:P].rearrange("p (h c) -> p h c", c=CAP), ACT.Copy)\
                .then_inc(*did("act", k_("ev:ht")))

        def down_pe(pe, prefix, s, it):
            k_ = lambda x: named(prefix, x)
            down = part(ring, s * SLOT + 4096, 2, D)
            b = take(pe, k_("down"), it)
            pe.wait_ge(*seen(pe, k_("ev:ht"), it))
            for hc in range(2):
                for g in range(2):
                    mm = pe.matmul(b[64 * g:64 * g + 64, :], hid[:, hc, :], down[:, hc, 512 * g:512 * g + 512],
                                   start=hc == 0, stop=hc == 1)
            mm.then_inc(*did("pe", k_("down")))

        def down_dve(dve, prefix, s, it, out_turn):
            k_ = lambda x: named(prefix, x)
            dve.wait_ge(*seen(dve, k_("down"), it))
            dve.wait_ge(y_out[s], it * 32 + 32 * out_turn)
            dve.tensor_copy(yt[:, s, :], bank(k_("down"))[:, :]).then_inc(*did("dve", k_("ev:down")))

        def expert_pe(pe, l, a, s, it, first_turn):
            me, before, par = f"e{l}.{s}.", f"e{l}.{(s - 1) % 4}.", s // 2
            hidden_pe(pe, me, s, par, it, first_turn,
                      None if s % 2 else (named(before, "ev:xg1"), it, 0 if s else 1))
            b = take(pe, named(me, f"xg{s % 2}"), it)
            if s % 2 == 0:
                pe.wait_ge(*seen(pe, named(me, "sel"), it))
            gather_part(pe, l, a, b, s % 2, 1 - par, range(2))
            turn_pe(pe, me, it)
            gather_part(pe, l, a, b, s % 2, 1 - par, range(2, 4)).then_inc(*did("pe", named(me, f"xg{s % 2}")))
            down_pe(pe, me, s, it)

        def expert_act(act, l, s, it):
            me = f"e{l}.{s}."
            hidden_act(act, me, it)
            turn_act(act, me, it)
            take_in_act(act, me, s % 2, 1 - s // 2, it)

        def expert_dve(dve, l, a, s, it):
            me, before = f"e{l}.{s}.", f"e{l}.{(s - 2) % 4}."
            if s % 2 == 0:
                select_dve(dve, l, a, me, 1 - s // 2, it, (named(before, "next"), it, 0 if s else 1))
            hidden_dve(dve, me, it)
            down_dve(dve, me, s, it, out_base[l][s])

        def expert_loop(eng, name, l, body):
            base = L.enter(name, f"experts{l}")
            with eng.Fori(0, NE // 4) as it:
                for s in range(4):
                    body(s, it)
            L.leave(name, base, NE // 4)

        n_extras = [16, 8]
        out_base, extra_base = [(1, 1, 1, 1)], []
        for l in range(2):
            extra_base.append(tuple(x + NE // 4 for x in out_base[l]))
            out_base.append(tuple(x + (n_extras[l] // 2 if s < 2 else 0) for s, x in enumerate(extra_base[l])))

        def extra_loop(eng, name, l, body):
            n = eng.value_load(n_extra[0:1, :], min_val=0, max_val=16)
            base = L.enter(name, f"extras{l}")
            with eng.Fori(0, n_extras[l] // 2) as it:
                with eng.If(n > it * 2):
                    body(0, it)
                    first = L.count[name]
                    with eng.If(n > it * 2 + 1):
                        body(1, it)
                    with eng.Else():
                        eng.drain()
                        eng.sem_inc(sems[name], max(L.count[name] - first, 1))
                with eng.Else():
                    eng.drain()
                    eng.sem_inc(sems[name], max(L.count[name], 1))
            L.leave(name, base, n_extras[l] // 2)

        def extra_pe(pe, l, a, s, it):
            me = f"x{l}.{s}."
            hidden_pe(pe, me, s, 0, it, turn["extra", EXTRA_ITEMS[0] * l + s][1],
                      None if s else (f"ev:x{l}.1.xg1", it, 1))
            turn_pe(pe, me, it)
            down_pe(pe, me, s, it)
            if s:
                gather_pe(pe, l, a, me, 0, it)

        def extra_act(act, l, s, it):
            me = f"x{l}.{s}."
            hidden_act(act, me, it)
            turn_act(act, me, it)
            for half in range(2 * s):
                take_in_act(act, me, half, 0, it)

        def extra_dve(dve, l, a, s, it):
            me = f"x{l}.{s}."
            hidden_dve(dve, me, it)
            down_dve(dve, me, s, it, extra_base[l][s])
            if s:
                select_dve(dve, l, a, me, 0, it, (me + "next", it, 1))

        def mixed_pe(pe, l, a):
            nt = (T - a) // P
            banks = [take(pe, f"z{l}.{c}") for c in range(DC)]
            for t in range(nt):
                pe.wait_ge(*seen(pe, f"z{l}.y{t}"))
                for c in range(DC):
                    mm = pe.transpose(banks[c][:, t * P:(t + 1) * P], got[0][:, t, c * P:(c + 1) * P], M["ident"])
                    if t == nt - 1:
                        mm.then_inc(*did("pe", f"z{l}.{c}"))

        def mixed_act(act, l, a):
            for t in range((T - a) // P):
                act.wait_ge(got_in[t], 32 * (l + 1))
                act.activation(got[0][:, t, :], got[0][:, t, :], ACT.Copy, scale=share[:, 0, t:t + 1])\
                    .then_inc(*did("act", f"z{l}.a{t}"))

        def mixed_dve(dve, l, a):
            for t in range((T - a) // P):
                dve.wait_ge(got_in[t], 32 * (l + 1))
                dve.wait_ge(*seen(dve, f"z{l}.a{t}"))
                dve.scalar_tensor_tensor(got[0][:, t, :], got[1][:, t, :], share[:, 1, t:t + 1], got[0][:, t, :],
                                         ALU.mult, ALU.add).then_inc(*did("dve", f"z{l}.y{t}"))
            residual_dve(dve, f"z{l}", l, 5, a, hT)

        def mixed_pool(pool, l, a):
            for i in range(4):
                pool.wait_ge(y_out[i], 32 * out_base[l + 1][i])
            for t in range((T - a) // P):
                for k in range(2):
                    pool.indirect_dma_start(out=got[k][:, t, :], out_offset=None, in_=dram["results"],
                                            in_offset=bass.IndirectOffsetOnAxis(ap=row_int[:, k, t:t + 1], axis=0))\
                        .then_inc(got_in[t], 16)

        F0 = 8192
        cq = part(feat_t, F0, 3, TC)
        ckv = part(feat_t, F0 + 768, 2, T)
        kpe = part(feat_t, F0 + 1792, T)
        qn = part(feat_t, F0 + 2304, MH, TC)
        qpe = part(feat_t, F0 + 4352, 4, TC)
        rope = part(feat_t, F0 + 5376, 2, TC)
        pmax = part(feat_t, F0 + 5888, 16)
        psum_ = part(feat_t, F0 + 5904, 16)
        kn = part(feat_t, 4096, MH, T)
        val = part(xT_t, 0, NT, D)
        prob = part(feat_t, F0 + 6144, 2, T)
        rope_tmp = part(feat_t, F0 + 7168, T)

        def mla_pe(pe):
            w = slot(turn["mla_in", 0][0], DC, 768)
            pe.wait_ge(*arrived(("mla_in", 0)))
            for j in range(6):
                a = TC if j < 3 else 0
                mm = proj_pe(pe, f"mi{j}", w, DC, j * P, lambda k: xT[:, k, a:T], T - a, P,
                             (lambda k: f"n11.x{k}") if j == 0 else None)
                mm.then_inc(*did("pe", f"mi{j}", *(["used:mla_in0"] if j == 5 else [])))
            b = take(pe, "kswap")
            pe.wait_ge(*seen(pe, "ev:mi5"))
            pe.matmul(b[:, 0:TC], M["swap"], kpe[:, TC:T], start=True, stop=True).then_inc(*did("pe", "kswap"))
            norm_pe(pe, "nq", TC, 3, (hm_t, 0))
            norm_pe(pe, "nkv", T, 2, (hm_t, 1536))
            w = slot(turn["mla_uq", 0][0], 3, 1536)
            pe.wait_ge(*arrived(("mla_uq", 0)))
            for j in range(12):
                mm = proj_pe(pe, f"uq{j}", w, 3, j * P, lambda k: cq[:, k, :], TC, P,
                             (lambda k: f"cq{k}") if j == 0 else None)
                mm.then_inc(*did("pe", f"uq{j}", *(["used:mla_uq0"] if j == 11 else [])))
            for j in range(4):
                b = take(pe, f"qswap{j}")
                pe.wait_ge(*seen(pe, f"ev:uq{8 + j}"))
                pe.matmul(b[:, 0:TC], M["swap"], qpe[:, j, :], start=True, stop=True).then_inc(*did("pe", f"qswap{j}"))
            w = slot(turn["mla_ukv", 0][0], 2, 2048)
            pe.wait_ge(*arrived(("mla_ukv", 0)))
            for j in range(8):
                proj_pe(pe, f"uk{j}", w, 2, j * P, lambda k: ckv[:, k, :], T, P,
                        (lambda k: f"ckv{k}") if j == 0 else None).then_inc(*did("pe", f"uk{j}"))
            for t in range(NT):
                for g in range(2):
                    b = take(pe, f"uv{t}.{g}")
                    for k in range(2):
                        mm = pe.matmul(b[:, :], ckv[:, k, t * P:(t + 1) * P], w[:, k, 1024 + 512 * g:1536 + 512 * g],
                                       start=k == 0, stop=k == 1)
                    mm.then_inc(*did("pe", f"uv{t}.{g}", *(["used:mla_ukv0"] if t == 3 and g == 1 else [])))
            def scores_pe(h, qt):
                qs = slice(qt * P, (qt + 1) * P)
                b = take(pe, f"s{h}.{qt}")
                if h == 0:
                    pe.wait_ge(*seen(pe, "ev:uk7"))
                    pe.wait_ge(*seen(pe, "qpe3"))
                pe.matmul(b[:, :], qn[:, h, qs], kn[:, h, :], start=True, stop=False)
                pe.matmul(b[:, :], qpe[half(h % 2), h // 2, qs], kpe[half(h % 2), :], start=False, stop=True)\
                    .then_inc(*did("pe", f"s{h}.{qt}"))

            for h in range(MH + 1):
                if h < MH:
                    scores_pe(h, 0)
                if h:
                    g = h - 1
                    for kp in range(2):
                        b = take(pe, f"pt{g}.{kp}")
                        for i in range(2):
                            for qt in range(2):
                                if kp == 0 and i == 0:
                                    pe.wait_ge(*seen(pe, f"p{g}.{qt}"))
                                mm = pe.transpose(b[:, (2 * i + qt) * P:(2 * i + qt + 1) * P],
                                                  prob[:, qt, (2 * kp + i) * P:(2 * kp + i + 1) * P], M["ident"])
                        mm.then_inc(*did("pe", f"pt{g}.{kp}"))
                if h < MH:
                    scores_pe(h, 1)
                if h:
                    b = take(pe, f"o{g}")
                    for kt_ in range(NT):
                        pe.wait_ge(*seen(pe, f"ev:pt{g}.{kt_ // 2}"))
                        if g == 0 and kt_ == 0:
                            pe.wait_ge(*seen(pe, "ev:uv3.1"))
                        mm = pe.matmul(b[:, 0:TC], val[:, kt_, g * P:(g + 1) * P], prob_T[:, kt_, :],
                                       start=kt_ == 0, stop=kt_ == NT - 1)
                    mm.then_inc(*did("pe", f"o{g}"))

        mix_lo = hm_t[:].rearrange("p (c t) -> p c t", t=T)[:, :, 0:TC]
        prob_T = mix_lo[:, 4:8, :]

        def mla_act(act):
            for j in range(6):
                act.wait_ge(*seen(act, f"mi{j}"))
                dst = cq[:, j, :] if j < 3 else ckv[:, j - 3, :] if j < 5 else kpe[:, :]
                act.activation(dst, bank(f"mi{j}")[:, 0:(TC if j < 3 else T)], ACT.Copy).then_inc(*did("act", f"ev:mi{j}"))
            norm_act(act, "nq", lambda k: cq[:, k, :], TC, 3, (hm_t, 0), ["ev:mi0", "ev:mi1", "ev:mi2"])
            norm_act(act, "nkv", lambda k: ckv[:, k, :], T, 2, (hm_t, 1536), ["ev:mi3", "ev:mi4"])
            for j in range(12):
                act.wait_ge(*seen(act, f"uq{j}"))
                dst = qn[:, j, :] if j < 8 else qpe[:, j - 8, :]
                act.activation(dst, bank(f"uq{j}")[:, 0:TC], ACT.Copy).then_inc(*did("act", f"ev:uq{j}"))
            for t in range(NT):
                for g in range(2):
                    act.wait_ge(*seen(act, f"uv{t}.{g}"))
                    act.activation(val[:, t, 512 * g:512 * g + 512], bank(f"uv{t}.{g}")[:, :], ACT.Copy)\
                        .then_inc(*did("act", f"ev:uv{t}.{g}"))
            for h in range(MH):
                for qt in range(2):
                    i = 2 * h + qt
                    act.wait_ge(*seen(act, f"max{h}.{qt}"))
                    if h:
                        act.wait_ge(*seen(act, f"pt{h - 1}.1"))
                    act.activation(prob[:, qt, :], bank(f"s{h}.{qt}")[:, :], ACT.Exp, bias=pmax[:, i:i + 1],
                                   scale=MLA_SCALE, accum_out=psum_[:, i:i + 1]).then_inc(*did("act", f"ev:s{h}.{qt}"))

        def rope_dve(dve, x, job, key, tmp, at):
            dve.wait_ge(*seen(dve, job))
            dve.tensor_tensor(tmp, bank(job)[:, 0:TC], rope[:, 1, :], ALU.mult).then_inc(*did("dve", "ev:" + job))
            dve.tensor_tensor(x, x, rope[:, 0, :], ALU.mult).then_inc(*did("dve", key + ".c"))
            dve.wait_ge(*seen(dve, key + ".c"))
            dve.tensor_tensor(x, x, tmp, ALU.add).then_inc(*did("dve", key))

        def mla_dve(dve):
            dve.wait_ge(rope_in, 16)
            rope_dve(dve, kpe[:, TC:T], "kswap", "kpe", rope_tmp[:, 0:TC], 0)
            for tag, x, n, chunks, g, at in (("nq", cq, TC, 3, "q_norm", 0), ("nkv", ckv, T, 2, "kv_norm", 1536)):
                norm_dve(dve, tag, lambda k: x[:, k, :], lambda k: x[:, k, :], n, chunks, (hm_t, at))
                for k in range(chunks):
                    dve.wait_ge(*seen(dve, f"{tag}.xr{k}"))
                    dve.tensor_scalar(x[:, k, :], x[:, k, :], V(g, k), None, ALU.mult)\
                        .then_inc(*did("dve", f"{'cq' if tag == 'nq' else 'ckv'}{k}"))
            for j in range(4):
                if j:
                    dve.wait_ge(*seen(dve, f"qpe{j - 1}"))
                rope_dve(dve, qpe[:, j, :], f"qswap{j}", f"qpe{j}", rope_tmp[:, 0:TC], 0)
            for j in range(8):
                dve.wait_ge(*seen(dve, f"uk{j}"))
                dve.tensor_copy(kn[:, j, :], bank(f"uk{j}")[:, :]).then_inc(*did("dve", f"ev:uk{j}"))
            def top_dve(h, qt):
                i = 2 * h + qt
                dve.wait_ge(*seen(dve, f"s{h}.{qt}"))
                dve.tensor_reduce(pmax[:, i:i + 1], bank(f"s{h}.{qt}")[:, :], AX, ALU.max, negate=True)\
                    .then_inc(*did("dve", f"mx{h}.{qt}"))
                dve.wait_ge(*seen(dve, f"mx{h}.{qt}"))
                dve.tensor_scalar(pmax[:, i:i + 1], pmax[:, i:i + 1], MLA_SCALE, None, ALU.mult)\
                    .then_inc(*did("dve", f"max{h}.{qt}"))

            for h in range(MH + 1):
                g = h - 1
                for qt in range(2 if h else 0):
                    i = 2 * g + qt
                    dve.wait_ge(*seen(dve, f"ev:s{g}.{qt}"))
                    dve.reciprocal(psum_[:, i:i + 1], psum_[:, i:i + 1]).then_inc(*did("dve", f"ri{g}.{qt}"))
                    dve.wait_ge(*seen(dve, f"ri{g}.{qt}"))
                    dve.tensor_scalar(prob[:, qt, :], prob[:, qt, :], psum_[:, i:i + 1], None, ALU.mult)\
                        .then_inc(*did("dve", f"p{g}.{qt}"))
                if h < MH:
                    top_dve(h, 0)
                for kp in range(2 if h else 0):
                    dve.wait_ge(*seen(dve, f"pt{g}.{kp}"))
                    if g:
                        dve.wait_ge(*seen(dve, f"o{g - 1}"))
                    dve.tensor_copy(prob_T[:, 2 * kp:2 * kp + 2, :],
                                    bank(f"pt{g}.{kp}")[:, :].rearrange("p (a b) -> p a b", b=TC))\
                        .then_inc(*did("dve", f"ev:pt{g}.{kp}"))
                if h < MH:
                    top_dve(h, 1)
                if h:
                    dve.wait_ge(*seen(dve, f"o{g}"))
                    dve.tensor_copy(mix[:, g, TC:T], bank(f"o{g}")[:, 0:TC]).then_inc(*did("dve", f"ev:o{g}"))

        def experts_pe(pe, l, a):
            expert_loop(pe, "pe", l, lambda s, it: expert_pe(pe, l, a, s, it, turn["expert", NE * l + s][1]))
            barrier(pe, "pe", f"experts{l}")
            extra_loop(pe, "pe", l, lambda s, it: extra_pe(pe, l, a, s, it))
            barrier(pe, "pe", f"extras{l}")
            mixed_pe(pe, l, a)

        def experts_act(act, l, a):
            expert_loop(act, "act", l, lambda s, it: expert_act(act, l, s, it))
            barrier(act, "act")
            extra_loop(act, "act", l, lambda s, it: extra_act(act, l, s, it))
            barrier(act, "act")
            mixed_act(act, l, a)

        def experts_dve(dve, l, a):
            expert_loop(dve, "dve", l, lambda s, it: expert_dve(dve, l, a, s, it))
            barrier(dve, "dve")
            extra_loop(dve, "dve", l, lambda s, it: extra_dve(dve, l, a, s, it))
            barrier(dve, "dve")
            mixed_dve(dve, l, a)

        @block.tensor
        def _(pe):
            pe.wait_ge(consts_in, 16 * N_CONST)
            pe.wait_ge(*seen(pe, "silu_c"))
            pe.wait_ge(*seen(pe, "sum32"))
            for g in range(ADA_FIRST):
                ada_sum_pe(pe, f"ada{g}", g % 2, 16 * turn["ada", g][1])
                ada_turn_pe(pe, f"ada{g}")
            norm_pe(pe, "n1", T, DC, NORM)
            for g in range(3):
                for j in range(4):
                    win_pe(pe, g, j)
            ret_pe(pe)
            for g in (5, 6):
                for j in range(4):
                    win_pe(pe, g, j)
                    if g == 5 and j == 1:
                        kk_pe(pe)
            lora_pe(pe)
            gate_pe(pe)
            barrier(pe, "pe")
            pair_loop(pe, "pe", pair_pe)
            barrier(pe, "pe")
            post_pe(pe)
            wout_pe(pe, "wout", "wo", 0, lambda k: f"mix{k - 4}" if k >= 4 else None)
            norm_pe(pe, "n20", T, DC, NORM)
            route_pe(pe, 0, 0)
            barrier(pe, "pe")
            experts_pe(pe, 0, 0)
            norm_pe(pe, "n11", T, DC, NORM2)
            mla_pe(pe)
            wout_pe(pe, "mla_o", "mo", TC, lambda k: f"ev:o{k}")
            norm_pe(pe, "n21", TC, DC, NORM2)
            route_pe(pe, 1, TC)
            barrier(pe, "pe")
            experts_pe(pe, 1, TC)
            norm_pe(pe, "nf", TC, DC, NORM2)

        @block.scalar
        def _(act):
            act.wait_ge(consts_in, 16 * N_CONST)
            act.wait_ge(*seen(act, "silu0"))
            for i, name in enumerate(("c_ctx", "c")):
                act.activation(silu_c[:, :, i], V(name), ACT.Silu).then_inc(*did("act", *(["silu_c"] if i else [])))
            for g in range(ADA_FIRST):
                ada_act(act, f"ada{g}")
            act.wait_ge(h_in, 16)
            act.wait_ge(*seen(act, "eps"))
            norm_act(act, "n1", lambda k: hm[:, k, :], T, DC, NORM)
            act.wait_ge(*seen(act, "gain0.0"))
            modulate_act(act, "n1", 0, 0, SEGS)
            ret_feat_act(act)
            ret_act(act)
            kk_act(act)
            lora_act(act)
            act.wait_ge(*seen(act, "P.E"))
            for step in range(3):
                prep_act(act, 0, step, None, "P.")
            gate_act(act)
            barrier(act, "act")
            pair_loop(act, "act", pair_act)
            barrier(act, "act")
            post_act(act)
            norm_act(act, "n20", lambda k: hT[:, k, :], T, DC, NORM, [f"wo.h{k}" for k in range(DC)])
            modulate_act(act, "n20", 0, 1, SEGS)
            route_act(act, 0, 0)
            barrier(act, "act")
            experts_act(act, 0, 0)
            norm_act(act, "n11", lambda k: hT[:, k, :], T, DC, NORM2, [f"z0.h{k}" for k in range(DC)])
            modulate_act(act, "n11", 1, 0, SEGS)
            mla_act(act)
            norm_act(act, "n21", lambda k: hT[:, k, TC:T], TC, DC, NORM2, [f"mo.h{k}" for k in range(DC)])
            modulate_act(act, "n21", 1, 1, SEGS[1:])
            route_act(act, 1, TC)
            barrier(act, "act")
            experts_act(act, 1, TC)
            norm_act(act, "nf", lambda k: hT[:, k, TC:T], TC, DC, NORM2, [f"z1.h{k}" for k in range(DC)])

        @block.vector
        def _(dve):
            dve.memset(small[:, 0:1], EPS).then_inc(*did("dve"))
            dve.memset(small[:, 1:2], GN_EPS).then_inc(*did("dve", "eps"))
            dve.memset(silu_c[:], 0.0).then_inc(*did("dve", "silu0"))
            dve.wait_ge(consts_in, 16 * N_CONST)
            dve.tensor_tensor(small[:, 24:26], M["eye2"][:, 0:2], M["eye2"][:, 32:34], ALU.add)\
                .then_inc(*did("dve", "sum32"))
            dve.tensor_tensor(small[:, 8:24], V("mu0"), V("mu1"), ALU.add).then_inc(*did("dve", "mu"))
            dve.wait_ge(*seen(dve, "mu"))
            dve.tensor_scalar(small[:, 8:24], small[:, 8:24], -1.0, 1.0, ALU.mult, ALU.add).then_inc(*did("dve", "one_mu"))
            dve.wait_ge(*seen(dve, "one_mu"))
            for g in range(ADA_FIRST):
                ada_dve(dve, f"ada{g}", 4 * g)
            gain_dve(dve, 0, 0, f"ev:ada{ADA_FIRST - 1}t")
            dve.wait_ge(h_in, 16)
            norm_dve(dve, "n1", lambda k: hm[:, k, :], lambda k: xT[:, k, :], T, DC, NORM)
            modulate_dve(dve, "n1", 0, 0, SEGS)
            dve.wait_ge(tables_in, 32)
            ret_dve(dve)
            kk_scale_dve(dve)
            for g in (5, 6):
                for j in range(4):
                    shift_dve(dve, g, j)
                    if g == 5:
                        kk_dve(dve, j)
            dve.wait_ge(*seen(dve, "ev:la0.0"))
            for step in range(1, 6):
                prep_dve(dve, 0, step, None, "P.")
            barrier(dve, "dve")
            pair_loop(dve, "dve", pair_dve)
            barrier(dve, "dve")
            for layer, which in ((0, 1), (1, 0), (1, 1)):
                gain_dve(dve, layer, which, f"ev:A{ADA_TURN - 1}t")
            post_dve(dve)
            dve.wait_ge(h_again, 16)
            residual_dve(dve, "wo", 0, 2, 0, hT)
            norm_dve(dve, "n20", lambda k: hT[:, k, :], lambda k: xT[:, k, :], T, DC, NORM)
            modulate_dve(dve, "n20", 0, 1, SEGS)
            dve.wait_ge(router_in, 48)
            route_dve(dve, 0, 0)
            barrier(dve, "dve")
            experts_dve(dve, 0, 0)
            norm_dve(dve, "n11", lambda k: hT[:, k, :], lambda k: xT[:, k, :], T, DC, NORM2)
            modulate_dve(dve, "n11", 1, 0, SEGS)
            mla_dve(dve)
            residual_dve(dve, "mo", 1, 2, TC, hT)
            norm_dve(dve, "n21", lambda k: hT[:, k, TC:T], lambda k: xT[:, k, TC:T], TC, DC, NORM2)
            modulate_dve(dve, "n21", 1, 1, SEGS[1:])
            dve.wait_ge(router_in, 96)
            route_dve(dve, 1, TC)
            barrier(dve, "dve")
            experts_dve(dve, 1, TC)
            norm_dve(dve, "nf", lambda k: hT[:, k, TC:T], lambda k: xT[:, k, 0:TC], TC, DC, NORM2)
            for k in range(DC):
                dve.wait_ge(*seen(dve, f"nf.xr{k}"))
                dve.tensor_scalar(xT[:, k, 0:TC], xT[:, k, 0:TC], V("final_g", k), None, ALU.mult)\
                    .then_inc(*did("dve", f"out{k}"))

        @block.gpsimd
        def _(pool):
            pool.wait_ge(tables_in, 32)
            pool.tensor_copy(level_t[:], part(ring, WORK + 9216, 2 * len(LEVELS) * P)).then_inc(*did("pool", "levels"))
            barrier(pool, "pool")
            pair_loop(pool, "pool", pair_pool)
            barrier(pool, "pool")
            for l, a in ((0, 0), (1, TC)):
                for _ in range(3):
                    barrier(pool, "pool")
                mixed_pool(pool, l, a)

        @block.sync
        def _(sp):
            sp.dma_start(vec[:], dram["vec"]).then_inc(consts_in, 16)
            sp.dma_start(mask_t[:], dram["masks"]).then_inc(consts_in, 16)

            def load(key):
                a, i = key
                before = previous[key]
                if before is not None:
                    sp.wait_ge(*seen(sp, f"used:{before[0]}{before[1]}"))
                s, n = turn[key]
                w = next(w for x, j, w, _ in items if (x, j) == key)
                sp.dma_start(ring[:, s * SLOT:s * SLOT + w], dram[a][i]).then_inc(loaded[s], 16)

            def passed(label):
                return phase, 4 * marks.get(("barrier", label), 1)

            def store(block, s):
                for g in range(2):
                    sp.dma_start(dram["results"][block, 512 * g:512 * g + 512], yt[64 * g:64 * g + 64, s, :])\
                        .then_inc(y_out[s], 16)

            for s in range(4):
                sp.sem_inc(y_out[s], 32)
            order = [(a, i) for a, i, _, _ in items]
            for l in range(2):
                start = 0 if l == 0 else order.index(("extra", EXTRA_ITEMS[0] - 1)) + 1
                for key in order[start:order.index(("expert", NE * l))]:
                    if key == ("ada", 2):
                        sp.dma_start(hm_t[:], dram["hT"]).then_inc(h_in, 16)
                    if key == ("win", 0):
                        sp.dma_start(part(ring, WORK + 9216, 2 * len(LEVELS) * P), dram["levels"]).then_inc(tables_in, 16)
                        sp.dma_start(part(ring, WORK + 6144, RH * 768), dram["decay"]).then_inc(tables_in, 16)
                    if key == ("win", 3):
                        for i in range(2):
                            sp.dma_start(dram["results"][(NE + 8 * i) * CAP:(NE + 8 + 8 * i) * CAP, :],
                                         dram["hT"].rearrange("p (a b) -> (p a) b", b=D)).then_inc(filled, 16)
                    if key[0] == "ada" and key[1] > ADA_FIRST:
                        continue
                    if key == ("ada", ADA_FIRST):
                        sp.wait_ge(*seen(sp, "used:win60"))
                        with sp.Fori(0, NPAIR) as it:
                            for i in range(ADA_TURN):
                                if i == 1:
                                    sp.wait_ge(*seen(sp, "used:lora0"))
                                sp.wait_ge(*seen(sp, *((f"A{i - 2}", it) if i > 1 else
                                                       (f"A{ADA_TURN - 1 - (ADA_TURN - 1 - i) % 2}", it, 1))))
                                sp.dma_start(slot(i % 2, 4096), dram["ada"][bass.ds(it * ADA_TURN + (ADA_FIRST + i), 1)]
                                             .rearrange("o p n -> (o p) n")).then_inc(loaded[i % 2], 16)
                        continue
                    if key == ("wout", 1):
                        sp.wait_ge(*seen(sp, "mix3"))
                        sp.dma_start(part(feat_t, 0, DC * T), dram["hT"]).then_inc(h_again, 16)
                        sp.dma_start(route_w, dram["route_w"][0]).then_inc(router_in, 16)
                        sp.dma_start(route_b[0:1, :], dram["route_b"][0:1]).then_inc(router_in, 16)
                        sp.dma_start(tab, dram["tab"]).then_inc(router_in, 16)
                    if key == ("mla_in", 0):
                        sp.wait_ge(*passed("extras0"))
                        for t in range(NT):
                            sp.wait_ge(got_in[t], 32)
                        sp.dma_start(rope, dram["rope"]).then_inc(rope_in, 16)
                    load(key)
                if l == 0:
                    sp.wait_ge(filled, 32)
                for s in range(4):
                    if l and s == 2:
                        sp.wait_ge(*seen(sp, "ev:o7"))
                        sp.wait_ge(*seen(sp, "mo.7"))
                        sp.dma_start(route_w, dram["route_w"][1]).then_inc(router_in, 16)
                        sp.dma_start(route_b[0:1, :], dram["route_b"][1:2]).then_inc(router_in, 16)
                        sp.dma_start(tab, dram["tab"]).then_inc(router_in, 16)
                    if l == 0 and s == 2:
                        sp.wait_ge(*seen(sp, "n20.x7"))
                    load(("expert", NE * l + s))
                with sp.Fori(0, NE // 4 - 1) as it:
                    for s in range(4):
                        sp.wait_ge(*seen(sp, f"e{l}.{s}.down", it))
                        sp.dma_start(slot(s, SLOT), dram["expert"][bass.ds(it * 4 + (NE * l + 4 + s), 1)]
                                     .rearrange("o p n -> (o p) n")).then_inc(loaded[s], 16)
                        sp.wait_ge(*seen(sp, f"ev:e{l}.{s}.down", it))
                        store(bass.ds(it * (4 * CAP) + s * CAP, CAP), s)
                n = sp.value_load(n_extra[0:1, :], min_val=0, max_val=16)

                def load_extra(s, x):
                    with sp.If(n > x):
                        e = sp.value_load(extra_of[0:1, bass.ds(x, 1)], min_val=0, max_val=NE - 1)
                        sp.dma_start(slot(s, SLOT), dram["expert"][bass.ds(e + NE * l, 1)]
                                     .rearrange("o p n -> (o p) n")).then_inc(loaded[s], 16)
                    with sp.Else():
                        sp.sem_inc(loaded[s], 16)

                for s in range(4):
                    sp.wait_ge(*seen(sp, f"ev:e{l}.{s}.down"))
                    store(slice((NE - 4 + s) * CAP, (NE - 3 + s) * CAP), s)
                    if s < 2:
                        load_extra(s, s)
                with sp.Fori(0, n_extras[l] // 2) as it:
                    with sp.If(n > it * 2):
                        sp.wait_ge(*seen(sp, f"ev:x{l}.0.down", it))
                        store(bass.ds(it * (2 * CAP) + NE * CAP, CAP), 0)
                        load_extra(0, it * 2 + 2)
                        with sp.If(n > it * 2 + 1):
                            sp.wait_ge(*seen(sp, f"ev:x{l}.1.down", it))
                            store(bass.ds(it * (2 * CAP) + (NE + 1) * CAP, CAP), 1)
                        with sp.Else():
                            sp.sem_inc(y_out[1], 32)
                        load_extra(1, it * 2 + 3)
                    with sp.Else():
                        for s in range(2):
                            sp.sem_inc(y_out[s], 32)
                            sp.sem_inc(loaded[s], 16)
                for s in range(4):
                    sp.wait_ge(y_out[s], 32 * out_base[l + 1][s])
            for k in range(DC):
                sp.wait_ge(*seen(sp, f"out{k}"))
                sp.dma_start(out[:, k, :], xT[:, k, 0:TC]).then_inc(stored, 16)
            sp.wait_ge(stored, 16 * DC)

        for i in range(ADA_TURN):
            L.new[f"used:ada{ADA_FIRST + ADA_TURN * (NPAIR - 1) + i}"] = L.new[f"A{i}"]
        for i in range(ADA_FIRST):
            L.new[f"used:ada{i}"] = L.new[f"ada{i}"]
        for l in range(2):
            for s in range(4):
                L.new[f"used:expert{NE * l + NE - 4 + s}"] = L.new[f"e{l}.{s}.down"]
            for s in range(2):
                L.new[f"used:extra{EXTRA_ITEMS[0] * l + EXTRA_ITEMS[l] - 2 + s}"] = L.new[f"x{l}.{s}.down"]
    return L.new


N_CONST = 2


def tables():
    import numpy as np

    i = np.arange(P)
    p, c = i[:, None], i[None, :]
    swap = ((p // 32 == c // 32) & ((p - c) % 32 == 16)).astype(np.float32)
    masks = dict(ident=p == c, ones=np.ones((P, P)), half_ones=p // 64 == c // 64, swap=swap, lt=p < c, le=p <= c,
                 gt=p > c, ge=p >= c, eye2=p % 64 == c % 64)
    masks = np.concatenate([np.asarray(masks[n], np.float32) for n in MASKS], 1)
    low = [((p // (2 * n) == c // (2 * n)) & (p // n % 2 == 1) & (c // n % 2 == 0)) for n in LEVELS]
    levels = np.concatenate([np.concatenate(low, 1), np.concatenate([m.T for m in low], 1)], 1).astype(np.float32)
    decay = np.zeros((P, RH, 768), np.float64)
    u, w = np.arange(-128, 256), np.arange(128, 512)
    for h in range(RH):
        lg = math.log1p(-2.0 ** (-5 - h))
        decay[:, h, :384] = np.exp(lg * np.abs(u[None] - p))
        decay[:, h, 384:] = np.exp(lg * (w[None] - p)) + np.exp(lg * (512 - w[None] + p))
    t = np.arange(TC)
    freq = (10000.0 ** (-np.arange(16, dtype=np.float32) / 16)).astype(np.float32)
    row, col = (t // 64).astype(np.float32)[None] * freq[:, None], (t % 64).astype(np.float32)[None] * freq[:, None]
    cos = np.concatenate([np.cos(row)] * 2 + [np.cos(col)] * 2, 0)
    sin = np.concatenate([-np.sin(row), np.sin(row), -np.sin(col), np.sin(col)], 0)
    rope = np.stack([np.tile(cos, (2, 1)), np.tile(sin, (2, 1))], 1).astype(np.float32)
    tab = np.concatenate([np.arange(EPG, 0, -1), CAP * np.arange(NE), CAP * (1 + np.arange(8)), np.arange(16),
                          np.arange(2 * CAP)]).astype(np.float32)
    tab = np.tile(tab[None], (P, 1))
    return dict(masks=masks, levels=levels, decay=decay.astype(np.float32).reshape(P, -1), rope=rope, tab=tab)


def laid_out(x, c, ctx, c_ctx, ada_w, ada_b, norm1_g, norm2_g, final_g, ev_w_in, ev_shift_mu, rwkv_w0, rwkv_w2,
             rwkv_a0, rwkv_a2, rwkv_g2, rwkv_k_k, rwkv_k_a, rwkv_r_k, rwkv_lnx_w, rwkv_lnx_b, ev_w_out, mla_w_in,
             mla_q_norm_g, mla_w_uq, mla_kv_norm_g, mla_w_ukv, mla_w_o, moe_w_grp, moe_b_grp, moe_w_exp, moe_b_exp,
             moe_w_gate, moe_w_up, moe_w_down):
    import numpy as np

    def cols(v, n):
        v = np.reshape(v, -1)
        return np.concatenate([v, np.zeros(n * P - v.size, v.dtype)]).reshape(n, P).T

    def slabs(w, width):
        k, n = w.shape
        return w.reshape(k // P, P, n // width, width).transpose(2, 1, 0, 3).reshape(n // width, P, -1)

    vals = dict(c=c, c_ctx=c_ctx, norm1_g0=norm1_g[0], norm1_g1=norm1_g[1], norm2_g0=norm2_g[0], norm2_g1=norm2_g[1],
                final_g=final_g, ada_b=ada_b.reshape(-1), mu0=ev_shift_mu[0, 0], mu1=ev_shift_mu[0, 1],
                w0_0=rwkv_w0[0, 0], w0_1=rwkv_w0[0, 1], a0_0=rwkv_a0[0, 0], a0_1=rwkv_a0[0, 1], k_k=rwkv_k_k,
                k_a=rwkv_k_a, r_k=rwkv_r_k, lnx_w=rwkv_lnx_w, lnx_b=rwkv_lnx_b, q_norm=mla_q_norm_g,
                kv_norm=mla_kv_norm_g)
    vec = np.concatenate([cols(vals[n], w) for n, (_, w) in VEC.items()], 1)
    hT = np.concatenate([ctx[0], x[0]], 0).T.reshape(DC, P, T).transpose(1, 0, 2).reshape(P, -1)
    g2 = np.concatenate([rwkv_g2[0], np.zeros((96, 512), rwkv_g2.dtype)], 0)
    lora = np.concatenate([rwkv_w2[0].reshape(P, 512), rwkv_a2[0].reshape(P, 512), g2[:P], g2[P:]], 1)[None]
    uq = mla_w_uq[0].reshape(-1, MH, 192)
    uq = np.concatenate([uq[:, :, :128].reshape(-1, 1024), uq[:, :, 128:].reshape(-1, 512)], 1)
    ukv = mla_w_ukv[0].reshape(-1, MH, 256)
    ukv = np.concatenate([ukv[:, :, :128].reshape(-1, 1024), ukv[:, :, 128:].reshape(-1, 1024)], 1)
    win = ev_w_in[0]
    mla_in = np.concatenate([mla_w_in[0], mla_w_in[0][:, 640:]], 1)
    e = 2 * NE

    def rows(w):
        w = w.reshape(e, w.shape[2] // P, P, w.shape[3])
        return w.transpose(0, 2, 1, 3).reshape(e, P, -1)

    expert = np.concatenate([rows(moe_w_gate), rows(moe_w_up), rows(moe_w_down)], 2)
    route_w = np.concatenate([moe_w_grp, moe_w_exp], 2).reshape(2, DC, P, NR).transpose(0, 2, 1, 3)
    return dict(vec=vec, hT=hT, ada=np.concatenate([slabs(ada_w[0], 512), slabs(ada_w[1], 512)], 0),
                win=slabs(win[:, :3072], 512), win6=slabs(win[:, 3072:], 416), lora=lora, wout=slabs(ev_w_out[0], 512),
                expert=expert, mla_in=slabs(mla_in, 768), mla_uq=slabs(uq, 1536), mla_ukv=slabs(ukv, 2048),
                mla_o=slabs(mla_w_o[0], 512), route_w=route_w,
                route_b=np.concatenate([moe_b_grp, moe_b_exp], 1), **tables())


def kernel(**inputs):
    import numpy as np
    import concourse.bacc as bacc
    from concourse.bass_utils import run_bass_kernel_spmd as run

    arrays = {n: np.ascontiguousarray(a) for n, a in laid_out(**{k: np.asarray(v) for k, v in inputs.items()}).items()}
    marks = {}
    for _ in range(2):
        nc = bacc.Bacc("TRN2", target_bir_lowering=False, num_devices=1)
        dram = {n: nc.dram_tensor("in_" + n, a.shape, mybir.dt.from_np(a.dtype), kind="ExternalInput").ap()
                for n, a in arrays.items()}
        dram["results"] = nc.dram_tensor("results", ((NE + 16) * CAP, D), F32, kind="Internal").ap()
        out = nc.dram_tensor("out", (P, DC, TC), F32, kind="ExternalOutput").ap()
        marks = build(nc, dram, out, marks)
    r = run(nc, [{"in_" + n: a for n, a in arrays.items()}], core_ids=[0])
    o = r.results[0]["out"]
    return np.ascontiguousarray(o.transpose(2, 1, 0).reshape(1, TC, D))
```
